# Optimizing a Trainium2 kernel written in Bass

```python
import jax
import jax.numpy as jnp
from jax import lax
import numpy as np
import math
import jax, jax.numpy as jnp

D_MODEL = 1024
BATCH = 1
SEQ = 2048
DEPTH = 1

CTX_LEN = 256
GRID_W = 64
D_MIX = D_MODEL
HEAD_DIM = 64
D_POOL = D_MIX // 4
D_RWKV = (D_MIX - D_POOL) // 2
D_HGRN = D_MIX - D_POOL - D_RWKV
POOL_WINDOWS = (2, 4, 8, 16)
N_POOL_GROUPS = len(POOL_WINDOWS)
POOL_GROUP = D_POOL // N_POOL_GROUPS
H_RWKV = D_RWKV // HEAD_DIM
H_HGRN = D_HGRN // HEAD_DIM
LORA_W = 64
LORA_A = 64
N_DIR = 2
HGRN_CHUNK = 32
D_RWKV_IN = 3 * D_RWKV + N_DIR * (LORA_W + LORA_A)
D_IN = D_POOL + D_RWKV_IN + 2 * D_HGRN + N_DIR * D_HGRN + D_MIX
ALPHA = float((2 * DEPTH) ** 0.25)
BETA = float((8 * DEPTH) ** -0.25)
LN_EPS = 1e-5
GN_EPS = 64e-5
RMS_EPS = 1e-6


def _layer_norm(x):
    xf = x.astype(jnp.float32)
    mu = jnp.mean(xf, axis=-1, keepdims=True)
    var = jnp.mean(jnp.square(xf - mu), axis=-1, keepdims=True)
    return (xf - mu) * lax.rsqrt(var + LN_EPS)

def _heads(z):
    return z.reshape(z.shape[:-1] + (z.shape[-1] // HEAD_DIM, HEAD_DIM))

def _split_proj(p):
    o0 = D_POOL
    o1 = o0 + D_RWKV_IN
    o2 = o1 + 2 * D_HGRN + N_DIR * D_HGRN
    return p[..., :o0], p[..., o0:o1], p[..., o1:o2], p[..., o2:]

def _centred_mean(u, axis, window):
    n = u.shape[axis]
    left = window // 2
    right = window - 1 - left
    t = jnp.arange(n)
    lo = jnp.maximum(t - left, 0)
    hi = jnp.minimum(t + right, n - 1) + 1
    pad = [(0, 0)] * u.ndim
    pad[axis] = (1, 0)
    cs = jnp.pad(jnp.cumsum(u, axis=axis), pad)
    total = jnp.take(cs, hi, axis=axis) - jnp.take(cs, lo, axis=axis)
    shape = [1] * u.ndim
    shape[axis] = n
    count = (hi - lo).astype(jnp.float32).reshape(shape)
    return total / count

def _pool_branch(u, grid, pool_w, pool_scale):
    b, n, _ = u.shape
    uf = u.astype(jnp.float32)
    if grid:
        rows = n // GRID_W
        uf = uf.reshape(b, rows, GRID_W, D_POOL)
        axis = 2
    else:
        axis = 1
    groups = []
    for g, win in enumerate(POOL_WINDOWS):
        ch = uf[..., g * POOL_GROUP:(g + 1) * POOL_GROUP]
        groups.append(_centred_mean(ch, axis, win) - ch)
    pooled = jnp.stack(groups, axis=-2)
    mixed = jnp.einsum('...gi,gio->...go', pooled, pool_w)
    return mixed.reshape(b, n, D_POOL) * pool_scale

def _shift3(u, w):
    up = jnp.pad(u, ((0, 0), (1, 1), (0, 0)))
    return w[0] * up[:, :-2] + w[1] * up[:, 1:-1] + w[2] * up[:, 2:]

def _rwkv_dir_inputs(u, d, w0, w_up, a0, a_up, k_k, k_a):
    r = u[..., :D_RWKV]
    k = u[..., D_RWKV:2 * D_RWKV]
    v = u[..., 2 * D_RWKV:3 * D_RWKV]
    o = 3 * D_RWKV
    xw = u[..., o + d * LORA_W:o + (d + 1) * LORA_W]
    o2 = o + N_DIR * LORA_W
    xa = u[..., o2 + d * LORA_A:o2 + (d + 1) * LORA_A]
    w_log = -jax.nn.softplus(-(w0[d] + jnp.tanh(xw) @ w_up[d])) - 0.5
    decay = jnp.exp(-jnp.exp(w_log))
    a = jax.nn.sigmoid(a0[d] + xa @ a_up[d])
    kk = _heads(k * k_k)
    kk = kk * lax.rsqrt(jnp.sum(kk * kk, axis=-1, keepdims=True) + 1e-12)
    k_mod = k * (1.0 + (a - 1.0) * k_a)
    return (_heads(r), _heads(decay), _heads(k_mod), _heads(v), kk, _heads(a))

def _rwkv_bonus(ins, r_k_d):
    r, k_mod, v = ins[0], ins[2], ins[3]
    return jnp.sum(r * k_mod * r_k_d, axis=-1, keepdims=True) * v

def _rwkv_scan(state, ins, emit):
    r, w, k, v, kk, a = (jnp.moveaxis(z, 1, 0) for z in ins)
    xs = (w, k, v, kk, a, r) if emit else (w, k, v, kk, a)

    def step(S, inp):
        w_t, k_t, v_t, kk_t, a_t = inp[:5]
        sa = jnp.einsum('bhvk,bhk->bhv', S, kk_t)
        S = (S * w_t[:, :, None, :] - sa[..., None] * (kk_t * a_t)[:, :, None, :]
             + v_t[..., None] * k_t[:, :, None, :])
        y = jnp.einsum('bhvk,bhk->bhv', S, inp[5]) if emit else None
        return S, y

    state, ys = lax.scan(step, state, xs)
    return state, (jnp.moveaxis(ys, 0, 1) if emit else None)

def _rwkv_readout(y, bonus, gn_g, gn_b):
    mu = jnp.mean(y, axis=-1, keepdims=True)
    var = jnp.mean(jnp.square(y - mu), axis=-1, keepdims=True)
    yn = (y - mu) * lax.rsqrt(var + GN_EPS) * gn_g.reshape(H_RWKV, HEAD_DIM) + gn_b.reshape(H_RWKV, HEAD_DIM)
    out = yn + bonus
    return out.reshape(out.shape[:-2] + (D_RWKV,))

def _rwkv_branch(u_ctx, u_lat, w0, w_up, a0, a_up, k_k, k_a, r_k, gn_g, gn_b, emit_ctx):
    b = u_lat.shape[0]
    y_ctx, y_lat, bonus_ctx, bonus_lat = 0.0, 0.0, 0.0, 0.0
    for d in range(N_DIR):
        ins_c = _rwkv_dir_inputs(u_ctx, d, w0, w_up, a0, a_up, k_k, k_a)
        ins_l = _rwkv_dir_inputs(u_lat, d, w0, w_up, a0, a_up, k_k, k_a)
        bonus_lat = bonus_lat + _rwkv_bonus(ins_l, r_k[d])
        if emit_ctx:
            bonus_ctx = bonus_ctx + _rwkv_bonus(ins_c, r_k[d])
        if d == 1:
            ins_c = tuple(jnp.flip(z, axis=1) for z in ins_c)
            ins_l = tuple(jnp.flip(z, axis=1) for z in ins_l)
        s0 = jnp.zeros((b, H_RWKV, HEAD_DIM, HEAD_DIM), jnp.float32)
        s_c, yc = _rwkv_scan(s0, ins_c, emit_ctx)
        _, yl = _rwkv_scan(s_c, ins_l, True)
        if d == 1:
            yl = jnp.flip(yl, axis=1)
            if emit_ctx:
                yc = jnp.flip(yc, axis=1)
        y_lat = y_lat + yl
        if emit_ctx:
            y_ctx = y_ctx + yc
    out_lat = _rwkv_readout(y_lat, bonus_lat, gn_g, gn_b)
    out_ctx = _rwkv_readout(y_ctx, bonus_ctx, gn_g, gn_b) if emit_ctx else None
    return out_ctx, out_lat

def _hgrn_dir_inputs(fh, d, lb_d):
    q = fh[..., :D_HGRN]
    i = fh[..., D_HGRN:2 * D_HGRN]
    z = fh[..., (2 + d) * D_HGRN:(3 + d) * D_HGRN]
    logf = jnp.logaddexp(jnp.log(lb_d), jnp.log1p(-lb_d) + jax.nn.log_sigmoid(z))
    k = (1.0 - lb_d) * jax.nn.sigmoid(-z)
    return (_heads(k), _heads(i), _heads(logf), _heads(q))

def _hgrn_scan(state, ins, emit):
    k, i, logf, q = ins
    b, n, h, dk = k.shape
    nc = n // HGRN_CHUNK

    def chunks(z):
        return z.reshape(b, nc, HGRN_CHUNK, h, dk).transpose(1, 0, 3, 2, 4)

    causal = jnp.tril(jnp.ones((HGRN_CHUNK, HGRN_CHUNK), dtype=bool))[:, :, None]

    def step(S, inp):
        k_c, i_c, lf_c = inp[:3]
        g = jnp.cumsum(lf_c, axis=2)
        g_last = g[:, :, -1:, :]
        if emit:
            q_c = inp[3]
            inter = jnp.einsum('bhtk,bhkv->bhtv', q_c * jnp.exp(g), S)
            rel = jnp.exp(jnp.where(causal, g[:, :, :, None, :] - g[:, :, None, :, :], -jnp.inf))
            scores = jnp.einsum('bhtk,bhsk,bhtsk->bhts', q_c, k_c, rel)
            o = inter + jnp.einsum('bhts,bhsv->bhtv', scores, i_c)
        else:
            o = None
        S = (jnp.exp(g_last[:, :, 0, :])[..., None] * S
             + jnp.einsum('bhsk,bhsv->bhkv', k_c * jnp.exp(g_last - g), i_c))
        return S, o

    xs = (chunks(k), chunks(i), chunks(logf), chunks(q)) if emit else (chunks(k), chunks(i), chunks(logf))
    state, o = lax.scan(step, state, xs)
    if emit:
        o = o.transpose(1, 0, 3, 2, 4).reshape(b, n, h, dk)
    return state, o

def _rms_heads(o, norm_g):
    on = o * lax.rsqrt(jnp.mean(o * o, axis=-1, keepdims=True) + RMS_EPS) * norm_g.reshape(H_HGRN, HEAD_DIM)
    return on.reshape(on.shape[:-2] + (D_HGRN,))

def _hgrn_branch(fh_ctx, fh_lat, lb, norm_g, emit_ctx):
    b = fh_lat.shape[0]
    o_ctx, o_lat = 0.0, 0.0
    for d in range(N_DIR):
        ins_c = _hgrn_dir_inputs(fh_ctx, d, lb[d])
        ins_l = _hgrn_dir_inputs(fh_lat, d, lb[d])
        if d == 1:
            ins_c = tuple(jnp.flip(z, axis=1) for z in ins_c)
            ins_l = tuple(jnp.flip(z, axis=1) for z in ins_l)
        s0 = jnp.zeros((b, H_HGRN, HEAD_DIM, HEAD_DIM), jnp.float32)
        s_c, oc = _hgrn_scan(s0, ins_c, emit_ctx)
        _, ol = _hgrn_scan(s_c, ins_l, True)
        if d == 1:
            ol = jnp.flip(ol, axis=1)
            if emit_ctx:
                oc = jnp.flip(oc, axis=1)
        o_lat = o_lat + ol
        if emit_ctx:
            o_ctx = o_ctx + oc
    out_ctx = _rms_heads(o_ctx, norm_g) if emit_ctx else None
    return out_ctx, _rms_heads(o_lat, norm_g)

def first_inputs(seed: int = 0) -> dict:
    key = jax.random.key(seed)
    ks = jax.random.split(key, 24)
    f32 = jnp.float32

    def nrm(k, shape, scale):
        return scale * jax.random.normal(k, shape, f32)

    return {
        "x": nrm(ks[0], (BATCH, SEQ, D_MODEL), 1.0),
        "c": nrm(ks[1], (BATCH, D_MODEL), 1.0),
        "ctx": nrm(ks[2], (BATCH, CTX_LEN, D_MODEL), 1.0),
        "c_ctx": nrm(ks[3], (D_MODEL,), 1.0),
        "mod_w": nrm(ks[4], (DEPTH, D_MODEL, 3 * D_MODEL), D_MODEL ** -0.5),
        "mod_b": nrm(ks[5], (DEPTH, 3 * D_MODEL), 0.02),
        "w_in": nrm(ks[6], (DEPTH, D_MODEL, D_IN), D_MODEL ** -0.5),
        "rwkv_shift": jnp.array([0.25, 0.5, 0.25], f32)[None, :, None] + nrm(ks[7], (DEPTH, 3, D_RWKV_IN), 0.05),
        "pool_w": nrm(ks[8], (DEPTH, N_POOL_GROUPS, POOL_GROUP, POOL_GROUP), POOL_GROUP ** -0.5),
        "pool_scale": 1.0 + nrm(ks[9], (DEPTH, D_POOL), 0.1),
        "rwkv_w0": jax.random.uniform(ks[10], (DEPTH, N_DIR, D_RWKV), f32, minval=-5.0, maxval=-0.5),
        "rwkv_w_up": nrm(ks[11], (DEPTH, N_DIR, LORA_W, D_RWKV), 0.5 * LORA_W ** -0.5),
        "rwkv_a0": nrm(ks[12], (DEPTH, N_DIR, D_RWKV), 0.1),
        "rwkv_a_up": nrm(ks[13], (DEPTH, N_DIR, LORA_A, D_RWKV), LORA_A ** -0.5),
        "rwkv_k_k": 0.85 + nrm(ks[14], (DEPTH, D_RWKV), 0.05),
        "rwkv_k_a": 1.0 + nrm(ks[15], (DEPTH, D_RWKV), 0.05),
        "rwkv_r_k": nrm(ks[16], (DEPTH, N_DIR, H_RWKV, HEAD_DIM), 0.1),
        "rwkv_gn_g": 1.0 + nrm(ks[17], (DEPTH, D_RWKV), 0.05),
        "rwkv_gn_b": nrm(ks[18], (DEPTH, D_RWKV), 0.02),
        "hgrn_lb_logits": nrm(ks[19], (N_DIR, DEPTH, D_HGRN), 0.5),
        "hgrn_norm_g": 1.0 + nrm(ks[20], (DEPTH, D_HGRN), 0.05),
        "w_out": nrm(ks[21], (DEPTH, D_MIX, D_MODEL), BETA * D_MIX ** -0.5),
        "ln_g": 1.0 + nrm(ks[22], (DEPTH, D_MODEL), 0.05),
        "ln_b": nrm(ks[23], (DEPTH, D_MODEL), 0.02),
    }

def first_block(x, c, ctx, c_ctx, mod_w, mod_b, w_in, rwkv_shift, pool_w, pool_scale,
              rwkv_w0, rwkv_w_up, rwkv_a0, rwkv_a_up, rwkv_k_k, rwkv_k_a, rwkv_r_k,
              rwkv_gn_g, rwkv_gn_b, hgrn_lb_logits, hgrn_norm_g, w_out, ln_g, ln_b):
    out_dtype = x.dtype
    lb_w = jax.nn.softmax(hgrn_lb_logits.astype(jnp.float32), axis=1)
    lb_all = jnp.maximum(jnp.cumsum(lb_w, axis=1) - lb_w[:, :1], 0.0)
    h_x = x.astype(jnp.float32)
    h_ctx = ctx.astype(jnp.float32)
    for l in range(DEPTH):
        last = l == DEPTH - 1
        mod_lat = jax.nn.silu(c.astype(jnp.float32)) @ mod_w[l] + mod_b[l]
        mod_c = jax.nn.silu(c_ctx.astype(jnp.float32)) @ mod_w[l] + mod_b[l]
        sh_l, sc_l, gt_l = jnp.split(mod_lat, 3, axis=-1)
        sh_c, sc_c, gt_c = jnp.split(mod_c, 3, axis=-1)
        p_lat = (_layer_norm(h_x) * (1.0 + sc_l[:, None]) + sh_l[:, None]) @ w_in[l]
        p_ctx = (_layer_norm(h_ctx) * (1.0 + sc_c) + sh_c) @ w_in[l]
        pv_l, u_l, fh_l, g_l = _split_proj(p_lat)
        pv_c, u_c, fh_c, g_c = _split_proj(p_ctx)
        u_l = _shift3(u_l, rwkv_shift[l])
        u_c = _shift3(u_c, rwkv_shift[l])
        y_rc, y_rl = _rwkv_branch(u_c, u_l, rwkv_w0[l], rwkv_w_up[l], rwkv_a0[l], rwkv_a_up[l],
                                  rwkv_k_k[l], rwkv_k_a[l], rwkv_r_k[l], rwkv_gn_g[l], rwkv_gn_b[l],
                                  not last)
        o_hc, o_hl = _hgrn_branch(fh_c, fh_l, lb_all[:, l], hgrn_norm_g[l], not last)
        pool_l = _pool_branch(pv_l, True, pool_w[l], pool_scale[l])
        mix_l = jnp.concatenate([pool_l, y_rl, o_hl], axis=-1) * jax.nn.silu(g_l)
        new_x = _layer_norm(ALPHA * h_x + gt_l[:, None] * (mix_l @ w_out[l])) * ln_g[l] + ln_b[l]
        if not last:
            pool_c = _pool_branch(pv_c, False, pool_w[l], pool_scale[l])
            mix_c = jnp.concatenate([pool_c, y_rc, o_hc], axis=-1) * jax.nn.silu(g_c)
            h_ctx = _layer_norm(ALPHA * h_ctx + gt_c * (mix_c @ w_out[l])) * ln_g[l] + ln_b[l]
        h_x = new_x
    return h_x.astype(out_dtype)


DEPTH_2 = 2

INNER = D_MODEL
A_WIDTH = INNER // 2
B_WIDTH = INNER - A_WIDTH
B_HEADS = B_WIDTH // HEAD_DIM
B_KV_HEADS = B_HEADS // 4
KV_WIDTH = B_KV_HEADS * HEAD_DIM
CONV_WIDTH = 31
Q_BLOCK = 128
ROPE_THETA = 10000.0
C_WIDTH = INNER // 2
C_GROUPS = 4
C_GROUP_DIM = C_WIDTH // C_GROUPS
D_WIDTH = INNER - C_WIDTH
D_HEADS = D_WIDTH // HEAD_DIM
NA_ROWS = 8
NA_COLS = 16
EPS = 1e-6
NEG_INF = -1e30
N_AB = (DEPTH_2 + 1) // 2
N_CD = DEPTH_2 // 2

AB_Q_OFF = 2 * A_WIDTH
AB_K_OFF = AB_Q_OFF + B_WIDTH
AB_V_OFF = AB_K_OFF + KV_WIDTH
AB_Z_OFF = AB_V_OFF + KV_WIDTH
AB_IN = AB_Z_OFF + INNER
CD_Q_OFF = C_WIDTH
CD_K_OFF = CD_Q_OFF + D_WIDTH
CD_V_OFF = CD_K_OFF + D_WIDTH
CD_Z_OFF = CD_V_OFF + D_WIDTH
CD_IN = CD_Z_OFF + INNER


def rms_norm(x, g):
    x32 = x.astype(jnp.float32)
    y = x32 * lax.rsqrt(jnp.mean(x32 * x32, axis=-1, keepdims=True) + EPS)
    return (y * g.astype(jnp.float32)).astype(x.dtype)

def layer_norm(x, g, b):
    x32 = x.astype(jnp.float32)
    mu = jnp.mean(x32, axis=-1, keepdims=True)
    xc = x32 - mu
    y = xc * lax.rsqrt(jnp.mean(xc * xc, axis=-1, keepdims=True) + EPS)
    return (y * g.astype(jnp.float32) + b.astype(jnp.float32)).astype(x.dtype)

def adaln(cond, w, b):
    m = jax.nn.silu(cond) @ w + b
    return jnp.split(m, 3, axis=-1)

def axial_rope(x):
    S = x.shape[1]
    t = jnp.arange(S)
    row = (t // GRID_W).astype(jnp.float32)
    col = (t % GRID_W).astype(jnp.float32)
    nf = HEAD_DIM // 4
    inv = ROPE_THETA ** (-jnp.arange(nf, dtype=jnp.float32) / nf)
    ang = jnp.concatenate([row[:, None] * inv, col[:, None] * inv], axis=-1)
    cos = jnp.cos(ang)[None, :, None, :]
    sin = jnp.sin(ang)[None, :, None, :]
    xp = x.astype(jnp.float32).reshape(x.shape[:-1] + (HEAD_DIM // 2, 2))
    a, b = xp[..., 0], xp[..., 1]
    out = jnp.stack([a * cos - b * sin, a * sin + b * cos], axis=-1)
    return out.reshape(x.shape).astype(x.dtype)

def dense_attn(q, k, v):
    Bq, Lq, Hq, dh = q.shape
    Hk = k.shape[2]
    qg = q.reshape(Bq, Lq, Hk, Hq // Hk, dh)
    s = jnp.einsum('bqkgd,bskd->bkgqs', qg, k).astype(jnp.float32) * (dh ** -0.5)
    p = jax.nn.softmax(s, axis=-1).astype(v.dtype)
    o = jnp.einsum('bkgqs,bskd->bqkgd', p, v)
    return o.reshape(Bq, Lq, Hq * dh)

def blocked_attn(q, k, v):
    Bq, S, Hq, dh = q.shape
    nb = S // Q_BLOCK
    qb = q.reshape(Bq, nb, Q_BLOCK, Hq, dh).transpose(1, 0, 2, 3, 4)
    ob = lax.map(lambda qi: dense_attn(qi, k, v), qb)
    return ob.transpose(1, 0, 2, 3).reshape(Bq, S, Hq * dh)

def dwconv(x, w, b):
    K = w.shape[0]
    y = lax.conv_general_dilated(x, w[:, None, :].astype(x.dtype), (1,), [(K // 2, K // 2)],
                                 dimension_numbers=('NWC', 'WIO', 'NWC'),
                                 feature_group_count=x.shape[-1])
    return y + b

def conformer_conv(a_val, a_gate, conv_w, conv_b, ln_g, ln_b):
    u = a_val * jax.nn.sigmoid(a_gate)
    u = dwconv(u, conv_w, conv_b)
    return jax.nn.silu(layer_norm(u, ln_g, ln_b))

def fourier_mix(f, w_c):
    Bf, L, _ = f.shape
    fg = f.reshape(Bf, L, C_GROUPS, C_GROUP_DIM).astype(jnp.float32)
    fr = jnp.fft.fft2(fg, axes=(1, 3), norm='ortho').real.astype(f.dtype)
    return jnp.einsum('blgc,gce->blge', fr, w_c).reshape(Bf, L, C_WIDTH)

def neighborhood_attn(q, k, v, kc, vc, rpb):
    Bq, S, H, dh = q.shape
    rows = S // GRID_W
    kr = min(NA_ROWS, rows)
    qg = q.reshape(Bq, rows, GRID_W, H, dh)
    kg = k.reshape(Bq, rows, GRID_W, H, dh)
    vg = v.reshape(Bq, rows, GRID_W, H, dh)
    r = jnp.arange(rows)
    rs = jnp.clip(r - kr // 2, 0, rows - kr)
    row_idx = rs[:, None] + jnp.arange(kr)[None, :]
    kb = kg[:, row_idx]
    vb = vg[:, row_idx]
    wq = jnp.arange(GRID_W)
    cs = jnp.clip(wq - NA_COLS // 2, 0, GRID_W - NA_COLS)
    col_ok = (wq[None, :] >= cs[:, None]) & (wq[None, :] < cs[:, None] + NA_COLS)
    dr_idx = row_idx - r[:, None] + (NA_ROWS - 1)
    dc_idx = jnp.clip(wq[None, :] - wq[:, None] + (NA_COLS - 1), 0, 2 * NA_COLS - 2)
    bias = rpb[:, dr_idx[:, None, :, None], dc_idx[None, :, None, :]]
    scale = dh ** -0.5
    s_win = jnp.einsum('brqhd,brkwhd->bhrqkw', qg, kb).astype(jnp.float32) * scale \
        + bias.astype(jnp.float32)[None]
    s_win = jnp.where(col_ok[:, None, :], s_win, NEG_INF).reshape(Bq, H, rows, GRID_W, kr * GRID_W)
    s_ctx = jnp.einsum('brqhd,bchd->bhrqc', qg, kc).astype(jnp.float32) * scale
    p = jax.nn.softmax(jnp.concatenate([s_win, s_ctx], axis=-1), axis=-1).astype(v.dtype)
    p_win = p[..., :kr * GRID_W].reshape(Bq, H, rows, GRID_W, kr, GRID_W)
    p_ctx = p[..., kr * GRID_W:]
    o = jnp.einsum('bhrqkw,brkwhd->brqhd', p_win, vb) + jnp.einsum('bhrqc,bchd->brqhd', p_ctx, vc)
    return o.reshape(Bq, S, H * dh)

def layer_ab(x, xc, c, c_ctx, w_ada, b_ada, norm_g, w_in, conv_w, conv_b, ln_g, ln_b,
             qn_g, kn_g, w_out, need_ctx):
    Bx, S, _ = x.shape
    L = xc.shape[1]
    shift, scale, gate = adaln(c[:, None, :], w_ada, b_ada)
    cshift, cscale, cgate = adaln(c_ctx, w_ada, b_ada)
    h = rms_norm(x, norm_g) * (1 + scale) + shift
    hc = rms_norm(xc, norm_g) * (1 + cscale) + cshift
    u = h @ w_in
    a_val, a_gate = u[..., :A_WIDTH], u[..., A_WIDTH:AB_Q_OFF]
    q = u[..., AB_Q_OFF:AB_K_OFF].reshape(Bx, S, B_HEADS, HEAD_DIM)
    k = u[..., AB_K_OFF:AB_V_OFF].reshape(Bx, S, B_KV_HEADS, HEAD_DIM)
    v = u[..., AB_V_OFF:AB_Z_OFF].reshape(Bx, S, B_KV_HEADS, HEAD_DIM)
    z = u[..., AB_Z_OFF:]
    uc = hc @ (w_in if need_ctx else w_in[:, AB_K_OFF:AB_Z_OFF])
    kv_off = AB_K_OFF if need_ctx else 0
    ck = uc[..., kv_off:kv_off + KV_WIDTH].reshape(Bx, L, B_KV_HEADS, HEAD_DIM)
    cv = uc[..., kv_off + KV_WIDTH:kv_off + 2 * KV_WIDTH].reshape(Bx, L, B_KV_HEADS, HEAD_DIM)
    ck = rms_norm(ck, kn_g)
    q = axial_rope(rms_norm(q, qn_g))
    k = axial_rope(rms_norm(k, kn_g))
    y_b = blocked_attn(q, jnp.concatenate([ck, k], axis=1), jnp.concatenate([cv, v], axis=1))
    y_a = conformer_conv(a_val, a_gate, conv_w, conv_b, ln_g, ln_b)
    y = jnp.concatenate([y_a, y_b], axis=-1) * jax.nn.silu(z)
    x = x + gate * (y @ w_out)
    if need_ctx:
        cq = rms_norm(uc[..., AB_Q_OFF:AB_K_OFF].reshape(Bx, L, B_HEADS, HEAD_DIM), qn_g)
        yc_b = dense_attn(cq, ck, cv)
        yc_a = conformer_conv(uc[..., :A_WIDTH], uc[..., A_WIDTH:AB_Q_OFF], conv_w, conv_b, ln_g, ln_b)
        yc = jnp.concatenate([yc_a, yc_b], axis=-1) * jax.nn.silu(uc[..., AB_Z_OFF:])
        xc = xc + cgate * (yc @ w_out)
    return x, xc

def layer_cd(x, xc, c, c_ctx, w_ada, b_ada, norm_g, w_in, w_fourier, rpb, w_out, need_ctx):
    Bx, S, _ = x.shape
    L = xc.shape[1]
    shift, scale, gate = adaln(c[:, None, :], w_ada, b_ada)
    cshift, cscale, cgate = adaln(c_ctx, w_ada, b_ada)
    h = rms_norm(x, norm_g) * (1 + scale) + shift
    hc = rms_norm(xc, norm_g) * (1 + cscale) + cshift
    u = h @ w_in
    f = u[..., :C_WIDTH]
    q = u[..., CD_Q_OFF:CD_K_OFF].reshape(Bx, S, D_HEADS, HEAD_DIM)
    k = u[..., CD_K_OFF:CD_V_OFF].reshape(Bx, S, D_HEADS, HEAD_DIM)
    v = u[..., CD_V_OFF:CD_Z_OFF].reshape(Bx, S, D_HEADS, HEAD_DIM)
    z = u[..., CD_Z_OFF:]
    uc = hc @ (w_in if need_ctx else w_in[:, CD_K_OFF:CD_Z_OFF])
    kv_off = CD_K_OFF if need_ctx else 0
    ck = uc[..., kv_off:kv_off + D_WIDTH].reshape(Bx, L, D_HEADS, HEAD_DIM)
    cv = uc[..., kv_off + D_WIDTH:kv_off + 2 * D_WIDTH].reshape(Bx, L, D_HEADS, HEAD_DIM)
    y_c = fourier_mix(f, w_fourier)
    y_d = neighborhood_attn(q, k, v, ck, cv, rpb)
    y = jnp.concatenate([y_c, y_d], axis=-1) * jax.nn.silu(z)
    x = x + gate * (y @ w_out)
    if need_ctx:
        cq = uc[..., CD_Q_OFF:CD_K_OFF].reshape(Bx, L, D_HEADS, HEAD_DIM)
        yc_d = dense_attn(cq, ck, cv)
        yc_c = fourier_mix(uc[..., :C_WIDTH], w_fourier)
        yc = jnp.concatenate([yc_c, yc_d], axis=-1) * jax.nn.silu(uc[..., CD_Z_OFF:])
        xc = xc + cgate * (yc @ w_out)
    return x, xc

def second_inputs(seed: int = 0) -> dict:
    key = jax.random.key(seed)
    ks = iter(jax.random.split(key, 32))
    nrm = lambda shape, s: jax.random.normal(next(ks), shape, jnp.float32) * s
    gain = lambda shape: 1.0 + nrm(shape, 0.05)
    return {
        "x": nrm((BATCH, SEQ, D_MODEL), 1.0),
        "c": nrm((BATCH, D_MODEL), 1.0),
        "ctx": nrm((BATCH, CTX_LEN, D_MODEL), 1.0),
        "c_ctx": nrm((D_MODEL,), 1.0),
        "ab_w_ada": nrm((N_AB, D_MODEL, 3 * D_MODEL), 0.5 * D_MODEL ** -0.5),
        "ab_b_ada": nrm((N_AB, 3 * D_MODEL), 0.01),
        "ab_norm_g": gain((N_AB, D_MODEL)),
        "ab_w_in": nrm((N_AB, D_MODEL, AB_IN), D_MODEL ** -0.5),
        "ab_conv_w": nrm((N_AB, CONV_WIDTH, A_WIDTH), CONV_WIDTH ** -0.5),
        "ab_conv_b": nrm((N_AB, A_WIDTH), 0.01),
        "ab_ln_g": gain((N_AB, A_WIDTH)),
        "ab_ln_b": nrm((N_AB, A_WIDTH), 0.01),
        "ab_q_norm_g": gain((N_AB, HEAD_DIM)),
        "ab_k_norm_g": gain((N_AB, HEAD_DIM)),
        "ab_w_out": nrm((N_AB, INNER, D_MODEL), INNER ** -0.5),
        "cd_w_ada": nrm((N_CD, D_MODEL, 3 * D_MODEL), 0.5 * D_MODEL ** -0.5),
        "cd_b_ada": nrm((N_CD, 3 * D_MODEL), 0.01),
        "cd_norm_g": gain((N_CD, D_MODEL)),
        "cd_w_in": nrm((N_CD, D_MODEL, CD_IN), D_MODEL ** -0.5),
        "cd_w_fourier": nrm((N_CD, C_GROUPS, C_GROUP_DIM, C_GROUP_DIM), C_GROUP_DIM ** -0.5),
        "cd_rpb": nrm((N_CD, D_HEADS, 2 * NA_ROWS - 1, 2 * NA_COLS - 1), 0.1),
        "cd_w_out": nrm((N_CD, INNER, D_MODEL), INNER ** -0.5),
        "final_norm_g": gain((D_MODEL,)),
    }

def second_block(x, c, ctx, c_ctx, ab_w_ada, ab_b_ada, ab_norm_g, ab_w_in, ab_conv_w, ab_conv_b,
              ab_ln_g, ab_ln_b, ab_q_norm_g, ab_k_norm_g, ab_w_out, cd_w_ada, cd_b_ada, cd_norm_g,
              cd_w_in, cd_w_fourier, cd_rpb, cd_w_out, final_norm_g):
    xc = ctx
    for layer in range(DEPTH_2):
        need_ctx = layer < DEPTH_2 - 1
        i = layer // 2
        if layer % 2 == 0:
            x, xc = layer_ab(x, xc, c, c_ctx, ab_w_ada[i], ab_b_ada[i], ab_norm_g[i], ab_w_in[i],
                             ab_conv_w[i], ab_conv_b[i], ab_ln_g[i], ab_ln_b[i],
                             ab_q_norm_g[i], ab_k_norm_g[i], ab_w_out[i], need_ctx)
        else:
            x, xc = layer_cd(x, xc, c, c_ctx, cd_w_ada[i], cd_b_ada[i], cd_norm_g[i], cd_w_in[i],
                             cd_w_fourier[i], cd_rpb[i], cd_w_out[i], need_ctx)
    return rms_norm(x, final_norm_g)


def setup_inputs(seed=0):
    out = dict(first_inputs(seed))
    for name, value in second_inputs(seed + 1).items():
        if name != "x":
            out[name + "_2"] = value
    return out


def reference(
    x, c, ctx, c_ctx, mod_w, mod_b, w_in, rwkv_shift, pool_w, pool_scale, rwkv_w0, rwkv_w_up,
    rwkv_a0, rwkv_a_up, rwkv_k_k, rwkv_k_a, rwkv_r_k, rwkv_gn_g, rwkv_gn_b, hgrn_lb_logits,
    hgrn_norm_g, w_out, ln_g, ln_b, c_2, ctx_2, c_ctx_2, ab_w_ada_2, ab_b_ada_2, ab_norm_g_2,
    ab_w_in_2, ab_conv_w_2, ab_conv_b_2, ab_ln_g_2, ab_ln_b_2, ab_q_norm_g_2, ab_k_norm_g_2,
    ab_w_out_2, cd_w_ada_2, cd_b_ada_2, cd_norm_g_2, cd_w_in_2, cd_w_fourier_2, cd_rpb_2,
    cd_w_out_2, final_norm_g_2,
):
    x = first_block(
        x, c, ctx, c_ctx, mod_w, mod_b, w_in, rwkv_shift, pool_w, pool_scale, rwkv_w0,
        rwkv_w_up, rwkv_a0, rwkv_a_up, rwkv_k_k, rwkv_k_a, rwkv_r_k, rwkv_gn_g, rwkv_gn_b,
        hgrn_lb_logits, hgrn_norm_g, w_out, ln_g, ln_b,
    )
    return second_block(
        x, c_2, ctx_2, c_ctx_2, ab_w_ada_2, ab_b_ada_2, ab_norm_g_2, ab_w_in_2, ab_conv_w_2,
        ab_conv_b_2, ab_ln_g_2, ab_ln_b_2, ab_q_norm_g_2, ab_k_norm_g_2, ab_w_out_2, cd_w_ada_2,
        cd_b_ada_2, cd_norm_g_2, cd_w_in_2, cd_w_fourier_2, cd_rpb_2, cd_w_out_2,
        final_norm_g_2,
    )


_drawn_inputs = setup_inputs


def setup_inputs(seed=0):
    import zlib

    import numpy as np

    out = dict(_drawn_inputs(seed))
    spreads = {}
    factors = {'ctx': 3.826,
     'c_ctx': 3.764,
     'mod_b': 3.835,
     'pool_scale': 4.452,
     'rwkv_w_up': 3.406,
     'rwkv_a0': 8.0,
     'rwkv_gn_g': 7.727,
     'rwkv_gn_b': 8.0,
     'hgrn_norm_g': 7.279,
     'ln_b': 2.872,
     'ctx_2': 4.484,
     'ab_b_ada_2': 8.0,
     'ab_norm_g_2': 8.0,
     'ab_conv_b_2': 8.0,
     'ab_ln_g_2': 8.0,
     'ab_ln_b_2': 8.0,
     'ab_q_norm_g_2': 8.0,
     'ab_k_norm_g_2': 8.0,
     'cd_b_ada_2': 8.0,
     'cd_norm_g_2': 6.981,
     'cd_rpb_2': 8.0}
    for name, (base, spread) in spreads.items():
        noise = np.random.default_rng([zlib.crc32(name.encode()), seed]).standard_normal(out[name].shape)
        drawn = base * np.exp(spread * noise) if base else spread * noise
        out[name] = jnp.asarray(drawn.astype(out[name].dtype))
    for name, factor in factors.items():
        out[name] = (out[name] * factor).astype(out[name].dtype)
    return out
```

```python
from contextlib import ExitStack

import numpy as np

import concourse.bass as bass
from concourse import mybir
from concourse.alu_op_type import AluOpType as ALU

F32 = mybir.dt.float32
ACT = mybir.ActivationFunctionType
AX = mybir.AxisListType.X
ds = bass.ds

P = 128
D = 1024
KT = D // P
SEQ = 2048
CTX = 256
T = SEQ + CTX
NT = 512
HD = 64
ALPHA = 2.0 ** 0.25


class Scope:

    def __init__(self, nc, ctx, name):
        self.nc, self.ctx, self.name, self.all_sems = nc, ctx, name, []
        ctx.callback(self.close)

    def close(self):
        self.nc.clear_and_free_semaphores(self.all_sems)
        self.nc.all_engine_barrier()

    def sb(self, name, shape, dt=F32):
        return self.ctx.enter_context(self.nc.sbuf_tensor(f"{self.name}_{name}", list(shape), dt))

    def banks(self, n):
        return [self.ctx.enter_context(self.nc.psum_tensor(f"{self.name}_bank{i}", [P, NT], F32)) for i in range(n)]

    def sem(self, name):
        self.all_sems.append(self.nc.alloc_semaphore(f"{self.name}_{name}"))
        return self.all_sems[-1]

    def sems(self, name, n):
        return [self.sem(f"{name}{i}") for i in range(n)]


class Chain:

    def __init__(self, eng, sem):
        self.eng, self.sem, self.done, self.base, self.n = eng, sem, 0, 0, 0

    def body(self, i, per):
        self.per, self.base, self.n = per, self.done + i * per, 0

    def end(self, count):
        assert self.n == self.per, (self.n, self.per)
        self.done += count * self.per
        self.base, self.n = self.done, 0

    def __call__(self, ins):
        ins.then_inc(self.sem, 1)
        self.n += 1
        self.eng.wait_ge(self.sem, self.base + self.n)


def modulation(nc, layers):
    NL = len(layers)
    NC = 3 * D // NT
    with ExitStack() as ctx:
        s = Scope(nc, ctx, "mod")
        cond = s.sb("cond", [P, NL, 2, KT])
        act = s.sb("act", [P, NL, KT, 2])
        w = [s.sb(f"w{u}", [P, KT, NT]) for u in range(2)]
        b = [s.sb(f"b{u}", [2, NT]) for u in range(2)]
        o = [s.sb(f"o{u}", [2, NT]) for u in range(2)]
        ps = s.banks(2)
        cond_in, act_ready = s.sem("cond_in"), s.sem("act_ready")
        w_full, w_free = s.sems("w_full", 2), s.sems("w_free", 2)
        o_full, o_out = s.sems("o_full", 2), s.sems("o_out", 2)

        with nc.Block() as block:
            @block.sync
            def _(sp):
                for l, (c, c_ctx, _, _, _) in enumerate(layers):
                    sp.dma_start(cond[:, l, 0, :], c[0].rearrange("(p k) -> p k", k=KT)).then_inc(cond_in, 16)
                    sp.dma_start(cond[:, l, 1, :], c_ctx.rearrange("(p k) -> p k", k=KT)).then_inc(cond_in, 16)
                for l, (_, _, wd, bd, _) in enumerate(layers):
                    wv = wd.rearrange("(p k) n -> p k n", k=KT)
                    with sp.Fori(0, NC // 2) as i:
                        for u in range(2):
                            sp.wait_ge(w_free[u], i + l * (NC // 2))
                            cols = ds((i * 2 + u) * NT, NT)
                            sp.dma_start(w[u][:], wv[:, :, cols]).then_inc(w_full[u], 16)
                            sp.wait_ge(o_full[u], i + l * (NC // 2))
                            sp.dma_start(b[u][:], bd[cols].partition_broadcast(2)).then_inc(w_full[u], 16)

            @block.scalar
            def _(act_e):
                act_e.wait_ge(cond_in, 32 * NL)
                nc.scalar.activation(act[:].rearrange("p l k r -> p l r k"), cond[:], ACT.Silu).then_inc(act_ready, 1)
                for l, (_, _, _, _, mod) in enumerate(layers):
                    with act_e.Fori(0, NC // 2) as i:
                        for u in range(2):
                            act_e.wait_ge(o_full[u], i + 1 + l * (NC // 2))
                            act_e.dma_start(mod[:, ds((i * 2 + u) * NT, NT)], o[u][:]).then_inc(o_out[u], 16)
                for u in range(2):
                    act_e.wait_ge(o_out[u], 16 * NL * (NC // 2))

            @block.tensor
            def _(pe):
                pe.wait_ge(act_ready, 1)
                for l in range(NL):
                    with pe.Fori(0, NC // 2) as i:
                        for u in range(2):
                            pe.wait_ge(w_full[u], (i + 1 + l * (NC // 2)) * 32)
                            pe.wait_ge(o_full[u], i + l * (NC // 2))
                            for k in range(KT):
                                mm = nc.tensor.matmul(ps[u][0:2, :], act[:, l, k, :], w[u][:, k, :],
                                                      start=(k == 0), stop=(k == KT - 1))
                            mm.then_inc(w_free[u], 1)

            @block.vector
            def _(dve):
                for l in range(NL):
                    with dve.Fori(0, NC // 2) as i:
                        for u in range(2):
                            dve.wait_ge(w_free[u], i + 1 + l * (NC // 2))
                            dve.wait_ge(o_out[u], (i + l * (NC // 2)) * 16)
                            nc.vector.tensor_tensor(o[u][:], ps[u][0:2, :], b[u][:], ALU.add).then_inc(o_full[u], 1)


def norm_project(nc, name, x_lat, x_ctx, mod, gain, w, out, groups, ident, eps):
    NLAT, NCTX = SEQ // P, CTX // P
    SPANS = [(x_lat, 0, 0, NLAT // 2, 0), (x_ctx, 1, SEQ, NCTX // 2, NLAT // 2)]
    CHUNKS = [(c * NT, NT) for c in range(SEQ // NT)] + [(SEQ, CTX)]
    with ExitStack() as ctx:
        s = Scope(nc, ctx, name)
        hT = s.sb("hT", [P, KT, T])
        with ExitStack() as ctx1:
            s1 = Scope(nc, ctx1, name + "n")
            idn = s1.sb("idn", [P, P])
            mv = s1.sb("mv", [P, 2, 2, KT])
            gn = s1.sb("gn", [P, KT])
            fac = s1.sb("fac", [P, 2, KT])
            x = [s1.sb(f"x{u}", [P, D]) for u in range(2)]
            xn = [s1.sb(f"xn{u}", [P, D]) for u in range(2)]
            st = [s1.sb(f"st{u}", [P, 2, 6]) for u in range(2)]
            ag = [s1.sb(f"ag{u}", [P, 2]) for u in range(2)]
            va = [s1.sb(f"va{u}", [P, 1]) for u in range(2)]
            sd = [s1.sb(f"sd{u}", [P, 1]) for u in range(2)]
            ps = s1.banks(4)
            aggr_turn = s1.sem("aggr_turn")
            const_in, fac_ready, chain = s1.sem("const_in"), s1.sem("fac_ready"), s1.sem("chain")
            x_full, xn_full = s1.sems("x_full", 2), s1.sems("xn_full", 2)
            var_ready, sd_ready = s1.sems("var_ready", 2), s1.sems("sd_ready", 2)
            tr_full, lo_free, hi_free = s1.sems("tr_full", 4), s1.sems("lo_free", 2), s1.sems("hi_free", 2)
            NCONST = 5 if gain is None else 6

            with nc.Block() as block:
                @block.sync
                def _(sp):
                    sp.dma_start(idn[:], ident).then_inc(const_in, 16)
                    for r in range(2):
                        for a in range(2):
                            sp.dma_start(mv[:, r, a, :], mod[r, a * D:(a + 1) * D].rearrange("(k p) -> p k", p=P),
                                         allow_slow_non_contiguous=True).then_inc(const_in, 16)
                    if gain is not None:
                        sp.dma_start(gn[:], gain.rearrange("(k p) -> p k", p=P), allow_slow_non_contiguous=True).then_inc(const_in, 16)
                    for src, _, _, rounds, before in SPANS:
                        with sp.Fori(0, rounds) as i:
                            for u in range(2):
                                sp.wait_ge(xn_full[u], i + before)
                                sp.dma_start(x[u][:], src[ds((i * 2 + u) * P, P), :]).then_inc(x_full[u], 16)

                @block.tensor
                def _(pe):
                    pe.wait_ge(const_in, 16 * NCONST)
                    for _, _, _, rounds, before in SPANS:
                        with pe.Fori(0, rounds) as i:
                            for u in range(2):
                                pe.wait_ge(xn_full[u], i + before + 1)
                                pe.wait_ge(lo_free[u], i + before)
                                pe.wait_ge(hi_free[u], i + before)
                                for k in range(KT):
                                    b = 2 * u + k // 4
                                    tr = nc.tensor.transpose(ps[b][:, (k % 4) * P:(k % 4 + 1) * P],
                                                             xn[u][:, k * P:(k + 1) * P], idn[:])
                                    if k % 4 == 3:
                                        tr.then_inc(tr_full[b], 1)

                @block.scalar
                def _(act):
                    act.wait_ge(const_in, 16 * NCONST)
                    act.wait_ge(fac_ready, 1)
                    for _, r, t0, rounds, before in SPANS:
                        with act.Fori(0, rounds) as i:
                            for u in range(2):
                                act.wait_ge(var_ready[u], i + before + 1)
                                nc.scalar.activation(sd[u][:], va[u][:], ACT.Sqrt).then_inc(sd_ready[u], 1)
                                act.wait_ge(tr_full[2 * u + 1], i + before + 1)
                                for j in range(4):
                                    k = 4 + j
                                    e = nc.scalar.activation(hT[:, k, ds((i * 2 + u) * P + t0, P)],
                                                             ps[2 * u + 1][:, j * P:(j + 1) * P], ACT.Identity,
                                                             bias=mv[:, r, 0, k:k + 1], scale=fac[:, r, k:k + 1])
                                e.then_inc(hi_free[u], 1)

                @block.vector
                def _(dve):
                    link = Chain(dve, chain)
                    dve.wait_ge(const_in, 16 * NCONST)
                    if gain is None:
                        nc.vector.tensor_scalar(fac[:], mv[:, :, 1, :], 1.0, None, ALU.add).then_inc(fac_ready, 1)
                        dve.wait_ge(fac_ready, 1)
                    else:
                        for r in range(2):
                            f = nc.vector.scalar_tensor_tensor(fac[:, r, :], mv[:, r, 1, :], 1.0, gn[:], ALU.add, ALU.mult)
                        f.then_inc(fac_ready, 1)
                        dve.wait_ge(fac_ready, 1)
                    for _, r, t0, rounds, before in SPANS:
                        with dve.Fori(0, rounds) as i:
                            link.body(i, 6 if gain is None else 8)
                            for u in range(2):
                                dve.wait_ge(x_full[u], (i + before + 1) * 16)
                                for h in range(2):
                                    b = nc.vector.bn_stats(st[u][:, h, :], x[u][:, h * NT:(h + 1) * NT])
                                link(b)
                                dve.sem_inc(aggr_turn, 1)
                                link(nc.vector.bn_aggr(ag[u][:], st[u][:]))
                                if gain is None:
                                    nc.vector.tensor_scalar(va[u][:], ag[u][:, 1:2], eps, None, ALU.add).then_inc(var_ready[u], 1)
                                else:
                                    link(nc.vector.scalar_tensor_tensor(va[u][:], ag[u][:, 0:1], ag[u][:, 0:1], ag[u][:, 1:2],
                                                                        ALU.mult, ALU.add))
                                    nc.vector.tensor_scalar(va[u][:], va[u][:], eps, None, ALU.add).then_inc(var_ready[u], 1)
                                dve.wait_ge(sd_ready[u], i + before + 1)
                                link(nc.vector.reciprocal(sd[u][:], sd[u][:]))
                                dve.wait_ge(tr_full[2 * u + 1], i + before)
                                if gain is None:
                                    n = nc.vector.tensor_scalar(xn[u][:], x[u][:], ag[u][:, 0:1], sd[u][:], ALU.subtract, ALU.mult)
                                else:
                                    n = nc.vector.tensor_scalar(xn[u][:], x[u][:], sd[u][:], None, ALU.mult)
                                n.then_inc(xn_full[u], 1)
                                dve.wait_ge(tr_full[2 * u], i + before + 1)
                                for k in range(4):
                                    e = nc.vector.tensor_scalar(hT[:, k, ds((i * 2 + u) * P + t0, P)],
                                                                ps[2 * u][:, k * P:(k + 1) * P],
                                                                fac[:, r, k:k + 1], mv[:, r, 0, k:k + 1], ALU.mult, ALU.add)
                                e.then_inc(lo_free[u], 1)
                        link.end(rounds)

        w_sb = [s.sb(f"w{u}", [P, KT, P]) for u in range(2)]
        o = [s.sb(f"o{u}", [P, T]) for u in range(2)]
        ps = s.banks(5)
        w_full, w_free, o_out = s.sems("w_full", 2), s.sems("w_free", 2), s.sems("o_out", 2)
        b_full, b_free = s.sems("b_full", 5), s.sems("b_free", 5)
        wv = w.rearrange("(k p) n -> p k n", p=P)

        def chunks(with_ctx):
            return list(enumerate(CHUNKS if with_ctx else CHUNKS[:-1]))

        def spans():
            by_slot, tiles, with_c = [0, 0], 0, 0
            for m0, m, with_ctx in groups:
                for first, slots, rounds in ((m0, 2, m // 2), (m0 + m // 2 * 2, 1, m % 2)):
                    if rounds:
                        yield first, slots, rounds, with_ctx, list(by_slot), tiles, with_c
                        for u in range(slots):
                            by_slot[u] += rounds
                        tiles += slots * rounds
                        with_c += slots * rounds * with_ctx
            ends[:] = by_slot

        ends = []

        with nc.Block() as block:
            @block.sync
            def _(sp):
                for m0, slots, rounds, _, before, _, _ in spans():
                    with sp.Fori(0, rounds) as i:
                        for u in range(slots):
                            sp.wait_ge(w_free[u], i + before[u])
                            sp.dma_start(w_sb[u][:], wv[:, :, ds((i * slots + u + m0) * P, P)]).then_inc(w_full[u], 16)

            @block.tensor
            def _(pe):
                for _, slots, rounds, with_ctx, before, tb, cb in spans():
                    with pe.Fori(0, rounds) as i:
                        for u in range(slots):
                            pe.wait_ge(w_full[u], (i + before[u] + 1) * 16)
                            for c, (t0, n) in chunks(with_ctx):
                                pe.wait_ge(b_free[c], i * slots + u + (cb if c == 4 else tb))
                                for k in range(KT):
                                    mm = nc.tensor.matmul(ps[c][:, 0:n], w_sb[u][:, k, :], hT[:, k, t0:t0 + n],
                                                          start=(k == 0), stop=(k == KT - 1))
                                mm.then_inc(b_full[c], 1)
                            pe.wait_ge(b_full[c], i * slots + u + 1 + (cb if c == 4 else tb))
                            pe.sem_inc(w_free[u], 1)

            def copy_out(eng, copy, i, u, slots, with_ctx, tb, cb, mine):
                for c, (t0, n) in chunks(with_ctx):
                    if c in mine:
                        eng.wait_ge(b_full[c], i * slots + u + 1 + (cb if c == 4 else tb))
                        copy(o[u][:, t0:t0 + n], ps[c][:, 0:n]).then_inc(b_free[c], 1)

            @block.vector
            def _(dve):
                for _, slots, rounds, with_ctx, before, tb, cb in spans():
                    with dve.Fori(0, rounds) as i:
                        for u in range(slots):
                            dve.wait_ge(o_out[u], (i + before[u]) * 16)
                            copy_out(dve, nc.vector.tensor_copy, i, u, slots, with_ctx, tb, cb, (0, 2, 4))

            @block.scalar
            def _(act):
                for m0, slots, rounds, with_ctx, before, tb, cb in spans():
                    with act.Fori(0, rounds) as i:
                        for u in range(slots):
                            act.wait_ge(o_out[u], (i + before[u]) * 16)
                            copy_out(act, nc.scalar.copy, i, u, slots, with_ctx, tb, cb, (1, 3))
                            for c, _ in chunks(with_ctx):
                                act.wait_ge(b_free[c], i * slots + u + 1 + (cb if c == 4 else tb))
                            width = T if with_ctx else SEQ
                            act.dma_start(out[ds((i * slots + u + m0) * P, P), 0:width], o[u][:, 0:width]).then_inc(o_out[u], 16)
                for u in range(2):
                    act.wait_ge(o_out[u], 16 * ends[u])


def out_project(nc, name, yT, zT, w, x_in, gate, kind, gain, bias, out, tiles, token0):
    a = ALPHA if kind == "ln" else 1.0
    with ExitStack() as ctx:
        s = Scope(nc, ctx, name)
        w_sb = s.sb("w", [P, KT, D])
        gate_r, gain_r, bias_r = s.sb("gate", [P, D]), s.sb("gain", [P, D]), s.sb("bias", [P, D])
        y = [s.sb(f"y{u}", [P, KT, P]) for u in range(2)]
        z = [s.sb(f"z{u}", [P, KT, P]) for u in range(2)]
        m = [s.sb(f"m{u}", [P, KT, P]) for u in range(2)]
        x = [s.sb(f"x{u}", [P, D]) for u in range(2)]
        r = [s.sb(f"r{u}", [P, D]) for u in range(2)]
        o = [s.sb(f"o{u}", [P, D]) for u in range(2)]
        st = [s.sb(f"st{u}", [P, 2, 6]) for u in range(2)]
        ag = [s.sb(f"ag{u}", [P, 2]) for u in range(2)]
        va = [s.sb(f"va{u}", [P, 1]) for u in range(2)]
        sd = [s.sb(f"sd{u}", [P, 1]) for u in range(2)]
        ps = s.banks(4)
        w_in, chain, aggr_turn = s.sem("w_in"), s.sem("chain"), s.sem("aggr_turn")
        yz_full, x_full = s.sems("yz_full", 2), s.sems("x_full", 2)
        silu_ready, mix_ready = s.sems("silu_ready", 2), s.sems("mix_ready", 2)
        y_full, res_ready = s.sems("y_full", 2), s.sems("res_ready", 2)
        var_ready, sd_ready = s.sems("var_ready", 2), s.sems("sd_ready", 2)
        o_full, o_out = s.sems("o_full", 2), s.sems("o_out", 2)
        rows = [gate] + ([gain] if kind != "plain" else []) + ([bias] if kind == "ln" else [])
        yv, zv = yT.rearrange("(k p) t -> p k t", p=P), zT.rearrange("(k p) t -> p k t", p=P)
        eps = 1e-5 if kind == "ln" else 1e-6
        rounds = tiles // 2

        with nc.Block() as block:
            @block.sync
            def _(sp):
                for row, dst in zip(rows, (gate_r, gain_r, bias_r)):
                    sp.dma_start(dst[:], row.partition_broadcast(P)).then_inc(w_in, 16)
                sp.dma_start(w_sb[:], w.rearrange("(k p) n -> p k n", p=P)).then_inc(w_in, 16)
                with sp.Fori(0, rounds) as i:
                    for u in range(2):
                        cols = ds((i * 2 + u) * P + token0, P)
                        sp.wait_ge(mix_ready[u], i)
                        sp.dma_start(y[u][:], yv[:, :, cols]).then_inc(yz_full[u], 16)
                        sp.dma_start(z[u][:], zv[:, :, cols]).then_inc(yz_full[u], 16)
                        sp.wait_ge(res_ready[u], i)
                        sp.dma_start(x[u][:], x_in[ds((i * 2 + u) * P, P), :]).then_inc(x_full[u], 16)

            @block.scalar
            def _(act):
                def silu(i, u):
                    act.wait_ge(yz_full[u], (i + 1) * 32)
                    nc.scalar.activation(z[u][:], z[u][:], ACT.Silu).then_inc(silu_ready[u], 1)

                def tail(i, u):
                    if kind != "plain":
                        act.wait_ge(var_ready[u], i + 1)
                        nc.scalar.activation(sd[u][:], va[u][:], ACT.Sqrt).then_inc(sd_ready[u], 1)
                    act.wait_ge(o_full[u], i + 1)
                    act.dma_start(out[ds((i * 2 + u) * P, P), :], o[u][:]).then_inc(o_out[u], 16)

                silu(0, 0)
                silu(0, 1)
                if rounds > 1:
                    with act.Fori(0, rounds - 1) as i:
                        for u in range(2):
                            silu(i + 1, u)
                            tail(i, u)
                tail(rounds - 1, 0)
                tail(rounds - 1, 1)
                for u in range(2):
                    act.wait_ge(o_out[u], 16 * rounds)

            @block.tensor
            def _(pe):
                pe.wait_ge(w_in, 16 * (len(rows) + 1))
                with pe.Fori(0, rounds) as i:
                    for u in range(2):
                        pe.wait_ge(mix_ready[u], i + 1)
                        pe.wait_ge(res_ready[u], i)
                        for h in range(2):
                            for k in range(KT):
                                mm = nc.tensor.matmul(ps[2 * u + h][:], m[u][:, k, :], w_sb[:, k, h * NT:(h + 1) * NT],
                                                      start=(k == 0), stop=(k == KT - 1))
                        mm.then_inc(y_full[u], 1)

            @block.vector
            def _(dve):
                link = Chain(dve, chain)
                dve.wait_ge(w_in, 16 * (len(rows) + 1))

                def mix(i, u):
                    dve.wait_ge(silu_ready[u], i + 1)
                    dve.wait_ge(y_full[u], i)
                    nc.vector.tensor_tensor(m[u][:], y[u][:], z[u][:], ALU.mult).then_inc(mix_ready[u], 1)

                def finish(i, u):
                    dve.wait_ge(y_full[u], i + 1)
                    dve.wait_ge(x_full[u], (i + 1) * 16)
                    for h in range(2):
                        c = slice(h * NT, (h + 1) * NT)
                        g = nc.vector.tensor_tensor(r[u][:, c], ps[2 * u + h][:], gate_r[:, c], ALU.mult)
                    link(g)
                    dve.wait_ge(o_out[u], i * 16)
                    dst = o if kind == "plain" else r
                    res = nc.vector.scalar_tensor_tensor(dst[u][:], x[u][:], a, r[u][:], ALU.mult, ALU.add)
                    res.then_inc(res_ready[u], 1)
                    if kind == "plain":
                        dve.wait_ge(res_ready[u], i + 1)
                        dve.sem_inc(o_full[u], 1)
                        return
                    dve.wait_ge(res_ready[u], i + 1)
                    for h in range(2):
                        b = nc.vector.bn_stats(st[u][:, h, :], r[u][:, h * NT:(h + 1) * NT])
                    link(b)
                    dve.sem_inc(aggr_turn, 1)
                    link(nc.vector.bn_aggr(ag[u][:], st[u][:]))
                    if kind == "ln":
                        link(nc.vector.tensor_copy(va[u][:], ag[u][:, 1:2]))
                    else:
                        link(nc.vector.scalar_tensor_tensor(va[u][:], ag[u][:, 0:1], ag[u][:, 0:1], ag[u][:, 1:2],
                                                            ALU.mult, ALU.add))
                    nc.vector.tensor_scalar(va[u][:], va[u][:], eps, None, ALU.add).then_inc(var_ready[u], 1)
                    dve.wait_ge(sd_ready[u], i + 1)
                    link(nc.vector.reciprocal(sd[u][:], sd[u][:]))
                    if kind == "ln":
                        link(nc.vector.tensor_scalar(r[u][:], r[u][:], ag[u][:, 0:1], sd[u][:], ALU.subtract, ALU.mult))
                        link(nc.vector.tensor_tensor(r[u][:], r[u][:], gain_r[:], ALU.mult))
                        nc.vector.tensor_tensor(o[u][:], r[u][:], bias_r[:], ALU.add).then_inc(o_full[u], 1)
                    else:
                        link(nc.vector.tensor_scalar(r[u][:], r[u][:], sd[u][:], None, ALU.mult))
                        nc.vector.tensor_tensor(o[u][:], r[u][:], gain_r[:], ALU.mult).then_inc(o_full[u], 1)

                steps = {"plain": 1, "ln": 7, "rms": 6}[kind]
                mix(0, 0)
                mix(0, 1)
                if rounds > 1:
                    with dve.Fori(0, rounds - 1) as i:
                        link.body(i, 2 * steps)
                        for u in range(2):
                            finish(i, u)
                            mix(i + 1, u)
                    link.end(rounds - 1)
                finish(rounds - 1, 0)
                finish(rounds - 1, 1)


POOL_CH, POOL_PAD = 256, 8


def pool_branch(nc, PT, w, scale, inv_count, yT):
    ROWS, W = SEQ // HD, HD
    WP = W + 2 * POOL_PAD
    with ExitStack() as ctx:
        s = Scope(nc, ctx, "pool")
        u = [s.sb(f"u{t}", [P, ROWS, WP]) for t in range(2)]
        a1, a2, a4, a8 = (s.sb(f"a{k}", [P, ROWS, WP]) for k in (1, 2, 4, 8))
        pooled = [s.sb(f"pooled{t}", [P, ROWS, W]) for t in range(2)]
        cnt = s.sb("cnt", [P, 2, W])
        wd = s.sb("wd", [P, 2, P])
        sc = s.sb("sc", [P, 2])
        o = [s.sb(f"o{t}", [P, SEQ]) for t in range(2)]
        ps = s.banks(4)
        zeroed, const_in, u_in = s.sem("zeroed"), s.sem("const_in"), s.sem("u_in")
        chain, pooled_ready, prod, scaled, stored = (s.sem(n) for n in ("chain", "pooled_ready", "prod", "scaled", "stored"))

        with nc.Block() as block:
            @block.sync
            def _(sp):
                sp.wait_ge(zeroed, 3)
                for t in range(2):
                    sp.dma_start(u[t][:, :, POOL_PAD:POOL_PAD + W],
                                 PT[t * P:(t + 1) * P, 0:SEQ].rearrange("p (r w) -> p r w", w=W)).then_inc(u_in, 16)
                sp.dma_start(cnt[:], inv_count).then_inc(const_in, 16)
                sp.dma_start(sc[:], scale.rearrange("(t p) -> p t", p=P), allow_slow_non_contiguous=True).then_inc(const_in, 16)
                for g in range(4):
                    h = g % 2 * HD
                    sp.dma_start(wd[h:h + HD, g // 2, h:h + HD], w[g]).then_inc(const_in, 16)
                for t in range(2):
                    sp.wait_ge(scaled, 4 * (t + 1))
                    sp.dma_start(yT[t * P:(t + 1) * P, 0:SEQ], o[t][:]).then_inc(stored, 16)
                sp.wait_ge(stored, 32)

            @block.vector
            def _(dve):
                link = Chain(dve, chain)
                for b in (u[0], u[1], wd):
                    nc.vector.memset(b[:], 0.0).then_inc(zeroed, 1)
                dve.wait_ge(u_in, 32)
                dve.wait_ge(const_in, 16 * 6)
                for t in range(2):
                    for dst, src, lo, hi, r in ((a1, u[t], 1, WP, (-1, 0)), (a2, a1, 2, WP - 1, (-1, 1)),
                                                (a4, a2, 4, WP - 3, (-2, 2)), (a8, a4, 8, WP - 7, (-4, 4))):
                        if t == 0 and dst in (a4, a8):
                            continue
                        link(nc.vector.tensor_tensor(dst[:, :, lo:hi], src[:, :, lo + r[0]:hi + r[0]],
                                                     src[:, :, lo + r[1]:hi + r[1]], ALU.add))
                    for h, sums in enumerate(((a1, a2), (a4, a8))[t]):
                        q = slice(h * HD, (h + 1) * HD)
                        link(nc.vector.tensor_tensor(pooled[t][q], sums[q, :, POOL_PAD:POOL_PAD + W],
                                                     cnt[q, t:t + 1, :].broadcast_to([HD, ROWS, W]), ALU.mult))
                    nc.vector.tensor_tensor(pooled[t][:], pooled[t][:], u[t][:, :, POOL_PAD:POOL_PAD + W], ALU.subtract
                                            ).then_inc(pooled_ready, 1)

            @block.tensor
            def _(pe):
                for t in range(2):
                    pe.wait_ge(pooled_ready, t + 1)
                    for c in range(4):
                        if t:
                            pe.wait_ge(scaled, c + 1)
                        nc.tensor.matmul(ps[c][:], wd[:, t, :], pooled[t][:, c * 8:(c + 1) * 8, :].rearrange("p r w -> p (r w)"),
                                         start=True, stop=True).then_inc(prod, 1)

            @block.scalar
            def _(act):
                for t in range(2):
                    for c in range(4):
                        act.wait_ge(prod, 4 * t + c + 1)
                        nc.scalar.activation(o[t][:, c * NT:(c + 1) * NT], ps[c][:], ACT.Copy, scale=sc[:, t:t + 1]).then_inc(scaled, 1)


D_R = 384
MT_R = D_R // P
CH = T // P
DECAY = 0.6065306597126334


def step_of(d, c):
    nl, ncx = SEQ // P, CTX // P
    if d == 0:
        return c - nl if c >= nl else c + ncx
    return ncx - 1 - (c - nl) if c >= nl else ncx + nl - 1 - c


def rwkv_inputs(nc, PT, row0, shift, w0, w_up, a0, a_up, k_k, k_a, r_k, head_ones, seg, R, E, bonusT):
    UW = T + 3
    SPLIT = [(0, SEQ, 1), (SEQ, CTX, SEQ + 2)]
    CHUNKS = [(c * NT, NT) for c in range(4)] + [(SEQ, CTX)]
    with ExitStack() as ctx:
        s = Scope(nc, ctx, "rin")
        raw = [s.sb(f"raw{i}", [P, UW]) for i in range(2)]
        tw, xa, r, k, v, kk, sg, a, cum, wi, w, tmp, t2, bon = (
            s.sb(n, [P, T]) for n in ("tw", "xa", "r", "k", "v", "kk", "sg", "a", "cum", "wi", "w", "tmp", "t2", "bon"))
        al, be, ka, rh = (s.sb(n, [P, T]) for n in ("al", "be", "ka", "rh"))
        e = s.sb("e", [P, 6, CH])
        sh = s.sb("sh", [P, 3, 11])
        prm = s.sb("prm", [P, 8, MT_R])
        rk = s.sb("rk", [P, 2, MT_R])
        wu, au = s.sb("wu", [P, D_R]), s.sb("au", [P, D_R])
        eps_col = s.sb("eps", [P, 1])
        ho, sgm = s.sb("ho", [P, P]), s.sb("sgm", [P, 2, T])
        ps = s.banks(8)
        const_in, raw_in, raw_used = s.sem("const_in"), s.sems("raw_in", 2), s.sems("raw_used", 2)
        chain, achain = s.sem("chain"), s.sem("achain")
        prod, taken = s.sem("prod"), s.sem("taken")
        tanh_ready, xa_ready, sq_ready, rt_ready = (s.sem(n) for n in ("tanh_ready", "xa_ready", "sq_ready", "rt_ready"))
        xw_ready, sig_ready, cum_ready, exp_ready, arrays_ready, dir_used = (
            s.sem(n) for n in ("xw_ready", "sig_ready", "cum_ready", "exp_ready", "arrays_ready", "dir_used"))
        stored, bon_ready, bon_sum, bon_out, pads = (s.sem(n) for n in ("stored", "bon_ready", "bon_sum", "bon_out", "pads"))
        ORDER = [9, 10] + [t for m in range(MT_R) for t in (m, 3 + m, 6 + m)]
        USES = []
        for m in range(MT_R):
            USES += [("norm", m, 0, c) for c in range(5)]
            for d in range(2):
                USES += [("w", m, d, c) for c in range(5)] + [("a", m, d, c) for c in range(5)]
            USES += [("bonus", m, 0, c) for c in range(4)]
        AT = {use: n for n, use in enumerate(USES)}

        with nc.Block() as block:
            @block.sync
            def _(sp):
                def col(dst, src):
                    sp.dma_start(dst, src, allow_slow_non_contiguous=True).then_inc(const_in, 16)
                for j in range(3):
                    col(sh[:, j, :], shift[j].rearrange("(t p) -> p t", p=P))
                for d in range(2):
                    col(prm[:, d, :], w0[d].rearrange("(t p) -> p t", p=P))
                    col(prm[:, 2 + d, :], a0[d].rearrange("(t p) -> p t", p=P))
                    col(rk[:, d, :], r_k[d].rearrange("(t h) k -> (h k) t", h=2))
                    sp.dma_start(wu[d * HD:(d + 1) * HD, :], w_up[d]).then_inc(const_in, 16)
                    sp.dma_start(au[d * HD:(d + 1) * HD, :], a_up[d]).then_inc(const_in, 16)
                col(prm[:, 4, :], k_k.rearrange("(t p) -> p t", p=P))
                col(prm[:, 5, :], k_a.rearrange("(t p) -> p t", p=P))
                sp.dma_start(ho[:], head_ones).then_inc(const_in, 16)
                sp.dma_start(sgm[:], seg).then_inc(const_in, 16)
                sp.wait_ge(pads, 3)
                for n, t in enumerate(ORDER):
                    if n >= 2:
                        sp.wait_ge(raw_used[n % 2], n // 2)
                    for t0, cnt, at in SPLIT:
                        sp.dma_start(raw[n % 2][:, at:at + cnt], PT[row0 + t * P:row0 + (t + 1) * P, t0:t0 + cnt]
                                     ).then_inc(raw_in[n % 2], 16)

            @block.gpsimd
            def _(pool):
                for b in (raw[0], raw[1]):
                    nc.gpsimd.memset(b[:], 0.0).then_inc(pads, 1)
                nc.gpsimd.memset(eps_col[:], 1e-12).then_inc(pads, 1)
                nst = 0
                for m in range(MT_R):
                    for d in range(2):
                        n = m * 2 + d
                        pool.wait_ge(arrays_ready, n + 1)
                        for j, arr in enumerate((al, rh, be, ka, v)):
                            for t0, cnt in ((0, SEQ // P), (SEQ // P, CTX // P)):
                                s0, step = step_of(d, t0), 1 if d == 0 else -1
                                lo = s0 if d == 0 else s0 - cnt + 1
                                dst = R[lo:lo + cnt, m, d, :, j, :].rearrange("c p t -> p c t")
                                if d:
                                    for c in range(cnt):
                                        pool.dma_start(R[s0 - c, m, d, :, j, :], arr[:, (t0 + c) * P:(t0 + c + 1) * P]).then_inc(stored, 16)
                                    nst += cnt
                                else:
                                    pool.dma_start(dst, arr[:, t0 * P:(t0 + cnt) * P].rearrange("p (c t) -> p c t", t=P)).then_inc(stored, 16)
                                    nst += 1
                        pool.wait_ge(stored, 16 * nst)
                        pool.sem_inc(dir_used, 1)
                    pool.wait_ge(bon_sum, m + 1)
                    pool.dma_start(bonusT[m * P:(m + 1) * P, :], bon[:, 0:SEQ]).then_inc(bon_out, 16)
                    pool.wait_ge(bon_out, 16 * (m + 1))
                pool.dma_start(E, e[:]).then_inc(bon_out, 16)
                pool.wait_ge(bon_out, 16 * (MT_R + 1))

            @block.vector
            def _(dve):
                link = Chain(dve, chain)
                dve.wait_ge(const_in, 16 * 17)
                link(nc.vector.tensor_scalar(prm[:, 6, :], prm[:, 5, :], -1.0, 1.0, ALU.mult, ALU.add))

                def shifted(n, dst):
                    t = ORDER[n]
                    dve.wait_ge(raw_in[n % 2], 32 * (n // 2 + 1))
                    src = raw[n % 2]
                    for j in range(3):
                        for t0, cnt, at in SPLIT:
                            x, o = src[:, at - 1 + j:at - 1 + j + cnt], dst[:, t0:t0 + cnt]
                            if j == 0:
                                ins = nc.vector.tensor_scalar(o, x, sh[:, 0, t:t + 1], None, ALU.mult)
                            else:
                                ins = nc.vector.scalar_tensor_tensor(o, x, sh[:, j, t:t + 1], o, ALU.mult, ALU.add)
                            last = ins
                        link(last)
                    dve.sem_inc(raw_used[n % 2], 1)

                shifted(0, tmp)
                dve.sem_inc(xw_ready, 1)
                shifted(1, xa)
                dve.sem_inc(xa_ready, 1)
                dve.wait_ge(tanh_ready, 1)
                for m in range(MT_R):
                    if m:
                        dve.wait_ge(dir_used, 2 * m)
                    for j, dst in enumerate((r, k, v)):
                        shifted(2 + 3 * m + j, dst)
                    link(nc.vector.tensor_scalar(kk[:], k[:], prm[:, 4, m:m + 1], None, ALU.mult))
                    nc.vector.tensor_tensor(tmp[:], kk[:], kk[:], ALU.mult).then_inc(sq_ready, 1)
                    dve.wait_ge(rt_ready, m + 1)
                    link(nc.vector.reciprocal(t2[:], t2[:]))
                    link(nc.vector.tensor_tensor(kk[:], kk[:], t2[:], ALU.mult))
                    for d in range(2):
                        n = m * 2 + d
                        dve.wait_ge(sig_ready, n + 1)
                        rev = slice(None, None, -1) if d else slice(None)
                        link(nc.vector.tensor_tensor_scan(cum[:, rev], sgm[:, d, rev], sg[:, rev], 0.0, ALU.mult, ALU.add))
                        nc.vector.tensor_tensor(tmp[:], cum[:], sg[:], ALU.subtract).then_inc(cum_ready, 1)
                        link(nc.vector.tensor_scalar(t2[:], a[:], prm[:, 5, m:m + 1], prm[:, 6, m:m + 1], ALU.mult, ALU.add))
                        link(nc.vector.tensor_tensor(t2[:], t2[:], k[:], ALU.mult))
                        link(nc.vector.tensor_tensor(a[:], a[:], kk[:], ALU.mult))
                        if d == 0:
                            if m:
                                dve.wait_ge(bon_out, 16 * m)
                            link(nc.vector.scalar_tensor_tensor(bon[:], r[:], rk[:, d, m:m + 1], t2[:], ALU.mult, ALU.mult))
                        dve.wait_ge(exp_ready, n + 1)
                        if n:
                            dve.wait_ge(dir_used, n)
                        link(nc.vector.tensor_tensor(be[:], a[:], wi[:], ALU.mult))
                        link(nc.vector.tensor_tensor(ka[:], t2[:], wi[:], ALU.mult))
                        link(nc.vector.tensor_tensor(rh[:], r[:], w[:], ALU.mult))
                        link(nc.vector.tensor_tensor(al[:], kk[:], tmp[:], ALU.mult))
                        at = P - 1 if d == 0 else 0
                        wv = w[:, :].rearrange("p (c t) -> p c t", t=P)[:, :, at]
                        for t0, cnt in ((0, SEQ // P), (SEQ // P, CTX // P)):
                            s0 = step_of(d, t0)
                            o = e[:, n, s0:s0 + cnt] if d == 0 else e[:, n, s0 - cnt + 1:s0 + 1]
                            src = wv[:, t0:t0 + cnt] if d == 0 else wv[:, t0:t0 + cnt][:, ::-1]
                            cp = nc.vector.tensor_copy(o, src)
                        cp.then_inc(arrays_ready, 1)
                        if d == 1:
                            link(nc.vector.scalar_tensor_tensor(t2[:], r[:], rk[:, d, m:m + 1], t2[:], ALU.mult, ALU.mult))
                            nc.vector.tensor_tensor(bon[:], bon[:], t2[:], ALU.add).then_inc(bon_ready, 1)
                            dve.wait_ge(bon_ready, m + 1)
                    for c in range(4):
                        q = AT[("bonus", m, 0, c)]
                        dve.wait_ge(prod, q + 1)
                        b = nc.vector.tensor_tensor(bon[:, c * NT:(c + 1) * NT], ps[q % 8][:], v[:, c * NT:(c + 1) * NT], ALU.mult)
                        b.then_inc(taken, 1)
                    dve.wait_ge(taken, AT[("bonus", m, 0, 3)] + 1)
                    dve.sem_inc(bon_sum, 1)

            @block.tensor
            def _(pe):
                pe.wait_ge(const_in, 16 * 17)
                pe.wait_ge(tanh_ready, 1)
                pe.wait_ge(xa_ready, 1)
                for q, (what, m, d, c) in enumerate(USES):
                    t0, n = CHUNKS[c]
                    if q >= 8:
                        pe.wait_ge(taken, q - 7)
                    out = ps[q % 8][:, 0:n]
                    h = slice(d * HD, (d + 1) * HD)
                    if what == "norm":
                        pe.wait_ge(sq_ready, m + 1)
                        mm = nc.tensor.matmul(out, ho[:], tmp[:, t0:t0 + n], start=True, stop=True)
                    elif what == "w":
                        mm = nc.tensor.matmul(out, wu[h, m * P:(m + 1) * P], tw[h, t0:t0 + n], start=True, stop=True)
                    elif what == "a":
                        mm = nc.tensor.matmul(out, au[h, m * P:(m + 1) * P], xa[h, t0:t0 + n], start=True, stop=True)
                    else:
                        pe.wait_ge(bon_ready, m + 1)
                        mm = nc.tensor.matmul(out, ho[:], bon[:, t0:t0 + n], start=True, stop=True)
                    mm.then_inc(prod, 1)

            @block.scalar
            def _(act):
                link = Chain(act, achain)
                act.wait_ge(const_in, 16 * 17)
                act.wait_ge(pads, 3)
                act.wait_ge(xw_ready, 1)
                nc.scalar.activation(tw[:], tmp[:], ACT.Tanh).then_inc(tanh_ready, 1)
                for m in range(MT_R):
                    for c, (t0, n) in enumerate(CHUNKS):
                        q = AT[("norm", m, 0, c)]
                        act.wait_ge(prod, q + 1)
                        nc.scalar.activation(t2[:, t0:t0 + n], ps[q % 8][:, 0:n], ACT.Sqrt, bias=eps_col[:, 0:1]).then_inc(taken, 1)
                    act.wait_ge(taken, q + 1)
                    act.sem_inc(rt_ready, 1)
                    for d in range(2):
                        nn = m * 2 + d
                        if nn:
                            act.wait_ge(arrays_ready, nn)
                        for what, dst, col in (("w", sg, d), ("a", a, 2 + d)):
                            for c, (t0, n) in enumerate(CHUNKS):
                                q = AT[(what, m, d, c)]
                                act.wait_ge(prod, q + 1)
                                nc.scalar.activation(dst[:, t0:t0 + n], ps[q % 8][:, 0:n], ACT.Sigmoid, bias=prm[:, col, m:m + 1]).then_inc(taken, 1)
                        act.wait_ge(taken, q + 1)
                        act.sem_inc(sig_ready, 1)
                        act.wait_ge(cum_ready, nn + 1)
                        link(nc.scalar.activation(w[:], cum[:], ACT.Exp, scale=-DECAY))
                        link(nc.scalar.activation(wi[:], cum[:], ACT.Exp, scale=DECAY))
                        nc.scalar.activation(tmp[:], tmp[:], ACT.Exp, scale=-DECAY).then_inc(exp_ready, 1)


def rwkv_scan(nc, R, E, masks, levels, ident, YR):
    NL = 4
    LV = 7
    X_AL, X_RH, X_BE, X_KA, X_V = range(5)
    NCX, NLT = CTX // P, SEQ // P
    BODY = [("gram", 1), ("first", 1)] + [(f"{w}{b}", 1) for b in range(1, LV) for w in "zn"] + [("x", 2), ("pt", 1)]
    KINDS = {False: BODY + [("chain", 1)], True: BODY + [("chain", 1), ("out", 2)]}

    with ExitStack() as ctx:
        s = Scope(nc, ctx, "rsc")
        X = [[s.sb(f"X{m}{d}", [P, 5, P]) for d in range(2)] for m in range(MT_R)]
        S = [[s.sb(f"S{m}{d}", [P, HD]) for d in range(2)] for m in range(MT_R)]
        TL = [s.sb(f"TL{d}", [P, 4, P]) for d in range(2)]
        M4 = [s.sb(f"M4{h}", [P, 4 * P]) for h in range(NL)]
        LB = [s.sb(f"LB{h}", [P, LV, P]) for h in range(NL)]
        W = [s.sb(f"W{h}", [P, HD + 2 * P]) for h in range(NL)]
        Z = [s.sb(f"Z{h}", [P, P]) for h in range(NL)]
        X12 = [s.sb(f"X12{h}", [P, P]) for h in range(NL)]
        X1T = [s.sb(f"X1T{h}", [P, P]) for h in range(NL)]
        PT = [s.sb(f"PT{h}", [P, HD]) for h in range(NL)]
        U = [s.sb(f"U{h}", [P, HD]) for h in range(NL)]
        Y = [[s.sb(f"Y{m}{d}", [P, P]) for d in range(2)] for m in range(MT_R)]
        mk = s.sb("mk", [P, 2, 4 * P])
        lv = s.sb("lv", [P, 2, LV, P])
        idn = s.sb("idn", [P, P])
        e = s.sb("e", [P, 6, CH])
        bank = s.banks(NL)
        tbank = [ctx.enter_context(nc.psum_tensor(f"rsc_tbank{d}", [P, 4, P], F32)) for d in range(2)]
        const_in, zeroed = s.sem("const_in"), s.sem("zeroed")
        x_in, x_used = s.sems("x_in", MT_R), s.sems("x_used", MT_R)
        prod, evac, lb_ready = s.sems("prod", NL), s.sems("evac", NL), s.sems("lb_ready", NL)
        t_prod, t_evac = s.sems("t_prod", 2), s.sems("t_evac", 2)
        y_out = s.sems("y_out", MT_R)

        def rows(h):
            return slice(h % 2 * HD, h % 2 * HD + HD)

        def counts(emit, i, m):
            p, v = (len(KINDS[emit]), sum(n for _, n in KINDS[emit]))
            p0, v0 = (len(KINDS[False]) * MT_R * NCX, sum(n for _, n in KINDS[False]) * MT_R * NCX) if emit else (0, 0)
            u0 = NCX * MT_R if emit else 0
            return (i * MT_R + m) * p + p0, (i * MT_R + m) * v + v0, i * MT_R + m + u0

        def scan(eng, unit):
            with eng.Fori(0, NCX) as i:
                for m in range(MT_R):
                    unit(False, i, m, *counts(False, i, m))
            with eng.Fori(0, NLT) as i:
                for m in range(MT_R):
                    unit(True, i, m, *counts(True, i, m))

        def walk(emit):
            v = 0
            for n, (name, k) in enumerate(KINDS[emit]):
                yield name, n, v
                v += k

        with nc.Block() as block:
            @block.sync
            def _(sp):
                for dst, src in ((mk, masks), (lv, levels), (idn, ident), (e, E)):
                    sp.dma_start(dst[:], src).then_inc(const_in, 16)

                def unit(emit, i, m, p, v, n):
                    step = i + NCX if emit else i
                    sp.wait_ge(x_used[m], step)
                    for d in range(2):
                        sp.dma_start(X[m][d][:], R[ds(step, 1), m, d].rearrange("o p a t -> p (o a) t")).then_inc(x_in[m], 16)

                scan(sp, unit)

            @block.gpsimd
            def _(pool):
                for m in range(MT_R):
                    for d in range(2):
                        nc.gpsimd.memset(S[m][d][:], 0.0).then_inc(zeroed, 1)
                pool.wait_ge(const_in, 64)

                def unit(emit, i, m, p, v, n):
                    for h in range(NL):
                        pool.wait_ge(evac[h], v + 1)
                        nc.gpsimd.tensor_tensor(LB[h][:], M4[h][:, 0:P].unsqueeze(1).broadcast_to([P, LV, P]),
                                                lv[:, h // 2, :, :], ALU.mult).then_inc(lb_ready[h], 1)
                        pool.wait_ge(lb_ready[h], n * 2 + 1)
                        nc.gpsimd.tensor_tensor(W[h][:, HD + P:], LB[h][:, 0, :], idn[:], ALU.add).then_inc(lb_ready[h], 1)

                scan(pool, unit)

            @block.tensor
            def _(pe):
                pe.wait_ge(const_in, 64)
                pe.wait_ge(zeroed, 6)

                def mm(out, l, r, start=True, stop=True):
                    return nc.tensor.matmul(out, l, r, start=start, stop=stop)

                def unit(emit, i, m, p, v, n):
                    step = i + NCX if emit else i
                    pe.wait_ge(x_in[m], (step + 1) * 32)
                    for d in range(2):
                        pe.wait_ge(t_evac[d], n)
                        for j, a in enumerate((X_AL, X_BE, X_KA, X_V)):
                            t = nc.tensor.transpose(tbank[d][:, j, :], X[m][d][:, a, :], idn[:])
                        t.then_inc(t_prod[d], 1)
                    for name, pn, vn in walk(emit):
                        for h in range(NL):
                            d, q, b = h // 2, rows(h), bank[h]
                            x, w = X[m][d], W[h]
                            pe.wait_ge(evac[h], v + vn)
                            if name == "gram":
                                mm(b[:, 0:2 * P], x[q, X_BE, :], x[q, X_AL:X_RH + 1, :].rearrange("p a t -> p (a t)"))
                                last = mm(b[:, 2 * P:], x[q, X_KA, :], x[q, X_AL:X_RH + 1, :].rearrange("p a t -> p (a t)"))
                            elif name == "first":
                                if h % 2 == 0:
                                    pe.wait_ge(t_evac[d], n + 1)
                                pe.wait_ge(lb_ready[h], n * 2 + 2)
                                mm(b[:, 0:HD], M4[h][:, 2 * P:3 * P], TL[d][:, 3, q])
                                last = nc.tensor.transpose(b[:, HD:HD + P], w[:, HD + P:], idn[:])
                            elif name[0] == "z":
                                last = mm(b[:, 0:P], LB[h][:, int(name[1]), :], w[:, HD:HD + P])
                            elif name[0] == "n":
                                if int(name[1]) < LV - 1:
                                    mm(b[:, P:2 * P], w[:, HD + P:], Z[h][:])
                                last = mm(b[:, 2 * P:3 * P], Z[h][:], w[:, HD + P:])
                            elif name == "x":
                                mm(b[:, 0:HD], w[:, HD + P:], TL[d][:, 0, q])
                                mm(b[:, HD:P], w[:, HD + P:], w[:, 0:HD])
                                last = mm(b[q, P:2 * P], TL[d][:, 0, q], w[:, HD + P:])
                            elif name == "pt":
                                last = mm(b[q, 0:HD], X12[h][:, 0:HD], TL[d][:, 1, q])
                            elif name == "chain":
                                if emit:
                                    mm(b[:, 0:HD], X1T[h][q, :], S[m][d][q, :])
                                mm(b[q, HD:P], TL[d][:, 2, q], TL[d][:, 3, q], stop=False)
                                mm(b[q, HD:P], PT[h][q, :], S[m][d][q, :], start=False, stop=False)
                                last = mm(b[q, HD:P], TL[d][:, 1, q], X12[h][:, HD:P], start=False)
                            else:
                                mm(b[q, P:2 * P], TL[d][:, 3, q], M4[h][:, 3 * P:], stop=False)
                                mm(b[q, P:2 * P], S[m][d][q, :], x[q, X_RH, :], start=False, stop=False)
                                last = mm(b[q, P:2 * P], U[h][:], M4[h][:, P:2 * P], start=False)
                            last.then_inc(prod[h], 1)

                scan(pe, unit)

            @block.scalar
            def _(act):
                act.wait_ge(const_in, 64)

                def unit(emit, i, m, p, v, n):
                    for d in range(2):
                        act.wait_ge(t_prod[d], n + 1)
                        nc.scalar.copy(TL[d][:], tbank[d][:]).then_inc(t_evac[d], 1)
                    for name, pn, vn in walk(emit):
                        for h in range(NL):
                            d, q, b = h // 2, rows(h), bank[h]
                            if name == "first":
                                act.wait_ge(prod[h], p + pn + 1)
                                nc.scalar.copy(W[h][:, 0:HD + P], b[:, 0:HD + P]).then_inc(evac[h], 1)
                            elif name[0] == "z":
                                act.wait_ge(prod[h], p + pn + 1)
                                nc.scalar.copy(Z[h][:], b[:, 0:P]).then_inc(evac[h], 1)
                            elif name == "x":
                                act.wait_ge(prod[h], p + pn + 1)
                                nc.scalar.mul(X12[h][:], b[:, 0:P], -1.0).then_inc(evac[h], 1)
                                nc.scalar.mul(X1T[h][q, :], b[q, P:2 * P], -1.0).then_inc(evac[h], 1)
                    if emit:
                        for h in range(NL):
                            act.wait_ge(evac[h], v + sum(k for _, k in KINDS[True]))
                        for d in range(2):
                            tok = (i * P) if d == 0 else (i * -P + (NLT - 1) * P)
                            act.dma_start(YR[d, m * P:(m + 1) * P, ds(tok, P)], Y[m][d][:]).then_inc(y_out[m], 16)

                scan(act, unit)
                for m in range(MT_R):
                    act.wait_ge(y_out[m], 32 * NLT)

            @block.vector
            def _(dve):
                dve.wait_ge(const_in, 64)

                def unit(emit, i, m, p, v, n):
                    step = i + NCX if emit else i
                    for name, pn, vn in walk(emit):
                        for h in range(NL):
                            d, q, b = h // 2, rows(h), bank[h]
                            if name in ("first", "x") or name[0] == "z":
                                continue
                            dve.wait_ge(prod[h], p + pn + 1)
                            if name == "gram":
                                ins = nc.vector.tensor_tensor(M4[h][:], b[:], mk[:, d, :], ALU.mult)
                            elif name[0] == "n":
                                lo = P if int(name[1]) < LV - 1 else 2 * P
                                w = W[h][:, HD + lo - P:]
                                ins = nc.vector.tensor_tensor(w, w, b[:, lo:3 * P], ALU.subtract)
                            elif name == "pt":
                                ins = nc.vector.tensor_tensor(PT[h][q, :], b[q, 0:HD], idn[q, q], ALU.add)
                            elif name == "chain" and emit:
                                ins = nc.vector.tensor_tensor(U[h][:], b[:, 0:HD], X12[h][:, HD:P], ALU.add)
                            else:
                                ins = nc.vector.tensor_scalar(S[m][d][q, :], b[q, HD:P],
                                                              e[q, m * 2 + d, ds(step, 1)], None, ALU.mult)
                                if emit:
                                    ins.then_inc(evac[h], 1)
                                    if h == 0:
                                        dve.wait_ge(y_out[m], i * 32)
                                    ins = nc.vector.tensor_copy(Y[m][d][q, :], b[q, P:2 * P])
                            ins.then_inc(evac[h], 1)
                    dve.sem_inc(x_used[m], 1)

                scan(dve, unit)


def hgrn(nc, PT, q0, i0, z0, seg, masks, ident, YH):
    LV = 7
    HALF = SEQ // 2
    HC = HALF // P
    NLT, NCX = SEQ // P, CTX // P
    WALK = [(d, c) for d in range(2) for c in sorted(range(CH), key=lambda c: step_of(d, c))]
    LAT = [(d, c) for d, c in WALK if c < NLT]
    NW, NL = len(WALK), len(LAT)
    with ExitStack() as ctx:
        s = Scope(nc, ctx, "hg")
        q, v, z, cum = s.sb("q", [P, SEQ]), s.sb("v", [P, T]), s.sb("z", [P, T]), s.sb("cum", [P, T])
        k = [s.sb(f"k{d}", [P, T]) for d in range(2)]
        qe = [s.sb(f"qe{d}", [P, SEQ]) for d in range(2)]
        ke = [s.sb(f"ke{d}", [P, T]) for d in range(2)]
        ec = [s.sb(f"ec{d}", [P, CH]) for d in range(2)]
        LVL = [s.sb(f"lv{u}", [P, LV, HALF]) for u in range(2)]
        sgm, mk, idn = s.sb("sgm", [P, T]), s.sb("mk", [P, 2, LV + 1, P]), s.sb("idn", [P, P])
        KI = [s.sb(f"KI{u}", [P, 2, P]) for u in range(2)]
        PR = [[s.sb(f"P{u}{h}", [P, LV + 1, P]) for h in range(2)] for u in range(2)]
        S = [s.sb(f"S{u}", [P, HD]) for u in range(2)]
        Y = [s.sb(f"Y{u}", [P, HALF]) for u in range(2)]
        sc = [ctx.enter_context(nc.psum_tensor(f"hg_sc{h}", [P, LV + 1, P], F32)) for h in range(2)]
        tb = [ctx.enter_context(nc.psum_tensor(f"hg_tb{u}", [P, 2, P], F32)) for u in range(2)]
        yb = s.banks(2)
        const_in = s.sem("const_in")
        qv_in, z_in, seg_in, qv_used = s.sem("qv_in"), s.sem("z_in"), s.sem("seg_in"), s.sem("qv_used")
        chain, achain = s.sem("chain"), s.sem("achain")
        ln_ready, arg_ready, cum_ready, kearg_ready, exp_ready = (
            s.sem(n) for n in ("ln_ready", "arg_ready", "cum_ready", "kearg_ready", "exp_ready"))
        kq_ready, lvarg, lvexp, lvl_ready = s.sem("kq_ready"), s.sems("lvarg", 2), s.sems("lvexp", 2), s.sems("lvl_ready", 2)
        sc_prod, sc_evac = s.sems("sc_prod", 2), s.sems("sc_evac", 2)
        t_prod, t_evac, y_prod, y_evac = s.sems("t_prod", 2), s.sems("t_evac", 2), s.sems("y_prod", 2), s.sems("y_evac", 2)
        y_out, lv_used = s.sems("y_out", 2), s.sems("lv_used", 2)

        def runs(d):
            return [(0, 0), (1, HALF)] if d == 0 else [(0, HALF), (1, 0)]

        def halves(ap, b, d):
            x = ap.rearrange("p (n h b) -> p n h b", h=2, b=b)
            return (x[:, :, 1, :], x[:, :, 0, :], x[:, :, 0, b - 1:b]) if d == 0 else (x[:, :, 0, :], x[:, :, 1, :], x[:, :, 1, 0:1])

        with nc.Block() as block:
            @block.sync
            def _(sp):
                sp.dma_start(mk[:], masks).then_inc(const_in, 16)
                sp.dma_start(idn[:], ident).then_inc(const_in, 16)
                with sp.Fori(0, MT_R) as m:
                    for d in range(2):
                        sp.wait_ge(cum_ready, m * 2 + d)
                        sp.dma_start(z[:], PT[ds(m * P + (z0 + d * D_R), P), :]).then_inc(z_in, 16)
                        sp.dma_start(sgm[:], seg[:, d, :]).then_inc(z_in, 16)
                        if d == 0:
                            sp.wait_ge(y_evac[0], m * (NW // 2))
                            sp.wait_ge(y_evac[1], m * (NW // 2))
                            sp.dma_start(q[:], PT[ds(m * P + q0, P), 0:SEQ]).then_inc(qv_in, 16)
                            sp.dma_start(v[:], PT[ds(m * P + i0, P), :]).then_inc(qv_in, 16)
                    for d in range(2):
                        for w, t0 in runs(d):
                            n = d * CH + NCX + HC * (w + 1) - 1
                            for b in range(2):
                                sp.wait_ge(y_evac[b], m * (NW // 2) + (n - (n % 2 != b)) // 2 + 1)
                            sp.dma_start(YH[d, ds(m * P, P), t0:t0 + HALF], Y[w][:]).then_inc(y_out[w], 16)
                for w in range(2):
                    sp.wait_ge(y_out[w], 16 * 2 * MT_R)

            @block.gpsimd
            def _(pool):
                with pool.Fori(0, MT_R) as m:
                    for d in range(2):
                        pool.wait_ge(kearg_ready, m * 2 + d + 1)
                        for u, t0 in runs(d):
                            pool.wait_ge(lv_used[u], m * 2 + d)
                            for j in range(LV):
                                later, earlier, r = halves(cum[:, t0:t0 + HALF], 2 ** j, d)
                                lo, eo, _ = halves(LVL[u][:, j, :], 2 ** j, d)
                                rb = r.broadcast_to([P, HALF >> (j + 1), 2 ** j])
                                nc.gpsimd.tensor_tensor(lo, later, rb, ALU.subtract)
                                last = nc.gpsimd.tensor_tensor(eo, rb, earlier, ALU.subtract)
                            last.then_inc(lvarg[u], 1)

            @block.scalar
            def _(act):
                act.wait_ge(const_in, 32)
                link = Chain(act, achain)

                def transposed(n, m):
                    u = n % 2
                    act.wait_ge(t_prod[u], m * (NW // 2) + n // 2 + 1)
                    nc.scalar.copy(KI[u][:], tb[u][:]).then_inc(t_evac[u], 1)

                with act.Fori(0, MT_R) as m:
                    link.body(m, 4)
                    for d in range(2):
                        act.wait_ge(z_in, (m * 2 + d + 1) * 32)
                        if d == 0:
                            act.wait_ge(y_evac[0], m * (NW // 2))
                            act.wait_ge(y_evac[1], m * (NW // 2))
                        link(nc.scalar.activation(k[d][:], z[:], ACT.Abs))
                        link(nc.scalar.activation(k[d][:], k[d][:], ACT.Exp, scale=-1.0))
                        nc.scalar.activation(k[d][:], k[d][:], ACT.Ln, bias=1.0).then_inc(ln_ready, 1)
                        act.wait_ge(kearg_ready, m * 2 + d + 1)
                        nc.scalar.activation(k[d][:], k[d][:], ACT.Exp)
                        nc.scalar.activation(qe[d][:], cum[:, 0:SEQ], ACT.Exp)
                        at = P - 1 if d == 0 else 0
                        nc.scalar.activation(ec[d][:], cum[:].rearrange("p (c t) -> p c t", t=P)[:, :, at], ACT.Exp)
                        nc.scalar.activation(ke[d][:], ke[d][:], ACT.Exp).then_inc(exp_ready, 1)
                        for u, t0 in runs(d):
                            act.wait_ge(lvarg[u], m * 2 + d + 1)
                            nc.scalar.activation(LVL[u][:], LVL[u][:], ACT.Exp).then_inc(lvexp[u], 1)
                        for n in range(d * CH, (d + 1) * CH):
                            transposed(n, m)

            @block.vector
            def _(dve):
                link = Chain(dve, chain)
                dve.wait_ge(const_in, 32)

                def prepare(m, d):
                    dve.wait_ge(ln_ready, m * 2 + d + 1)
                    link(nc.vector.scalar_tensor_tensor(ke[d][:], z[:], 0.0, k[d][:], ALU.min, ALU.subtract))
                    link(nc.vector.tensor_tensor(k[d][:], ke[d][:], z[:], ALU.subtract))
                    rev = slice(None, None, -1) if d else slice(None)
                    for u in range(2):
                        dve.wait_ge(lvarg[u], m * 2 + d)
                    nc.vector.tensor_tensor_scan(cum[:, rev], sgm[:, rev], ke[d][:, rev], 0.0, ALU.mult, ALU.add).then_inc(cum_ready, 1)
                    dve.wait_ge(cum_ready, m * 2 + d + 1)
                    at = P - 1 if d == 0 else 0
                    cv = cum[:].rearrange("p (c t) -> p c t", t=P)
                    nc.vector.tensor_tensor(ke[d][:].rearrange("p (c t) -> p c t", t=P), cv[:, :, at:at + 1].broadcast_to([P, CH, P]),
                                            cv, ALU.subtract).then_inc(kearg_ready, 1)
                    dve.wait_ge(exp_ready, m * 2 + d + 1)
                    dve.wait_ge(qv_in, (m + 1) * 32)
                    nc.vector.tensor_tensor(ke[d][:], ke[d][:], k[d][:], ALU.mult)
                    nc.vector.tensor_tensor(qe[d][:], qe[d][:], q[:], ALU.mult).then_inc(kq_ready, 1)

                def scale(m, d, u, t0):
                    dve.wait_ge(lvexp[u], m * 2 + d + 1)
                    for j in range(LV):
                        lo, eo, _ = halves(LVL[u][:, j, :], 2 ** j, d)
                        lq, _, _ = halves(q[:, t0:t0 + HALF], 2 ** j, d)
                        _, ek, _ = halves(k[d][:, t0:t0 + HALF], 2 ** j, d)
                        nc.vector.tensor_tensor(lo, lo, lq, ALU.mult)
                        last = nc.vector.tensor_tensor(eo, eo, ek, ALU.mult)
                    last.then_inc(lvl_ready[u], 1)

                def scores(m, n, h):
                    d, c = WALK[n]
                    nl = LAT.index((d, c))
                    dve.wait_ge(sc_prod[h], m * NL + nl + 1)
                    nc.vector.tensor_tensor(PR[n % 2][h][:], sc[h][:], mk[:, d], ALU.mult).then_inc(sc_evac[h], 1)

                def chunk_out(m, n):
                    d, c = WALK[n]
                    u = n % 2
                    dve.wait_ge(y_prod[u], m * (NW // 2) + n // 2 + 1)
                    if n:
                        dve.wait_ge(y_evac[1 - u], m * (NW // 2) + (n + 1) // 2)
                    if n % CH == 0:
                        st = nc.vector.tensor_copy(S[u][:], yb[u][:, P:P + HD])
                    else:
                        st = nc.vector.scalar_tensor_tensor(S[u][:], S[1 - u][:], ec[d][:, c:c + 1], yb[u][:, P:P + HD], ALU.mult, ALU.add)
                    if c < NLT:
                        nl = LAT.index((d, c))
                        w = nl // HC % 2
                        if nl % HC == 0:
                            dve.wait_ge(y_out[w], (m * 2 + d) * 16)
                        t = (c * P) % HALF
                        st = nc.vector.tensor_copy(Y[w][:, t:t + P], yb[u][:, 0:P])
                    st.then_inc(y_evac[u], 1)

                with dve.Fori(0, MT_R) as m:
                    link.body(m, 4)
                    for d in range(2):
                        prepare(m, d)
                        for n in range(d * CH, (d + 1) * CH):
                            k0 = n - d * CH
                            if k0 >= NCX and (k0 - NCX) % HC == 0:
                                scale(m, d, *runs(d)[(k0 - NCX) // HC])
                            if WALK[n][1] < NLT:
                                for h in range(2):
                                    scores(m, n, h)
                                if (k0 - NCX) % HC == HC - 1:
                                    dve.sem_inc(lv_used[(k0 - NCX) // HC], 1)
                            if n:
                                chunk_out(m, n - 1)
                    chunk_out(m, NW - 1)

            @block.tensor
            def _(pe):
                pe.wait_ge(const_in, 32)

                def front(m, n):
                    d, c = WALK[n]
                    u, t = n % 2, slice(c * P, (c + 1) * P)
                    if n % CH == 0:
                        pe.wait_ge(kq_ready, m * 2 + d + 1)
                    pe.wait_ge(t_evac[u], m * (NW // 2) + n // 2)
                    nc.tensor.transpose(tb[u][:, 0, :], ke[d][:, t], idn[:])
                    nc.tensor.transpose(tb[u][:, 1, :], v[:, t], idn[:]).then_inc(t_prod[u], 1)
                    if c >= NLT:
                        return
                    nl = LAT.index((d, c))
                    w = nl // HC % 2
                    if nl % HC == 0:
                        pe.wait_ge(lvl_ready[w], m * 2 + d + 1)
                    tl = slice(c * P % HALF, c * P % HALF + P)
                    for h in range(2):
                        r = slice(h * HD, (h + 1) * HD)
                        pe.wait_ge(sc_evac[h], m * NL + nl)
                        for j in range(LV):
                            nc.tensor.matmul(sc[h][:, j, :], LVL[w][r, j, tl], LVL[w][r, j, tl], start=True, stop=True)
                        nc.tensor.matmul(sc[h][:, LV, :], k[d][r, t], q[r, t], start=True, stop=True).then_inc(sc_prod[h], 1)

                def back(m, n):
                    d, c = WALK[n]
                    u, t = n % 2, slice(c * P, (c + 1) * P)
                    pe.wait_ge(t_evac[u], m * (NW // 2) + n // 2 + 1)
                    pe.wait_ge(y_evac[u], m * (NW // 2) + n // 2)
                    pe.wait_ge(y_evac[1 - u], m * (NW // 2) + (n + 1) // 2)
                    if c < NLT:
                        nl = LAT.index((d, c))
                        for h in range(2):
                            pe.wait_ge(sc_evac[h], m * NL + nl + 1)
                    for h in range(2):
                        r = slice(h * HD, (h + 1) * HD)
                        last = nc.tensor.matmul(yb[u][r, P:P + HD], KI[u][:, 0, r], KI[u][:, 1, r], start=True, stop=True)
                        if c < NLT:
                            for j in range(LV + 1):
                                nc.tensor.matmul(yb[u][r, 0:P], KI[u][:, 1, r], PR[u][h][:, j, :], start=(j == 0), stop=False)
                            last = nc.tensor.matmul(yb[u][r, 0:P], S[1 - u][r, :], qe[d][r, t], start=False, stop=True)
                    last.then_inc(y_prod[u], 1)

                with pe.Fori(0, MT_R) as m:
                    front(m, 0)
                    for n in range(NW):
                        if n + 1 < NW:
                            front(m, n + 1)
                        back(m, n)


def head_norm(nc, name, items, mean_ones, rope=None):
    with ExitStack() as ctx:
        s = Scope(nc, ctx, name)
        WMAX = max(it["w"] for it in items)
        NI = len(items)
        a, b, p = ([s.sb(f"{n}{h}", [P, WMAX]) for h in range(2)] for n in "abp")
        g = s.sb("g", [P, NI, 2])
        ep = s.sb("ep", [P, NI])
        mo = s.sb("mo", [P, P])
        cs = s.sb("cs", [P, 2, SEQ if rope else 1])
        sw = s.sb("sw", [P, P])
        banks = s.banks(8)
        bank = [banks[0:4], banks[4:8]]
        const_in, set_up = s.sem("const_in"), s.sem("set_up")
        a_in, stored = s.sems("a_in", 2), s.sems("stored", 2)
        prod, sums, done = s.sems("prod", 2), s.sems("sums", 2), s.sems("done", 2)
        squared, root = s.sems("squared", 2), s.sems("root", 2)
        chain = s.sem("chain")
        NCONST = 1 + sum(P // it[key].shape[0] for it in items for key in ("gain", "bias") if it[key] is not None) + (3 if rope else 0)

        def chunks(it):
            return [(j, j * NT, min(NT, it["w"] - j * NT)) for j in range(-(-it["w"] // NT))]

        def groups():
            for n in range(0, NI, 2):
                yield [(h, n + h, items[n + h]) for h in range(2) if n + h < NI]

        def before(n, what):
            return sum(what(items[k]) for k in range(n % 2, n, 2))

        def loads(it):
            return 1 + (it["b"] is not None) + (it["plus"] is not None)

        def prods(it):
            return it["center"] + 1 + it["rotate"]

        with nc.Block() as block:
            @block.sync
            def _(sp):
                sp.dma_start(mo[:], mean_ones).then_inc(const_in, 16)
                if rope:
                    for dst, src in ((cs[:, 0, :], rope[0]), (cs[:, 1, :], rope[1]), (sw[:], rope[2])):
                        sp.dma_start(dst, src).then_inc(const_in, 16)
                for n, it in enumerate(items):
                    for j, key in enumerate(("gain", "bias")):
                        if it[key] is not None:
                            v = it[key]
                            for r in range(P // v.shape[0]):
                                sp.dma_start(g[r * v.shape[0]:(r + 1) * v.shape[0], n, j:j + 1], v.rearrange("(p o) -> p o", o=1)
                                             ).then_inc(const_in, 16)
                for gr in groups():
                    for h, n, it in gr:
                        if n >= 2:
                            sp.wait_ge(stored[h], 16 * (n // 2))
                        for dst, key in ((a, "a"), (b, "b"), (p, "plus")):
                            if it[key] is not None:
                                sp.dma_start(dst[h][:, 0:it["w"]], it[key]).then_inc(a_in[h], 16)

            @block.gpsimd
            def _(pool):
                for n, it in enumerate(items):
                    nc.gpsimd.memset(ep[:, n:n + 1], it["eps"]).then_inc(set_up, 1)

            @block.vector
            def _(dve):
                link = Chain(dve, chain)
                dve.wait_ge(const_in, 16 * NCONST)
                for gr in groups():
                    for h, n, it in gr:
                        w = it["w"]
                        dve.wait_ge(a_in[h], 16 * (before(n, loads) + loads(it)))
                        if it["b"] is not None:
                            nc.vector.tensor_tensor(a[h][:, 0:w], a[h][:, 0:w], b[h][:, 0:w], ALU.add).then_inc(sums[h], 1)
                        else:
                            dve.sem_inc(sums[h], 1)
                    for h, n, it in gr:
                        if it["center"]:
                            dve.wait_ge(prod[h], before(n, prods) + 1)
                            for j, t, c in chunks(it):
                                x = nc.vector.tensor_tensor(a[h][:, t:t + c], a[h][:, t:t + c], bank[h][j][:, 0:c], ALU.subtract)
                            x.then_inc(done[h], 1)
                    for h, n, it in gr:
                        w = it["w"]
                        dve.wait_ge(root[h], n // 2 + 1)
                        link(nc.vector.reciprocal(b[h][:, 0:w], b[h][:, 0:w]))
                        link(nc.vector.tensor_tensor(a[h][:, 0:w], a[h][:, 0:w], b[h][:, 0:w], ALU.mult))
                        o = nc.vector.tensor_scalar(a[h][:, 0:w], a[h][:, 0:w], g[:, n, 0:1],
                                                    None if it["bias"] is None else g[:, n, 1:2], ALU.mult,
                                                    *(() if it["bias"] is None else (ALU.add,)))
                        if it["plus"] is not None:
                            link(o)
                            o = nc.vector.tensor_tensor(a[h][:, 0:w], a[h][:, 0:w], p[h][:, 0:w], ALU.add)
                        o.then_inc(done[h], 1)
                    for h, n, it in gr:
                        if it["rotate"]:
                            w = it["w"]
                            dve.wait_ge(prod[h], before(n, prods) + prods(it))
                            for j, t, c in chunks(it):
                                x = nc.vector.tensor_tensor(b[h][:, t:t + c], bank[h][j][:, 0:c], cs[:, 1, t:t + c], ALU.mult)
                            nc.vector.tensor_tensor(a[h][:, 0:w], a[h][:, 0:w], cs[:, 0, 0:w], ALU.mult).then_inc(chain, 1)
                            link.n += 1
                            dve.wait_ge(chain, link.base + link.n)
                            nc.vector.tensor_tensor(a[h][:, 0:w], a[h][:, 0:w], b[h][:, 0:w], ALU.add).then_inc(done[h], 1)

            def dones(it):
                return it["center"] + 1 + it["rotate"]

            @block.tensor
            def _(pe):
                pe.wait_ge(const_in, 16 * NCONST)
                for gr in groups():
                    for h, n, it in gr:
                        if n >= 2:
                            pe.wait_ge(done[h], before(n, dones))
                        if it["center"]:
                            pe.wait_ge(sums[h], n // 2 + 1)
                            for j, t, c in chunks(it):
                                x = nc.tensor.matmul(bank[h][j][:, 0:c], mo[:], a[h][:, t:t + c], start=True, stop=True)
                            x.then_inc(prod[h], 1)
                    for h, n, it in gr:
                        pe.wait_ge(squared[h], n // 2 + 1)
                        for j, t, c in chunks(it):
                            x = nc.tensor.matmul(bank[h][j][:, 0:c], mo[:], b[h][:, t:t + c], start=True, stop=True)
                        x.then_inc(prod[h], 1)
                    for h, n, it in gr:
                        if it["rotate"]:
                            pe.wait_ge(done[h], before(n, dones) + dones(it) - 1)
                            for j, t, c in chunks(it):
                                x = nc.tensor.matmul(bank[h][j][:, 0:c], sw[:], a[h][:, t:t + c], start=True, stop=True)
                            x.then_inc(prod[h], 1)

            @block.scalar
            def _(act):
                act.wait_ge(set_up, NI)
                for gr in groups():
                    for h, n, it in gr:
                        w = it["w"]
                        act.wait_ge(sums[h], n // 2 + 1)
                        if it["b"] is None:
                            act.wait_ge(a_in[h], 16 * (before(n, loads) + loads(it)))
                        if it["center"]:
                            act.wait_ge(done[h], before(n, dones) + 1)
                        nc.scalar.activation(b[h][:, 0:w], a[h][:, 0:w], ACT.Square).then_inc(squared[h], 1)
                    for h, n, it in gr:
                        act.wait_ge(prod[h], before(n, prods) + it["center"] + 1)
                        for j, t, c in chunks(it):
                            x = nc.scalar.activation(b[h][:, t:t + c], bank[h][j][:, 0:c], ACT.Sqrt, bias=ep[:, n:n + 1])
                        x.then_inc(root[h], 1)
                    for h, n, it in gr:
                        act.wait_ge(done[h], before(n, dones) + dones(it))
                        act.dma_start(it["out"], a[h][:, 0:it["w"]]).then_inc(stored[h], 16)
                for h in range(min(2, NI)):
                    act.wait_ge(stored[h], 16 * len(range(h, NI, 2)))


def conformer(nc, PT, w, b, ln_g, ln_b, ident, mean_ones, yT):
    NTL, K = 4, 31
    R = K // 2
    AT = [(0, SEQ, R), (SEQ, CTX, R + SEQ + R)]
    UW = R + SEQ + R + CTX + R
    CHUNKS = [(c * NT, NT) for c in range(4)] + [(SEQ, CTX)]
    ON_PE = (2, 3)
    with ExitStack() as ctx:
        s = Scope(nc, ctx, "cf")
        u = [s.sb(f"u{t}", [P, UW]) for t in range(NTL)]
        y = [s.sb(f"y{t}", [P, T]) for t in range(NTL)]
        g = [s.sb(f"g{i}", [P, T]) for i in range(2)]
        dg = s.sb("dg", [P, K, P])
        wt = s.sb("wt", [P, NTL, K])
        pr = s.sb("pr", [P, 3, NTL])
        idn, mo, ep = s.sb("idn", [P, P]), s.sb("mo", [P, P]), s.sb("ep", [P, 1])
        ps = s.banks(8)
        const_in, pads, g_in, u_in, gated, sig = (s.sem(n) for n in ("const_in", "pads", "g_in", "u_in", "gated", "sig"))
        dg_ready, tap_prod, tap_out, chain, conv_done = (s.sem(n) for n in ("dg_ready", "tap_prod", "tap_out", "chain", "conv_done"))
        mean_prod, centred, squared, var_prod, root, normed, acted, stored, used = (
            s.sem(n) for n in ("mean_prod", "centred", "squared", "var_prod", "root", "normed", "acted", "stored", "used"))

        with nc.Block() as block:
            @block.sync
            def _(sp):
                for t in range(NTL):
                    sp.dma_start(wt[:, t, :], w[:, t * P:(t + 1) * P].rearrange("k p -> p k"), allow_slow_non_contiguous=True).then_inc(const_in, 16)
                for j, v in enumerate((b, ln_g, ln_b)):
                    sp.dma_start(pr[:, j, :], v.rearrange("(t p) -> p t", p=P), allow_slow_non_contiguous=True).then_inc(const_in, 16)
                sp.dma_start(idn[:], ident).then_inc(const_in, 16)
                sp.dma_start(mo[:], mean_ones).then_inc(const_in, 16)
                sp.wait_ge(pads, NTL + 1)
                for n, t in enumerate((2, 0, 3, 1)):
                    for t0, cnt, at in AT:
                        sp.dma_start(u[t][:, at:at + cnt], PT[t * P:(t + 1) * P, t0:t0 + cnt]).then_inc(u_in, 16)
                    if n >= 2:
                        sp.wait_ge(gated, 2 * (n - 1))
                    sp.dma_start(g[n % 2][:], PT[(NTL + t) * P:(NTL + t + 1) * P, :]).then_inc(g_in, 16)
                    sp.wait_ge(g_in, 16 * (n + 1))
                    sp.wait_ge(u_in, 32 * (n + 1))
                for t in range(NTL):
                    sp.wait_ge(acted, t + 1)
                    sp.dma_start(yT[t * P:(t + 1) * P, :], y[t][:]).then_inc(stored, 16)
                sp.wait_ge(stored, 16 * NTL)

            @block.gpsimd
            def _(pool):
                for t in range(NTL):
                    nc.gpsimd.memset(u[t][:], 0.0).then_inc(pads, 1)
                nc.gpsimd.memset(ep[:], 1e-6).then_inc(pads, 1)
                pool.wait_ge(const_in, 16 * 9)
                for n, t in enumerate(ON_PE):
                    if n:
                        pool.wait_ge(tap_prod, 4)
                    for k in range(K):
                        nc.gpsimd.tensor_scalar(dg[:, k, :], idn[:], wt[:, t, k:k + 1], None, ALU.mult).then_inc(dg_ready, 1)

            @block.vector
            def _(dve):
                link = Chain(dve, chain)
                dve.wait_ge(const_in, 16 * 9)

                def gate(n, t):
                    dve.wait_ge(sig, n + 1)
                    dve.wait_ge(u_in, 32 * (n + 1))
                    for t0, cnt, at in AT:
                        nc.vector.tensor_tensor(u[t][:, at:at + cnt], u[t][:, at:at + cnt], g[n % 2][:, t0:t0 + cnt], ALU.mult).then_inc(gated, 1)
                    dve.wait_ge(gated, 2 * (n + 1))

                def taps(t, spans):
                    for k in range(K):
                        for t0, cnt, at in spans:
                            src, o = u[t][:, at - R + k:at - R + k + cnt], y[t][:, t0:t0 + cnt]
                            if k == 0:
                                x = nc.vector.tensor_scalar(o, src, wt[:, t, 0:1], pr[:, 0, t:t + 1], ALU.mult, ALU.add)
                            else:
                                x = nc.vector.scalar_tensor_tensor(o, src, wt[:, t, k:k + 1], o, ALU.mult, ALU.add)
                        link(x)

                gate(0, 2)
                gate(1, 0)
                gate(2, 3)
                gate(3, 1)
                for t in range(NTL):
                    taps(t, AT[1:] if t in ON_PE else AT)
                dve.sem_inc(conv_done, 1)
                dve.wait_ge(mean_prod, 5)
                for t in range(NTL):
                    for c, (t0, n) in enumerate(CHUNKS):
                        x = nc.vector.tensor_tensor(y[t][:, t0:t0 + n], y[t][:, t0:t0 + n], ps[c][:, 0:n], ALU.subtract)
                    x.then_inc(centred, 1)
                dve.wait_ge(root, 1)
                link(nc.vector.reciprocal(g[0][:], g[0][:]))
                for t in range(NTL):
                    nc.vector.tensor_tensor(y[t][:], y[t][:], g[0][:], ALU.mult).then_inc(normed, 1)

            @block.tensor
            def _(pe):
                pe.wait_ge(const_in, 16 * 9)
                for n, t in enumerate(ON_PE):
                    pe.wait_ge(gated, 2 if t == 2 else 6)
                    for k in range(K):
                        pe.wait_ge(dg_ready, n * K + k + 1)
                        for c in range(4):
                            x = nc.tensor.matmul(ps[4 * n + c][:], dg[:, k, :], u[t][:, c * NT + k:c * NT + k + NT],
                                                 start=(k == 0), stop=(k == K - 1))
                            if k == K - 1:
                                x.then_inc(tap_prod, 1)
                pe.wait_ge(conv_done, 1)
                pe.wait_ge(tap_out, 8)
                for c, (t0, n) in enumerate(CHUNKS):
                    for t in range(NTL):
                        x = nc.tensor.matmul(ps[c][:, 0:n], mo[:], y[t][:, t0:t0 + n], start=(t == 0), stop=(t == NTL - 1))
                    x.then_inc(mean_prod, 1)
                for c, (t0, n) in enumerate(CHUNKS):
                    pe.wait_ge(centred, NTL)
                    for t in range(NTL):
                        pe.wait_ge(squared, t + 1)
                        x = nc.tensor.matmul(ps[c][:, 0:n], mo[:], u[t][:, t0:t0 + n], start=(t == 0), stop=(t == NTL - 1))
                    x.then_inc(var_prod, 1)

            @block.scalar
            def _(act):
                act.wait_ge(const_in, 16 * 9)
                act.wait_ge(pads, NTL + 1)
                for n in range(NTL):
                    act.wait_ge(g_in, 16 * (n + 1))
                    nc.scalar.activation(g[n % 2][:], g[n % 2][:], ACT.Sigmoid).then_inc(sig, 1)
                for n, t in enumerate(ON_PE):
                    for c in range(4):
                        act.wait_ge(tap_prod, 4 * n + c + 1)
                        nc.scalar.activation(y[t][:, c * NT:(c + 1) * NT], ps[4 * n + c][:], ACT.Identity, bias=pr[:, 0, t:t + 1]).then_inc(tap_out, 1)
                for t in range(NTL):
                    act.wait_ge(centred, t + 1)
                    nc.scalar.activation(u[t][:, 0:T], y[t][:], ACT.Square).then_inc(squared, 1)
                for c, (t0, n) in enumerate(CHUNKS):
                    act.wait_ge(var_prod, c + 1)
                    x = nc.scalar.activation(g[0][:, t0:t0 + n], ps[c][:, 0:n], ACT.Sqrt, bias=ep[:, 0:1])
                x.then_inc(root, 1)
                for t in range(NTL):
                    act.wait_ge(normed, t + 1)
                    nc.scalar.activation(y[t][:], y[t][:], ACT.Silu, bias=pr[:, 2, t:t + 1], scale=pr[:, 1, t:t + 1]).then_inc(acted, 1)


def attention(nc, QK, VT, ident, yT, row0):
    NH, NK, QT = 8, T // P, T // P
    NQL = SEQ // P
    SC = HD ** -0.5
    CHUNKS = [(c * NT, NT) for c in range(4)] + [(SEQ, CTX)]
    VG = [range(0, 5), range(5, 10), range(10, 14), range(14, 18)]
    NGRP = len(VG) + NQL * 5 + 2
    assert NGRP % 2 == 0
    with ExitStack() as ctx:
        s = Scope(nc, ctx, "at")
        q, k = [s.sb(f"q{u}", [P, T]) for u in range(2)], [s.sb(f"k{u}", [P, T]) for u in range(2)]
        vt = [s.sb(f"vt{u}", [HD, T]) for u in range(2)]
        v = s.sb("v", [P, NK, HD])
        pr = [s.sb(f"p{u}", [P, T]) for u in range(2)]
        pt = [s.sb(f"pt{u}", [P, NK, P]) for u in range(2)]
        mx = [s.sb(f"mx{u}", [P, 5]) for u in range(2)]
        nb = [s.sb(f"nb{u}", [P, 1]) for u in range(2)]
        sm = [s.sb(f"sm{u}", [P, 5]) for u in range(2)]
        rs = [s.sb(f"rs{u}", [P, 1]) for u in range(2)]
        o = [s.sb(f"o{u}", [P, HD]) for u in range(2)]
        y = [s.sb(f"y{u}", [HD, T]) for u in range(2)]
        idn = s.sb("idn", [P, P])
        sb_ = s.banks(5)
        tb = [ctx.enter_context(nc.psum_tensor(f"at_tb{u}", [P, NT], F32)) for u in range(2)]
        ob = ctx.enter_context(nc.psum_tensor("at_ob", [P, NT], F32))
        const_in, chain = s.sem("const_in"), s.sem("chain")
        in_full, in_used = s.sems("in_full", 2), s.sems("in_used", 2)
        s_full, s_free = s.sems("s_full", 5), s.sems("s_free", 5)
        t_full, t_free = s.sems("t_full", 2), s.sems("t_free", 2)
        nb_ready, sum_ready, pt_ready, v_ready = s.sem("nb_ready"), s.sem("sum_ready"), s.sems("pt_ready", 5), s.sem("v_ready")
        o_full, o_norm, ot_full, ot_out = s.sem("o_full"), s.sem("o_norm"), s.sem("ot_full"), s.sem("ot_out")
        y_out, turn_ = s.sems("y_out", 2), s.sem("turn")

        def chunks(t):
            return [(c, *CHUNKS[c]) for c in (range(5) if t < NQL else (4,))]

        def cnt(h, t, c):
            return h * (NQL if c < 4 else QT) + t

        def grp(h, g):
            return g % 2, h * (NGRP // 2) + g // 2

        def gidx(t, g):
            return len(VG) + (t * 5 + g if t < NQL else NQL * 5 + t - NQL)

        def heads(eng, body):
            with eng.Fori(0, 2) as kv:
                with eng.Fori(0, 2) as j:
                    for u in range(2):
                        body(kv, kv * 4 + j * 2 + u, kv * 2 + j, u)

        BY_DVE = (0, 2)

        with nc.Block() as block:
            @block.sync
            def _(sp):
                sp.dma_start(idn[:], ident).then_inc(const_in, 16)

                def body(kv, h, pair, u):
                    sp.wait_ge(in_used[u], pair)
                    for r in range(2):
                        sp.dma_start(q[u][r * HD:(r + 1) * HD, :], QK[ds(h * HD, HD), :]).then_inc(in_full[u], 16)
                        sp.dma_start(k[u][r * HD:(r + 1) * HD, :], QK[ds(kv * HD + NH * HD, HD), :]).then_inc(in_full[u], 16)
                    sp.dma_start(vt[u][:], VT[ds(kv * HD, HD), :]).then_inc(in_full[u], 16)

                heads(sp, body)

            @block.tensor
            def _(pe):
                pe.wait_ge(const_in, 16)

                def scores(h, u, t):
                    for c, t0, n in chunks(t):
                        r = slice(c % 2 * HD, c % 2 * HD + HD)
                        pe.wait_ge(s_free[c], cnt(h, t, c))
                        nc.tensor.matmul(sb_[c][:, 0:n], q[u][r, t * P:(t + 1) * P], k[u][r, t0:t0 + n], start=True, stop=True
                                         ).then_inc(s_full[c], 1)

                def output(h, u, t):
                    x = t % 2
                    gs = range(5) if t < NQL else (4,)

                    def turn(g):
                        b, n = grp(h, gidx(t, g))
                        pe.wait_ge(t_free[b], n)
                        pe.wait_ge(s_free[g], cnt(h, t, g) + 1)
                        for j in range(4 if g < 4 else 2):
                            tr = nc.tensor.transpose(tb[b][:, j * P:(j + 1) * P], pr[x][:, (4 * g + j) * P:(4 * g + j + 1) * P], idn[:])
                        tr.then_inc(t_full[b], 1)

                    def product(g):
                        pe.wait_ge(pt_ready[g], cnt(h, t, g) + 1)
                        for j in range(4 if g < 4 else 2):
                            kt = 4 * g + j
                            m = nc.tensor.matmul(ob[:, 0:HD], pt[x][:, kt, :], v[:, kt, :], start=(g == gs[0] and j == 0), stop=(kt == NK - 1))
                        return m

                    turn(gs[0])
                    if len(gs) > 1:
                        turn(gs[1])
                    pe.wait_ge(ot_out, h * QT + t)
                    for n, g in enumerate(gs):
                        m = product(g)
                        if n + 2 < len(gs):
                            turn(gs[n + 2])
                    m.then_inc(o_full, 1)

                def last(h, t):
                    pe.wait_ge(o_norm, h * QT + t + 1)
                    pe.sem_inc(turn_, 1)
                    nc.tensor.transpose(ob[0:HD, HD:HD + P], o[t % 2][:], idn[:]).then_inc(ot_full, 1)

                def body(kv, h, pair, u):
                    pe.wait_ge(in_full[u], (pair + 1) * 80)
                    for g, tiles in enumerate(VG):
                        b, n = grp(h, g)
                        pe.wait_ge(t_free[b], n)
                        pe.sem_inc(turn_, 1)
                        for j, kt in enumerate(tiles):
                            tr = nc.tensor.transpose(tb[b][:, j * HD:(j + 1) * HD], vt[u][:, kt * P:(kt + 1) * P], idn[0:HD, 0:HD])
                        tr.then_inc(t_full[b], 1)
                    scores(h, u, 0)
                    pe.wait_ge(v_ready, (h + 1) * len(VG))
                    for t in range(QT):
                        if t + 1 < QT:
                            scores(h, u, t + 1)
                        output(h, u, t)
                        last(h, t)

                heads(pe, body)

            @block.vector
            def _(dve):
                dve.wait_ge(const_in, 16)
                link = Chain(dve, chain)

                def maxima(h, t):
                    x = t % 2
                    for c, _, n in chunks(t):
                        dve.wait_ge(s_full[c], cnt(h, t, c) + 1)
                        m = nc.vector.reduce_max(mx[x][:, c:c + 1], sb_[c][:, 0:n], AX)
                    link(m)
                    src = mx[x][:] if t < NQL else mx[x][:, 4:5]
                    link(nc.vector.reduce_max(rs[x][:], src, AX))
                    nc.vector.tensor_scalar(nb[x][:], rs[x][:], -SC, None, ALU.mult).then_inc(nb_ready, 1)
                    dve.wait_ge(nb_ready, h * QT + t + 1)

                def out(h, t, u):
                    x = t % 2
                    for g in (BY_DVE if t < NQL else ()):
                        b, n = grp(h, gidx(t, g))
                        dve.wait_ge(t_full[b], n + 1)
                        nc.vector.tensor_copy(pt[x][:, 4 * g:4 * g + 4, :].rearrange("p a b -> p (a b)"), tb[b][:]).then_inc(pt_ready[g], 1)
                        dve.wait_ge(pt_ready[g], cnt(h, t, g) + 1)
                        dve.sem_inc(t_free[b], 1)
                    dve.wait_ge(sum_ready, h * QT + t + 1)
                    src = sm[x][:] if t < NQL else sm[x][:, 4:5]
                    link(nc.vector.reduce_sum(rs[x][:], src, AX))
                    link(nc.vector.reciprocal(rs[x][:], rs[x][:]))
                    dve.wait_ge(o_full, h * QT + t + 1)
                    nc.vector.tensor_scalar(o[x][:], ob[:, 0:HD], rs[x][:], None, ALU.mult).then_inc(o_norm, 1)
                    dve.wait_ge(ot_full, h * QT + t + 1)
                    if t == 0:
                        dve.wait_ge(y_out[u], y_before)
                    nc.vector.tensor_copy(y[u][:, t * P:(t + 1) * P], ob[0:HD, HD:HD + P]).then_inc(ot_out, 1)

                def body(kv, h, pair, u):
                    nonlocal y_before
                    y_before = pair * 16
                    link.base, link.n = h * (4 * QT), 0
                    maxima(h, 0)
                    for t in range(QT):
                        if t + 1 < QT:
                            maxima(h, t + 1)
                        out(h, t, u)
                    assert link.n == 4 * QT, link.n
                    dve.sem_inc(in_used[u], 1)

                y_before = 0
                heads(dve, body)

            @block.scalar
            def _(act):
                act.wait_ge(const_in, 16)

                def exps(h, t):
                    x = t % 2
                    act.wait_ge(nb_ready, h * QT + t + 1)
                    if t >= 2:
                        act.wait_ge(o_full, h * QT + t - 1)
                    for c, t0, n in chunks(t):
                        nc.scalar.activation(pr[x][:, t0:t0 + n], sb_[c][:, 0:n], ACT.Exp, bias=nb[x][:], scale=SC,
                                             accum_out=sm[x][:, c:c + 1]).then_inc(s_free[c], 1)
                    for c, _, _ in chunks(t):
                        act.wait_ge(s_free[c], cnt(h, t, c) + 1)
                    act.sem_inc(sum_ready, 1)

                def take(h, t):
                    x = t % 2
                    for g in range(5) if t < NQL else (4,):
                        if g in BY_DVE and t < NQL:
                            continue
                        b, n = grp(h, gidx(t, g))
                        act.wait_ge(t_full[b], n + 1)
                        w = 4 if g < 4 else 2
                        nc.scalar.copy(pt[x][:, 4 * g:4 * g + w, :].rearrange("p a b -> p (a b)"), tb[b][:, 0:w * P]).then_inc(pt_ready[g], 1)
                        act.wait_ge(pt_ready[g], cnt(h, t, g) + 1)
                        act.sem_inc(t_free[b], 1)

                def body(kv, h, pair, u):
                    for g, tiles in enumerate(VG):
                        b, n = grp(h, g)
                        act.wait_ge(t_full[b], n + 1)
                        nc.scalar.copy(v[:, tiles[0]:tiles[-1] + 1, :].rearrange("p a b -> p (a b)"), tb[b][:, 0:len(tiles) * HD]).then_inc(v_ready, 1)
                        act.wait_ge(v_ready, h * len(VG) + g + 1)
                        act.sem_inc(t_free[b], 1)
                    exps(h, 0)
                    for t in range(QT):
                        if t + 1 < QT:
                            exps(h, t + 1)
                        take(h, t)
                    act.wait_ge(ot_out, (h + 1) * QT)
                    act.dma_start(yT[ds(h * HD + row0, HD), :], y[u][:]).then_inc(y_out[u], 16)

                heads(act, body)
                for u in range(2):
                    act.wait_ge(y_out[u], 16 * NH // 2)


def fourier(nc, PT, w, dft_c, dft_l, yT):
    G, Q = 4, 4
    NTK = SEQ // P
    with ExitStack() as ctx:
        s = Scope(nc, ctx, "ft")
        f = [s.sb(f"f{u}", [P, G, P]) for u in range(2)]
        ab = [s.sb(f"ab{t}", [P, 2, G, P]) for t in range(NTK)]
        t1 = s.sb("t1", [P, 2, G, P])
        t2 = s.sb("t2", [P, 2, G, P])
        wg, cc = s.sb("wg", [P, G, P]), s.sb("cc", [P, 2, P])
        cw = s.sb("cw", [P, G, 2, P])
        dl = [s.sb(f"dl{u}", [P, 2, Q, NT]) for u in range(2)]
        y = [s.sb(f"y{g}", [P, SEQ]) for g in range(G)]
        ps = s.banks(8)
        const_in, f_in, cw_prod, cw_ready = (s.sem(n) for n in ("const_in", "f_in", "cw_prod", "cw_ready"))
        fin, f_used = s.sems("fin", 2), s.sem("f_used")
        ab_prod, ab_dve, ab_act, chain, folded = (s.sem(n) for n in ("ab_prod", "ab_dve", "ab_act", "chain", "folded"))
        dl_in, y_prod, y_out, stored = s.sems("dl_in", 2), s.sem("y_prod"), s.sem("y_out"), s.sem("stored")

        with nc.Block() as block:
            @block.sync
            def _(sp):
                sp.dma_start(wg[:], w.rearrange("g c e -> c g e")).then_inc(const_in, 16)
                sp.dma_start(cc[:], dft_c).then_inc(const_in, 16)
                fv = PT[0:G * P, 0:SEQ].rearrange("(g p) t -> p g t", p=P)
                for t in range(NTK):
                    if t >= 2:
                        sp.wait_ge(ab_prod, 2 * (t - 1))
                    sp.dma_start(f[t % 2][:], fv[:, :, t * P:(t + 1) * P]).then_inc(fin[t % 2], 16)
                for r in range(4):
                    if r >= 2:
                        sp.wait_ge(y_prod, G * (r - 1))
                    sp.dma_start(dl[r % 2][:], dft_l[:, r]).then_inc(dl_in[r % 2], 16)
                sp.wait_ge(y_out, 4 * G)
                for g in range(G):
                    sp.dma_start(yT[g * P:(g + 1) * P, 0:SEQ], y[g][:]).then_inc(stored, 16)
                sp.wait_ge(stored, 16 * G)

            @block.tensor
            def _(pe):
                pe.wait_ge(const_in, 32)
                for g in range(G):
                    for j in range(2):
                        x = nc.tensor.matmul(ps[g][:, j * P:(j + 1) * P], cc[:, j, :], wg[:, g, :], start=True, stop=True)
                x.then_inc(cw_prod, 1)
                pe.wait_ge(cw_ready, G)
                for t in range(NTK):
                    pe.wait_ge(fin[t % 2], 16 * (t // 2 + 1))
                    for j in range(2):
                        b = 4 * (t % 2) + j
                        if t >= 2:
                            pe.wait_ge((ab_dve, ab_act)[j], t - 1)
                        for h in range(2):
                            x = nc.tensor.matmul(ps[b][:, h * 2 * P:(h + 1) * 2 * P], f[t % 2][:, 2 * j + h, :],
                                                 cw[:, 2 * j + h, :, :].rearrange("p a e -> p (a e)"), start=True, stop=True)
                        x.then_inc(ab_prod, 1)
                pe.wait_ge(folded, Q)
                pe.wait_ge(ab_dve, NTK)
                pe.wait_ge(ab_act, NTK)
                for r in range(4):
                    pe.wait_ge(dl_in[r % 2], 16 * (r // 2 + 1))
                    for g in range(G):
                        n = r * G + g
                        if n >= 8:
                            pe.wait_ge(y_out, n - 7)
                        for j in range(Q):
                            for c in range(2):
                                x = nc.tensor.matmul(ps[n % 8][:], ab[j + 4 * r][:, c, g, :], dl[r % 2][:, c, j, :],
                                                     start=(j == 0 and c == 0), stop=(j == Q - 1 and c == 1))
                        x.then_inc(y_prod, 1)

            @block.scalar
            def _(act):
                for t in range(NTK):
                    act.wait_ge(ab_prod, 2 * t + 2)
                    nc.scalar.copy(ab[t][:, :, 2:4, :].rearrange("p a g e -> p g a e"),
                                   ps[4 * (t % 2) + 1][:].rearrange("p (g a e) -> p g a e", g=2, a=2)).then_inc(ab_act, 1)
                for n in range(4 * G):
                    r, g = n // G, n % G
                    act.wait_ge(y_prod, n + 1)
                    nc.scalar.mul(y[g][:, r::4], ps[n % 8][:], (SEQ * P) ** -0.5).then_inc(y_out, 1)

            @block.vector
            def _(dve):
                link = Chain(dve, chain)
                dve.wait_ge(cw_prod, 1)
                for g in range(G):
                    nc.vector.tensor_copy(cw[:, g, :, :].rearrange("p a e -> p (a e)"), ps[g][:, 0:2 * P]).then_inc(cw_ready, 1)
                for t in range(NTK):
                    dve.wait_ge(ab_prod, 2 * t + 1)
                    nc.vector.tensor_copy(ab[t][:, :, 0:2, :].rearrange("p a g e -> p g a e"),
                                          ps[4 * (t % 2)][:].rearrange("p (g a e) -> p g a e", g=2, a=2)).then_inc(ab_dve, 1)
                dve.wait_ge(ab_act, NTK)
                dve.wait_ge(ab_dve, NTK)
                tt = nc.vector.tensor_tensor
                for j in range(Q):
                    a0, a1, a2, a3 = (ab[j + 4 * q] for q in range(4))
                    tt(t1[:], a0[:], a2[:], ALU.subtract)
                    link(tt(t2[:], a1[:], a3[:], ALU.subtract))
                    tt(a0[:], a0[:], a2[:], ALU.add)
                    link(tt(a1[:], a1[:], a3[:], ALU.add))
                    tt(a2[:], a0[:], a1[:], ALU.subtract)
                    link(tt(a3[:, 0], t1[:, 0], t2[:, 1], ALU.add))
                    tt(a3[:, 1], t1[:, 1], t2[:, 0], ALU.subtract)
                    link(tt(a0[:], a0[:], a1[:], ALU.add))
                    tt(a1[:, 0], t1[:, 0], t2[:, 1], ALU.subtract)
                    link(tt(a1[:, 1], t1[:, 1], t2[:, 0], ALU.add))
                    dve.sem_inc(folded, 1)


def neighbours(nc, QKV, rpb, one_hot, ident, yT, row0):
    NH, QT, ROW = 8, SEQ // P, 64
    R, NDC, NDD = 8, 31, 16
    MASK = -1e30
    SC = HD ** -0.5
    NV = T // P
    VG = [range(0, 5), range(5, 10), range(10, 14), range(14, 18)]
    NGRP = len(VG) + 2 * QT

    def window(j):
        lo = min(max(2 * j - 4, 0), SEQ // ROW - R)
        inner = 2 <= j < QT - 2
        return lo, R + inner, lo - 2 * j + R - 1, inner

    with ExitStack() as ctx:
        s = Scope(nc, ctx, "na")
        bt = s.sb("bt", [P, NH, NDD, ROW])
        bi = s.sb("bi", [P, NH, R + 1, ROW])
        idn = s.sb("idn", [P, P])
        with ExitStack() as ctx1:
            s1 = Scope(nc, ctx1, "nat")
            oh = s1.sb("oh", [64, ROW, P])
            rp = s1.sb("rp", [64, NH, NDD])
            ps = s1.banks(4)
            const_in, filled, rp_ready, prod, taken = (s1.sem(n) for n in ("const_in", "filled", "rp_ready", "prod", "taken"))
            inner_ready, masked = s1.sem("inner_ready"), s1.sem("masked")
            with nc.Block() as block:
                @block.sync
                def _(sp):
                    sp.dma_start(oh[:], one_hot).then_inc(const_in, 16)
                    sp.dma_start(idn[:], ident).then_inc(const_in, 16)
                    sp.wait_ge(filled, 1)
                    for half in range(2):
                        for h in range(NH):
                            sp.dma_start(rp[32 * half:32 * half + NDC, h, half:half + 15], rpb[h].rearrange("r c -> c r"),
                                         allow_slow_non_contiguous=True).then_inc(const_in, 16)

                @block.vector
                def _(dve):
                    nc.vector.memset(rp[:], MASK).then_inc(filled, 1)
                    dve.wait_ge(const_in, 16 * 18)
                    nc.vector.tensor_scalar(rp[:], rp[:], 1.0 / SC, None, ALU.mult).then_inc(rp_ready, 1)
                    for n in range(ROW // 4):
                        dve.wait_ge(prod, n + 1)
                        nc.vector.tensor_copy(bt[:].rearrange("p h d w -> p (h d) w")[:, :, 4 * n:4 * n + 4],
                                              ps[n % 4][:].rearrange("p (w x) -> p x w", w=4)).then_inc(taken, 1)
                    dve.wait_ge(taken, ROW // 4)
                    nc.vector.tensor_copy(bi[:], bt[:, :, 3:3 + R + 1, :]).then_inc(inner_ready, 1)
                    dve.wait_ge(inner_ready, 1)
                    nc.vector.memset(bi[0:64, :, R, :], MASK / SC).then_inc(masked, 1)
                    nc.vector.memset(bi[64:128, :, 0, :], MASK / SC).then_inc(masked, 1)

                @block.tensor
                def _(pe):
                    pe.wait_ge(rp_ready, 1)
                    for n in range(ROW // 4):
                        if n >= 4:
                            pe.wait_ge(taken, n - 3)
                        for i in range(4):
                            x = nc.tensor.matmul(ps[n % 4][:, i * P:(i + 1) * P], oh[:, 4 * n + i, :], rp[:].rearrange("p h d -> p (h d)"),
                                                 start=True, stop=True)
                        x.then_inc(prod, 1)

        q, k = [s.sb(f"q{u}", [P, SEQ]) for u in range(2)], [s.sb(f"k{u}", [P, T]) for u in range(2)]
        vt = [s.sb(f"vt{u}", [HD, T]) for u in range(2)]
        v = s.sb("v", [P, NV, HD])
        NKEY = (R + 1) * ROW
        sw = [s.sb(f"sw{u}", [P, NKEY]) for u in range(2)]
        pr = [s.sb(f"p{u}", [P, NKEY + CTX]) for u in range(2)]
        pt = [s.sb(f"pt{u}", [P, 7, P]) for u in range(2)]
        mx = [s.sb(f"mx{u}", [P, 2]) for u in range(2)]
        nb = [s.sb(f"nb{u}", [P, 1]) for u in range(2)]
        sm = [s.sb(f"sm{u}", [P, 2]) for u in range(2)]
        rs = [s.sb(f"rs{u}", [P, 1]) for u in range(2)]
        o = [s.sb(f"o{u}", [P, HD]) for u in range(2)]
        y = [s.sb(f"y{u}", [HD, SEQ]) for u in range(2)]
        win = s.banks(4)
        tb = [ctx.enter_context(nc.psum_tensor(f"na_tb{u}", [P, NT], F32)) for u in range(2)]
        ob = ctx.enter_context(nc.psum_tensor("na_ob", [P, NT], F32))
        chain = s.sem("chain")
        in_full, in_used = s.sems("in_full", 2), s.sems("in_used", 2)
        s_full, s_free = s.sems("s_full", 2), s.sems("s_free", 2)
        t_full, t_free = s.sems("t_full", 2), s.sems("t_free", 2)
        nb_ready, p_ready, pt_ready, v_ready = s.sem("nb_ready"), s.sem("p_ready"), s.sems("pt_ready", 2), s.sem("v_ready")
        o_full, o_norm, ot_full, ot_out = s.sem("o_full"), s.sem("o_norm"), s.sem("ot_full"), s.sem("ot_out")
        y_out, turn_ = s.sems("y_out", 2), s.sem("turn")

        def tiles(j):
            lo, rows, _, _ = window(j)
            n = rows * ROW
            a = [(i * P, min(P, n - i * P), lo * ROW // P + i) for i in range(-(-n // P))]
            return a + [(n + i * P, P, SEQ // P + i) for i in range(2)]

        def heads(eng, body):
            with eng.Fori(0, NH // 2) as i:
                for u in range(2):
                    body(i * 2 + u, i, u)

        def grp(h, g):
            return g % 2, h * (NGRP // 2) + g // 2

        with nc.Block() as block:
            @block.sync
            def _(sp):
                def body(h, pair, u):
                    sp.wait_ge(in_used[u], pair)
                    for r in range(2):
                        sp.dma_start(q[u][r * HD:(r + 1) * HD, :], QKV[ds(h * HD, HD), 0:SEQ]).then_inc(in_full[u], 16)
                        sp.dma_start(k[u][r * HD:(r + 1) * HD, :], QKV[ds(h * HD + NH * HD, HD), :]).then_inc(in_full[u], 16)
                    sp.dma_start(vt[u][:], QKV[ds(h * HD + 2 * NH * HD, HD), :]).then_inc(in_full[u], 16)

                heads(sp, body)

            @block.tensor
            def _(pe):
                def scores(h, u, j):
                    x = j % 2
                    lo, rows, _, _ = window(j)
                    n, a = rows * ROW, lo * ROW
                    pe.wait_ge(s_free[x], h * (QT // 2) + j // 2)
                    qs = slice(j * P, (j + 1) * P)
                    nc.tensor.matmul(win[2 * x][:], q[u][0:HD, qs], k[u][0:HD, a:a + NT], start=True, stop=True)
                    if n > NT:
                        nc.tensor.matmul(win[2 * x + 1][:, CTX:CTX + ROW], q[u][HD:P, qs], k[u][HD:P, a + NT:a + n], start=True, stop=True)
                    nc.tensor.matmul(win[2 * x + 1][:, 0:CTX], q[u][HD:P, qs], k[u][HD:P, SEQ:T], start=True, stop=True
                                     ).then_inc(s_full[x], 1)

                def output(h, j):
                    x = j % 2
                    tl = tiles(j)
                    pe.wait_ge(p_ready, h * QT + j + 1)
                    for g in range(2):
                        b, n = grp(h, len(VG) + 2 * j + g)
                        pe.wait_ge(t_free[b], n)
                        pe.sem_inc(turn_, 1)
                        for i, (c, w, _) in enumerate(tl[4 * g:4 * g + 4]):
                            tr = nc.tensor.transpose(tb[b][0:w, i * P:(i + 1) * P], pr[x][:, c:c + w], idn[:])
                        tr.then_inc(t_full[b], 1)
                    pe.wait_ge(ot_out, h * QT + j)
                    for n, (c, w, vt_) in enumerate(tl):
                        if n % 4 == 0:
                            pe.wait_ge(pt_ready[n // 4], h * QT + j + 1)
                        m = nc.tensor.matmul(ob[:, 0:HD], pt[x][0:w, n, :], v[0:w, vt_, :], start=(n == 0), stop=(n == len(tl) - 1))
                    m.then_inc(o_full, 1)

                def last(h, j):
                    pe.wait_ge(o_norm, h * QT + j + 1)
                    pe.sem_inc(turn_, 1)
                    nc.tensor.transpose(ob[0:HD, HD:HD + P], o[j % 2][:], idn[:]).then_inc(ot_full, 1)

                def body(h, pair, u):
                    pe.wait_ge(in_full[u], (pair + 1) * 80)
                    for g, tl in enumerate(VG):
                        b, n = grp(h, g)
                        pe.wait_ge(t_free[b], n)
                        pe.sem_inc(turn_, 1)
                        for i, kt in enumerate(tl):
                            tr = nc.tensor.transpose(tb[b][:, i * HD:(i + 1) * HD], vt[u][:, kt * P:(kt + 1) * P], idn[0:HD, 0:HD])
                        tr.then_inc(t_full[b], 1)
                    scores(h, u, 0)
                    pe.wait_ge(v_ready, (h + 1) * len(VG))
                    for j in range(QT):
                        if j + 1 < QT:
                            scores(h, u, j + 1)
                        output(h, j)
                        last(h, j)

                heads(pe, body)

            @block.vector
            def _(dve):
                link = Chain(dve, chain)

                def weights(h, j):
                    x = j % 2
                    lo, rows, d0, inner = window(j)
                    n = rows * ROW
                    dve.wait_ge(s_full[x], h * (QT // 2) + j // 2 + 1)
                    table = bi[:, ds(h, 1), :, :] if inner else bt[:, ds(h, 1), d0:d0 + R, :]
                    table = table.rearrange("p o d w -> p (o d) w")
                    last = nc.vector.tensor_tensor(sw[x][:, 0:NT].rearrange("p (d w) -> p d w", w=ROW),
                                                   win[2 * x][:].rearrange("p (d w) -> p d w", w=ROW), table[:, 0:R, :], ALU.add)
                    if inner:
                        last = nc.vector.tensor_tensor(sw[x][:, NT:n].rearrange("p (d w) -> p d w", w=ROW),
                                                       win[2 * x + 1][:, CTX:CTX + ROW].rearrange("p (d w) -> p d w", w=ROW), table[:, R:R + 1, :], ALU.add)
                    link(last)
                    nc.vector.reduce_max(mx[x][:, 0:1], sw[x][:, 0:n], AX)
                    link(nc.vector.reduce_max(mx[x][:, 1:2], win[2 * x + 1][:, 0:CTX], AX))
                    link(nc.vector.reduce_max(rs[x][:], mx[x][:], AX))
                    nc.vector.tensor_scalar(nb[x][:], rs[x][:], -SC, None, ALU.mult).then_inc(nb_ready, 1)
                    dve.wait_ge(nb_ready, h * QT + j + 1)

                def out(h, j, u):
                    x = j % 2
                    b, n = grp(h, len(VG) + 2 * j)
                    dve.wait_ge(t_full[b], n + 1)
                    nc.vector.tensor_copy(pt[x][:, 0:4, :].rearrange("p a b -> p (a b)"), tb[b][:]).then_inc(pt_ready[0], 1)
                    dve.wait_ge(pt_ready[0], h * QT + j + 1)
                    dve.sem_inc(t_free[b], 1)
                    nc.vector.tensor_tensor(rs[x][:], sm[x][:, 0:1], sm[x][:, 1:2], ALU.add).then_inc(chain, 1)
                    link.n += 1
                    dve.wait_ge(chain, link.base + link.n)
                    link(nc.vector.reciprocal(rs[x][:], rs[x][:]))
                    dve.wait_ge(o_full, h * QT + j + 1)
                    nc.vector.tensor_scalar(o[x][:], ob[:, 0:HD], rs[x][:], None, ALU.mult).then_inc(o_norm, 1)
                    dve.wait_ge(ot_full, h * QT + j + 1)
                    if j == 0:
                        dve.wait_ge(y_out[u], y_before)
                    nc.vector.tensor_copy(y[u][:, j * P:(j + 1) * P], ob[0:HD, HD:HD + P]).then_inc(ot_out, 1)

                y_before = 0

                def body(h, pair, u):
                    nonlocal y_before
                    y_before = pair * 16
                    link.base, link.n = h * (5 * QT), 0
                    weights(h, 0)
                    for j in range(QT):
                        if j + 1 < QT:
                            weights(h, j + 1)
                        out(h, j, u)
                    assert link.n == 5 * QT, link.n
                    dve.sem_inc(in_used[u], 1)

                heads(dve, body)

            @block.scalar
            def _(act):
                def exps(h, j):
                    x = j % 2
                    lo, rows, _, _ = window(j)
                    n = rows * ROW
                    act.wait_ge(nb_ready, h * QT + j + 1)
                    if j >= 2:
                        act.wait_ge(o_norm, h * QT + j - 1)
                    nc.scalar.activation(pr[x][:, n:n + CTX], win[2 * x + 1][:, 0:CTX], ACT.Exp, bias=nb[x][:], scale=SC,
                                         accum_out=sm[x][:, 1:2]).then_inc(s_free[x], 1)
                    nc.scalar.activation(pr[x][:, 0:n], sw[x][:, 0:n], ACT.Exp, bias=nb[x][:], scale=SC,
                                         accum_out=sm[x][:, 0:1]).then_inc(p_ready, 1)

                def take(h, j):
                    x = j % 2
                    tl = tiles(j)
                    b, n = grp(h, len(VG) + 2 * j + 1)
                    act.wait_ge(t_full[b], n + 1)
                    if tl[4][1] < P:
                        nc.scalar.copy(pt[x][0:HD, 4, :], tb[b][0:HD, 0:P])
                        c = nc.scalar.copy(pt[x][:, 5:7, :].rearrange("p a b -> p (a b)"), tb[b][:, P:3 * P])
                    else:
                        c = nc.scalar.copy(pt[x][:, 4:6, :].rearrange("p a b -> p (a b)"), tb[b][:, 0:2 * P])
                    c.then_inc(pt_ready[1], 1)
                    act.wait_ge(pt_ready[1], h * QT + j + 1)
                    act.sem_inc(t_free[b], 1)

                def body(h, pair, u):
                    for g, tl in enumerate(VG):
                        b, n = grp(h, g)
                        act.wait_ge(t_full[b], n + 1)
                        nc.scalar.copy(v[:, tl[0]:tl[-1] + 1, :].rearrange("p a b -> p (a b)"), tb[b][:, 0:len(tl) * HD]).then_inc(v_ready, 1)
                        act.wait_ge(v_ready, h * len(VG) + g + 1)
                        act.sem_inc(t_free[b], 1)
                    exps(h, 0)
                    for j in range(QT):
                        if j + 1 < QT:
                            exps(h, j + 1)
                        take(h, j)
                    act.wait_ge(ot_out, (h + 1) * QT)
                    act.dma_start(yT[ds(h * HD + row0, HD), 0:SEQ], y[u][:]).then_inc(y_out[u], 16)

                heads(act, body)
                for u in range(2):
                    act.wait_ge(y_out[u], 16 * NH // 2)


def program(nc, a, out):
    def scratch(name, shape):
        return nc.dram_tensor(name, list(shape), F32).ap()

    mods = [scratch(f"mod{i}", (2, 3 * D)) for i in range(3)]
    pT1, pT2, pT3 = scratch("pT1", (33 * P, T)), scratch("pT2", (22 * P, T)), scratch("pT3", (24 * P, T))
    y1, y2, y3 = (scratch(f"y{i}", (D, T)) for i in range(3))
    R, E = scratch("rwkv_chunks", (CH, MT_R, 2, P, 5, P)), scratch("rwkv_ends", (P, 6, CH))
    bonus, YR, YH = scratch("bonus", (D_R, SEQ)), scratch("y_rwkv", (2, D_R, SEQ)), scratch("y_hgrn", (2, D_R, SEQ))
    x1, x2, c2, qk = scratch("x1", (SEQ, D)), scratch("x2", (SEQ, D)), scratch("c2", (CTX, D)), scratch("qk", (5 * P, T))

    modulation(nc, [(a["c"], a["c_ctx"], a["mod_w"][0], a["mod_b"][0], mods[0]),
                    (a["c_2"], a["c_ctx_2"], a["ab_w_ada_2"][0], a["ab_b_ada_2"][0], mods[1]),
                    (a["c_2"], a["c_ctx_2"], a["cd_w_ada_2"][0], a["cd_b_ada_2"][0], mods[2])])

    norm_project(nc, "p1", a["x"][0], a["ctx"][0], mods[0], None, a["w_in"][0], pT1,
                 [(0, 2, False), (2, 11, True), (13, 3, False), (16, 9, True), (25, 8, False)], a["ident"], 1e-5)
    pool_branch(nc, pT1, a["pool_w"][0], a["pool_scale"][0], a["inv_count"], y1)
    rwkv_inputs(nc, pT1, 2 * P, *[a[n][0] for n in ("rwkv_shift", "rwkv_w0", "rwkv_w_up", "rwkv_a0", "rwkv_a_up", "rwkv_k_k",
                                                    "rwkv_k_a", "rwkv_r_k")], a["head_ones"], a["seg"], R, E, bonus)
    rwkv_scan(nc, R, E, a["masks"], a["levels"], a["ident"], YR)
    hgrn(nc, pT1, 13 * P, 16 * P, 19 * P, a["seg"], a["hgrn_masks"], a["ident"], YH)
    items = []
    for m in range(MT_R):
        r = slice(m * P, (m + 1) * P)
        items.append(dict(w=SEQ, a=YR[0, r, :], b=YR[1, r, :], center=1, eps=64e-5, gain=a["rwkv_gn_g"][0, r],
                          bias=a["rwkv_gn_b"][0, r], plus=bonus[r, :], rotate=0, out=y1[(2 + m) * P:(3 + m) * P, 0:SEQ]))
        items.append(dict(w=SEQ, a=YH[0, r, :], b=YH[1, r, :], center=0, eps=1e-6, gain=a["hgrn_norm_g"][0, r],
                          bias=None, plus=None, rotate=0, out=y1[(5 + m) * P:(6 + m) * P, 0:SEQ]))
    head_norm(nc, "hn", items, a["head_mean"])
    out_project(nc, "o1", y1, pT1[25 * P:33 * P, :], a["w_out"][0], a["x"][0], mods[0][0, 2 * D:3 * D], "ln", a["ln_g"][0],
                a["ln_b"][0], x1, SEQ // P, 0)

    norm_project(nc, "p2", x1, a["ctx_2"][0], mods[1], a["ab_norm_g_2"][0], a["ab_w_in_2"][0], pT2, [(0, 22, True)], a["ident"], 1e-6)
    conformer(nc, pT2, a["ab_conv_w_2"][0], a["ab_conv_b_2"][0], a["ab_ln_g_2"][0], a["ab_ln_b_2"][0], a["ident"], a["mean_512"], y2)
    items = []
    for cols, rotate in ((slice(0, SEQ), 1), (slice(SEQ, T), 0)):
        for t in range(5):
            items.append(dict(w=cols.stop - cols.start, a=pT2[(8 + t) * P:(9 + t) * P, cols], b=None, center=0, eps=1e-6,
                              gain=a["ab_q_norm_g_2" if t < 4 else "ab_k_norm_g_2"][0], bias=None, plus=None, rotate=rotate,
                              out=qk[t * P:(t + 1) * P, cols]))
    head_norm(nc, "qk", items, a["head_mean"], (a["rope_cos"], a["rope_sin"], a["rope_swap"]))
    attention(nc, qk, pT2[13 * P:14 * P, :], a["ident"], y2, 512)
    gates = mods[1]
    out_project(nc, "o2", y2, pT2[14 * P:22 * P, :], a["ab_w_out_2"][0], x1, gates[0, 2 * D:3 * D], "plain", None, None, x2, SEQ // P, 0)
    out_project(nc, "o3", y2, pT2[14 * P:22 * P, :], a["ab_w_out_2"][0], a["ctx_2"][0], gates[1, 2 * D:3 * D], "plain", None, None,
                c2, CTX // P, SEQ)

    norm_project(nc, "p3", x2, c2, mods[2], a["cd_norm_g_2"][0], a["cd_w_in_2"][0], pT3,
                 [(0, 8, False), (8, 8, True), (16, 8, False)], a["ident"], 1e-6)
    fourier(nc, pT3, a["cd_w_fourier_2"][0], a["dft_c"], a["dft_l"], y3)
    neighbours(nc, pT3[4 * P:16 * P, :], a["cd_rpb_2"][0], a["one_hot"], a["ident"], y3, 512)
    out_project(nc, "o4", y3, pT3[16 * P:24 * P, :], a["cd_w_out_2"][0], x2, mods[2][0, 2 * D:3 * D], "rms", a["final_norm_g_2"], None,
                out[0], SEQ // P, 0)


def constants():
    f = np.float32
    c = {"ident": np.eye(P, dtype=f), "mean_512": np.full((P, P), 1 / 512, f)}
    ones = np.kron(np.eye(2), np.ones((HD, HD))).astype(f)
    c["head_ones"], c["head_mean"] = ones, ones / HD
    t = np.arange(HD)
    c["inv_count"] = np.zeros((P, 2, HD), f)
    for g, win in enumerate((2, 4, 8, 16)):
        left = win // 2
        n = np.minimum(t + win - 1 - left, HD - 1) + 1 - np.maximum(t - left, 0)
        c["inv_count"][g % 2 * HD:(g % 2 + 1) * HD, g // 2] = 1.0 / n
    m = np.ones((2, T), f)
    m[0, 0::P], m[1, P - 1::P] = 0, 0
    c["seg"] = np.broadcast_to(m, (P, 2, T)).copy()
    s, t = np.arange(P)[:, None], np.arange(P)[None]
    c["masks"] = np.zeros((P, 2, 4 * P), f)
    lv = np.zeros((P, 2, 7, P), f)
    for d in range(2):
        strict, incl = (s < t, s <= t) if d == 0 else (s > t, s >= t)
        c["masks"][:, d] = np.concatenate([strict, incl, strict, incl], 1)
        for j in range(7):
            b = 2 ** j
            late_t, late_s = t % (2 * b) >= b, s % (2 * b) >= b
            lv[:, d, j] = (s // (2 * b) == t // (2 * b)) & ((late_t & ~late_s) if d == 0 else (~late_t & late_s))
    c["hgrn_masks"] = np.concatenate([lv, np.broadcast_to(np.eye(P, dtype=f)[:, None, None], (P, 2, 1, P))], 2)
    c["levels"] = lv.copy()
    c["levels"][:, :, 0] *= -1
    tok = np.arange(SEQ)
    inv = f(10000.0) ** (-np.arange(16, dtype=f) / f(16))
    ang = np.concatenate([(tok // 64).astype(f)[:, None] * inv, (tok % 64).astype(f)[:, None] * inv], -1).astype(f)
    c["rope_cos"], c["rope_sin"] = (np.tile(np.repeat(fn(ang).T, 2, axis=0), (2, 1)).astype(f) for fn in (np.cos, np.sin))
    c["rope_swap"] = np.zeros((P, P), f)
    for i in range(0, P, 2):
        c["rope_swap"][i + 1, i], c["rope_swap"][i, i + 1] = -1.0, 1.0
    n = np.arange(P)
    a = 2 * np.pi * (np.outer(n, n) % P) / P
    c["dft_c"] = np.stack([np.cos(a), np.sin(a)], 1).astype(f)
    m = np.arange(512)[:, None]
    c["dft_l"] = np.zeros((P, 4, 2, 4, 512), f)
    for r in range(4):
        a = 2 * np.pi * ((m * (4 * np.arange(512)[None] + r)) % SEQ) / SEQ
        for j, v in enumerate((np.cos(a), -np.sin(a))):
            c["dft_l"][:, r, j] = v.reshape(4, P, 512).transpose(1, 0, 2)
    c["one_hot"] = np.zeros((64, 64, P), f)
    for wq in range(64):
        cs = min(max(wq - 8, 0), 48)
        for wk in range(64):
            for r in range(2):
                c["one_hot"][32 * r + (wk - wq + 15 if cs <= wk < cs + 16 else 31), wk, 64 * r + wq] = 1
    return c


_INS = ["x", "c", "ctx", "c_ctx", "mod_w", "mod_b", "w_in", "rwkv_shift", "pool_w", "pool_scale", "rwkv_w0", "rwkv_w_up",
        "rwkv_a0", "rwkv_a_up", "rwkv_k_k", "rwkv_k_a", "rwkv_r_k", "rwkv_gn_g", "rwkv_gn_b", "hgrn_norm_g", "w_out", "ln_g",
        "ln_b", "c_2", "ctx_2", "c_ctx_2", "ab_w_ada_2", "ab_b_ada_2", "ab_norm_g_2", "ab_w_in_2", "ab_conv_w_2",
        "ab_conv_b_2", "ab_ln_g_2", "ab_ln_b_2", "ab_q_norm_g_2", "ab_k_norm_g_2", "ab_w_out_2", "cd_w_ada_2", "cd_b_ada_2",
        "cd_norm_g_2", "cd_w_in_2", "cd_w_fourier_2", "cd_rpb_2", "cd_w_out_2", "final_norm_g_2"]


def kernel(**inputs):
    import numpy as _np
    import concourse.bacc as _bacc
    from concourse import mybir as _mybir
    from concourse.bass_utils import run_bass_kernel_spmd as _run

    nc = _bacc.Bacc("TRN2", target_bir_lowering=False, num_devices=1)
    arrays, aps = {}, {}
    for name, value in [(n, inputs[n]) for n in _INS] + list(constants().items()):
        a = _np.ascontiguousarray(value)
        arrays[f"in_{name}_dram"] = a
        aps[name] = nc.dram_tensor(f"in_{name}_dram", a.shape, _mybir.dt.from_np(a.dtype), kind="ExternalInput").ap()
    out = nc.dram_tensor("out_0_dram", (1, SEQ, D), F32, kind="ExternalOutput").ap()
    program(nc, aps, out)
    r = _run(nc, [arrays], core_ids=[0])
    return r.results[0]["out_0_dram"]
```

```python
from contextlib import ExitStack

import numpy as np

import concourse.bass as bass
from concourse import mybir
from concourse.alu_op_type import AluOpType as ALU

F32 = mybir.dt.float32
F32R = mybir.dt.float32r
ACT = mybir.ActivationFunctionType
AX = mybir.AxisListType.X
ds = bass.ds

P = 128
D = 1024
KT = D // P
SEQ = 2048
CTX = 256
T = SEQ + CTX
NT = 512
HD = 64
ALPHA = 2.0 ** 0.25


class Scope:

    def __init__(self, nc, ctx, name):
        self.nc, self.ctx, self.name, self.all_sems = nc, ctx, name, []
        ctx.callback(self.close)

    def close(self):
        self.nc.clear_and_free_semaphores(self.all_sems)
        self.nc.all_engine_barrier()

    def sb(self, name, shape, dt=F32):
        return self.ctx.enter_context(self.nc.sbuf_tensor(f"{self.name}_{name}", list(shape), dt))

    def banks(self, n):
        return [self.ctx.enter_context(self.nc.psum_tensor(f"{self.name}_bank{i}", [P, NT], F32)) for i in range(n)]

    def sem(self, name):
        self.all_sems.append(self.nc.alloc_semaphore(f"{self.name}_{name}"))
        return self.all_sems[-1]

    def sems(self, name, n):
        return [self.sem(f"{name}{i}") for i in range(n)]


class Chain:

    def __init__(self, eng, sem):
        self.eng, self.sem, self.done, self.base, self.n = eng, sem, 0, 0, 0

    def body(self, i, per):
        self.per, self.base, self.n = per, self.done + i * per, 0

    def end(self, count):
        assert self.n == self.per, (self.n, self.per)
        self.done += count * self.per
        self.base, self.n = self.done, 0

    def __call__(self, ins):
        ins.then_inc(self.sem, 1)
        self.n += 1
        self.eng.wait_ge(self.sem, self.base + self.n)


def modulation(nc, layers):
    NL = len(layers)
    NC = 3 * D // NT
    with ExitStack() as ctx:
        s = Scope(nc, ctx, "mod")
        cond = s.sb("cond", [P, NL, 2, KT])
        act = s.sb("act", [P, NL, KT, 2])
        w = [s.sb(f"w{u}", [P, KT, NT]) for u in range(2)]
        b = [s.sb(f"b{u}", [2, NT]) for u in range(2)]
        o = [s.sb(f"o{u}", [2, NT]) for u in range(2)]
        ps = s.banks(2)
        cond_in, act_ready = s.sem("cond_in"), s.sem("act_ready")
        w_full, w_free = s.sems("w_full", 2), s.sems("w_free", 2)
        o_full, o_out = s.sems("o_full", 2), s.sems("o_out", 2)

        with nc.Block() as block:
            @block.sync
            def _(sp):
                for l, (c, c_ctx, _, _, _) in enumerate(layers):
                    sp.dma_start(cond[:, l, 0, :], c[0].rearrange("(p k) -> p k", k=KT)).then_inc(cond_in, 16)
                    sp.dma_start(cond[:, l, 1, :], c_ctx.rearrange("(p k) -> p k", k=KT)).then_inc(cond_in, 16)
                for l, (_, _, wd, bd, _) in enumerate(layers):
                    wv = wd.rearrange("(p k) n -> p k n", k=KT)
                    with sp.Fori(0, NC // 2) as i:
                        for u in range(2):
                            sp.wait_ge(w_free[u], i + l * (NC // 2))
                            cols = ds((i * 2 + u) * NT, NT)
                            sp.dma_start(w[u][:], wv[:, :, cols]).then_inc(w_full[u], 16)
                            sp.wait_ge(o_full[u], i + l * (NC // 2))
                            sp.dma_start(b[u][:], bd[cols].partition_broadcast(2)).then_inc(w_full[u], 16)

            @block.scalar
            def _(act_e):
                act_e.wait_ge(cond_in, 32 * NL)
                nc.scalar.activation(act[:].rearrange("p l k r -> p l r k"), cond[:], ACT.Silu).then_inc(act_ready, 1)
                for l, (_, _, _, _, mod) in enumerate(layers):
                    with act_e.Fori(0, NC // 2) as i:
                        for u in range(2):
                            act_e.wait_ge(o_full[u], i + 1 + l * (NC // 2))
                            act_e.dma_start(mod[:, ds((i * 2 + u) * NT, NT)], o[u][:]).then_inc(o_out[u], 16)
                for u in range(2):
                    act_e.wait_ge(o_out[u], 16 * NL * (NC // 2))

            @block.tensor
            def _(pe):
                pe.wait_ge(act_ready, 1)
                for l in range(NL):
                    with pe.Fori(0, NC // 2) as i:
                        for u in range(2):
                            pe.wait_ge(w_full[u], (i + 1 + l * (NC // 2)) * 32)
                            pe.wait_ge(o_full[u], i + l * (NC // 2))
                            for k in range(KT):
                                mm = nc.tensor.matmul(ps[u][0:2, :], act[:, l, k, :], w[u][:, k, :],
                                                      start=(k == 0), stop=(k == KT - 1))
                            mm.then_inc(w_free[u], 1)

            @block.vector
            def _(dve):
                for l in range(NL):
                    with dve.Fori(0, NC // 2) as i:
                        for u in range(2):
                            dve.wait_ge(w_free[u], i + 1 + l * (NC // 2))
                            dve.wait_ge(o_out[u], (i + l * (NC // 2)) * 16)
                            nc.vector.tensor_tensor(o[u][:], ps[u][0:2, :], b[u][:], ALU.add).then_inc(o_full[u], 1)


def split_high(eng, high, x):
    return eng.tensor_copy(high, x)


def split_low(eng, low, x, high):
    return eng.tensor_tensor(low, x, high.bitcast(F32), ALU.subtract)


def split_product(nc, out, lhs, rhs, start, stop):
    nc.tensor.matmul(out, lhs[0], rhs[0], start=start, stop=False)
    nc.tensor.matmul(out, lhs[0], rhs[1], start=False, stop=False)
    return nc.tensor.matmul(out, lhs[1], rhs[0], start=False, stop=stop)


def norm_project(nc, name, x_lat, x_ctx, mod, gain, w, out, groups, ident, eps):
    NLAT, NCTX = SEQ // P, CTX // P
    SPANS = [(x_lat, 0, 0, NLAT // 2, 0), (x_ctx, 1, SEQ, NCTX // 2, NLAT // 2)]
    CHUNKS = [(c * NT, NT) for c in range(SEQ // NT)] + [(SEQ, CTX)]
    with ExitStack() as ctx:
        s = Scope(nc, ctx, name)
        hT = [s.sb(f"hT_{part}", [P, KT, T], F32R) for part in ("high", "low")]
        with ExitStack() as ctx1:
            s1 = Scope(nc, ctx1, name + "n")
            idn = s1.sb("idn", [P, P])
            mv = s1.sb("mv", [P, 2, 2, KT])
            gn = s1.sb("gn", [P, KT])
            fac = s1.sb("fac", [P, 2, KT])
            x = [s1.sb(f"x{u}", [P, D]) for u in range(2)]
            xn = [s1.sb(f"xn{u}", [P, D]) for u in range(2)]
            st = [s1.sb(f"st{u}", [P, 2, 6]) for u in range(2)]
            ag = [s1.sb(f"ag{u}", [P, 2]) for u in range(2)]
            va = [s1.sb(f"va{u}", [P, 1]) for u in range(2)]
            sd = [s1.sb(f"sd{u}", [P, 1]) for u in range(2)]
            hf = [s1.sb(f"h{u}", [P, KT, P]) for u in range(2)]
            ps = s1.banks(4)
            split, high_ready, pool_turn = s1.sems("split", 2), s1.sems("high_ready", 2), s1.sem("pool_turn")
            aggr_turn = s1.sem("aggr_turn")
            const_in, fac_ready, chain = s1.sem("const_in"), s1.sem("fac_ready"), s1.sem("chain")
            x_full, xn_full = s1.sems("x_full", 2), s1.sems("xn_full", 2)
            var_ready, sd_ready = s1.sems("var_ready", 2), s1.sems("sd_ready", 2)
            tr_full, lo_free, hi_free = s1.sems("tr_full", 4), s1.sems("lo_free", 2), s1.sems("hi_free", 2)
            NCONST = 5 if gain is None else 6

            with nc.Block() as block:
                @block.sync
                def _(sp):
                    sp.dma_start(idn[:], ident).then_inc(const_in, 16)
                    for r in range(2):
                        for a in range(2):
                            sp.dma_start(mv[:, r, a, :], mod[r, a * D:(a + 1) * D].rearrange("(k p) -> p k", p=P),
                                         allow_slow_non_contiguous=True).then_inc(const_in, 16)
                    if gain is not None:
                        sp.dma_start(gn[:], gain.rearrange("(k p) -> p k", p=P), allow_slow_non_contiguous=True).then_inc(const_in, 16)
                    for src, _, _, rounds, before in SPANS:
                        with sp.Fori(0, rounds) as i:
                            for u in range(2):
                                sp.wait_ge(xn_full[u], i + before)
                                sp.dma_start(x[u][:], src[ds((i * 2 + u) * P, P), :]).then_inc(x_full[u], 16)

                @block.tensor
                def _(pe):
                    pe.wait_ge(const_in, 16 * NCONST)
                    for _, _, _, rounds, before in SPANS:
                        with pe.Fori(0, rounds) as i:
                            for u in range(2):
                                pe.wait_ge(xn_full[u], i + before + 1)
                                pe.wait_ge(lo_free[u], i + before)
                                pe.wait_ge(hi_free[u], i + before)
                                for k in range(KT):
                                    b = 2 * u + k // 4
                                    tr = nc.tensor.transpose(ps[b][:, (k % 4) * P:(k % 4 + 1) * P],
                                                             xn[u][:, k * P:(k + 1) * P], idn[:])
                                    if k % 4 == 3:
                                        tr.then_inc(tr_full[b], 1)

                @block.scalar
                def _(act):
                    act.wait_ge(const_in, 16 * NCONST)
                    act.wait_ge(fac_ready, 1)
                    for _, r, t0, rounds, before in SPANS:
                        with act.Fori(0, rounds) as i:
                            for u in range(2):
                                act.wait_ge(var_ready[u], i + before + 1)
                                nc.scalar.activation(sd[u][:], va[u][:], ACT.Sqrt).then_inc(sd_ready[u], 1)
                                act.wait_ge(tr_full[2 * u + 1], i + before + 1)
                                act.wait_ge(split[u], i + before)
                                for j in range(4):
                                    k = 4 + j
                                    e = nc.scalar.activation(hf[u][:, k, :],
                                                             ps[2 * u + 1][:, j * P:(j + 1) * P], ACT.Identity,
                                                             bias=mv[:, r, 0, k:k + 1], scale=fac[:, r, k:k + 1])
                                e.then_inc(hi_free[u], 1)

                @block.gpsimd
                def _(pool):
                    for _, _, t0, rounds, before in SPANS:
                        with pool.Fori(0, rounds) as i:
                            for u in range(2):
                                to = ds((i * 2 + u) * P + t0, P)
                                pool.wait_ge(lo_free[u], i + before + 1)
                                pool.wait_ge(hi_free[u], i + before + 1)
                                pool.sem_inc(pool_turn, 1)
                                split_high(nc.gpsimd, hT[0][:, :, to], hf[u][:]).then_inc(high_ready[u], 1)
                                pool.wait_ge(high_ready[u], i + before + 1)
                                split_low(nc.gpsimd, hT[1][:, :, to], hf[u][:], hT[0][:, :, to]).then_inc(split[u], 1)

                @block.vector
                def _(dve):
                    link = Chain(dve, chain)
                    dve.wait_ge(const_in, 16 * NCONST)
                    if gain is None:
                        nc.vector.tensor_scalar(fac[:], mv[:, :, 1, :], 1.0, None, ALU.add).then_inc(fac_ready, 1)
                        dve.wait_ge(fac_ready, 1)
                    else:
                        for r in range(2):
                            f = nc.vector.scalar_tensor_tensor(fac[:, r, :], mv[:, r, 1, :], 1.0, gn[:], ALU.add, ALU.mult)
                        f.then_inc(fac_ready, 1)
                        dve.wait_ge(fac_ready, 1)
                    for _, r, t0, rounds, before in SPANS:
                        with dve.Fori(0, rounds) as i:
                            link.body(i, 6 if gain is None else 8)
                            for u in range(2):
                                dve.wait_ge(x_full[u], (i + before + 1) * 16)
                                for h in range(2):
                                    b = nc.vector.bn_stats(st[u][:, h, :], x[u][:, h * NT:(h + 1) * NT])
                                link(b)
                                dve.sem_inc(aggr_turn, 1)
                                link(nc.vector.bn_aggr(ag[u][:], st[u][:]))
                                if gain is None:
                                    nc.vector.tensor_scalar(va[u][:], ag[u][:, 1:2], eps, None, ALU.add).then_inc(var_ready[u], 1)
                                else:
                                    link(nc.vector.scalar_tensor_tensor(va[u][:], ag[u][:, 0:1], ag[u][:, 0:1], ag[u][:, 1:2],
                                                                        ALU.mult, ALU.add))
                                    nc.vector.tensor_scalar(va[u][:], va[u][:], eps, None, ALU.add).then_inc(var_ready[u], 1)
                                dve.wait_ge(sd_ready[u], i + before + 1)
                                link(nc.vector.reciprocal(sd[u][:], sd[u][:]))
                                dve.wait_ge(tr_full[2 * u + 1], i + before)
                                if gain is None:
                                    n = nc.vector.tensor_scalar(xn[u][:], x[u][:], ag[u][:, 0:1], sd[u][:], ALU.subtract, ALU.mult)
                                else:
                                    n = nc.vector.tensor_scalar(xn[u][:], x[u][:], sd[u][:], None, ALU.mult)
                                n.then_inc(xn_full[u], 1)
                                dve.wait_ge(tr_full[2 * u], i + before + 1)
                                dve.wait_ge(split[u], i + before)
                                for k in range(4):
                                    e = nc.vector.tensor_scalar(hf[u][:, k, :],
                                                                ps[2 * u][:, k * P:(k + 1) * P],
                                                                fac[:, r, k:k + 1], mv[:, r, 0, k:k + 1], ALU.mult, ALU.add)
                                e.then_inc(lo_free[u], 1)
                        link.end(rounds)

        w_sb = [s.sb(f"w{u}", [P, KT, P]) for u in range(2)]
        w_part = [[s.sb(f"w{u}_{part}", [P, KT, P], F32R) for part in ("high", "low")] for u in range(2)]
        high_ready, w_split, w_used, pool_turn = s.sems("w_high_ready", 2), s.sems("w_split", 2), s.sems("w_used", 2), s.sem("pool_turn")
        o = [s.sb(f"o{u}", [P, T]) for u in range(2)]
        ps = s.banks(5)
        w_full, o_out = s.sems("w_full", 2), s.sems("o_out", 2)
        b_full, b_free = s.sems("b_full", 5), s.sems("b_free", 5)
        wv = w.rearrange("(k p) n -> p k n", p=P)

        def chunks(with_ctx):
            return list(enumerate(CHUNKS if with_ctx else CHUNKS[:-1]))

        def spans():
            by_slot, tiles, with_c = [0, 0], 0, 0
            for m0, m, with_ctx in groups:
                for first, slots, rounds in ((m0, 2, m // 2), (m0 + m // 2 * 2, 1, m % 2)):
                    if rounds:
                        yield first, slots, rounds, with_ctx, list(by_slot), tiles, with_c
                        for u in range(slots):
                            by_slot[u] += rounds
                        tiles += slots * rounds
                        with_c += slots * rounds * with_ctx
            ends[:] = by_slot

        ends = []

        with nc.Block() as block:
            @block.sync
            def _(sp):
                for m0, slots, rounds, _, before, _, _ in spans():
                    with sp.Fori(0, rounds) as i:
                        for u in range(slots):
                            sp.wait_ge(w_split[u], i + before[u])
                            sp.dma_start(w_sb[u][:], wv[:, :, ds((i * slots + u + m0) * P, P)]).then_inc(w_full[u], 16)

            @block.gpsimd
            def _(pool):
                for _, slots, rounds, _, before, _, _ in spans():
                    with pool.Fori(0, rounds) as i:
                        for u in range(slots):
                            pool.wait_ge(w_full[u], (i + before[u] + 1) * 16)
                            pool.wait_ge(w_used[u], i + before[u])
                            pool.sem_inc(pool_turn, 1)
                            split_high(nc.gpsimd, w_part[u][0][:], w_sb[u][:]).then_inc(high_ready[u], 1)
                            pool.wait_ge(high_ready[u], i + before[u] + 1)
                            split_low(nc.gpsimd, w_part[u][1][:], w_sb[u][:], w_part[u][0][:]).then_inc(w_split[u], 1)

            @block.tensor
            def _(pe):
                for _, slots, rounds, with_ctx, before, tb, cb in spans():
                    with pe.Fori(0, rounds) as i:
                        for u in range(slots):
                            pe.wait_ge(w_split[u], i + before[u] + 1)
                            for c, (t0, n) in chunks(with_ctx):
                                pe.wait_ge(b_free[c], i * slots + u + (cb if c == 4 else tb))
                                for k in range(KT):
                                    mm = split_product(nc, ps[c][:, 0:n], [a[:, k, :] for a in w_part[u]], [a[:, k, t0:t0 + n] for a in hT],
                                                       k == 0, k == KT - 1)
                                mm.then_inc(b_full[c], 1)
                            pe.wait_ge(b_full[c], i * slots + u + 1 + (cb if c == 4 else tb))
                            pe.sem_inc(w_used[u], 1)

            def copy_out(eng, copy, i, u, slots, with_ctx, tb, cb, mine):
                for c, (t0, n) in chunks(with_ctx):
                    if c in mine:
                        eng.wait_ge(b_full[c], i * slots + u + 1 + (cb if c == 4 else tb))
                        copy(o[u][:, t0:t0 + n], ps[c][:, 0:n]).then_inc(b_free[c], 1)

            @block.vector
            def _(dve):
                for _, slots, rounds, with_ctx, before, tb, cb in spans():
                    with dve.Fori(0, rounds) as i:
                        for u in range(slots):
                            dve.wait_ge(o_out[u], (i + before[u]) * 16)
                            copy_out(dve, nc.vector.tensor_copy, i, u, slots, with_ctx, tb, cb, (0, 2, 4))

            @block.scalar
            def _(act):
                for m0, slots, rounds, with_ctx, before, tb, cb in spans():
                    with act.Fori(0, rounds) as i:
                        for u in range(slots):
                            act.wait_ge(o_out[u], (i + before[u]) * 16)
                            copy_out(act, nc.scalar.copy, i, u, slots, with_ctx, tb, cb, (1, 3))
                            for c, _ in chunks(with_ctx):
                                act.wait_ge(b_free[c], i * slots + u + 1 + (cb if c == 4 else tb))
                            width = T if with_ctx else SEQ
                            act.dma_start(out[ds((i * slots + u + m0) * P, P), 0:width], o[u][:, 0:width]).then_inc(o_out[u], 16)
                for u in range(2):
                    act.wait_ge(o_out[u], 16 * ends[u])


def out_project(nc, name, yT, zT, w, x_in, gate, kind, gain, bias, out, tiles, token0):
    a = ALPHA if kind == "ln" else 1.0
    with ExitStack() as ctx:
        s = Scope(nc, ctx, name)
        w_sb = [s.sb(f"w{u}", [P, D]) for u in range(2)]
        w_part = [s.sb(f"w_{part}", [P, KT, D], F32R) for part in ("high", "low")]
        m_part = [[s.sb(f"m{u}_{part}", [P, KT, P], F32R) for part in ("high", "low")] for u in range(2)]
        w_full, w_high, w_split = s.sems("w_full", 2), s.sem("w_high"), s.sems("w_split", 2)
        m_high, m_split, pool_turn = s.sems("m_high", 2), s.sems("m_split", 2), s.sem("pool_turn")
        gate_r, gain_r, bias_r = s.sb("gate", [P, D]), s.sb("gain", [P, D]), s.sb("bias", [P, D])
        y = [s.sb(f"y{u}", [P, KT, P]) for u in range(2)]
        z = [s.sb(f"z{u}", [P, KT, P]) for u in range(2)]
        m = [s.sb(f"m{u}", [P, KT, P]) for u in range(2)]
        x = [s.sb(f"x{u}", [P, D]) for u in range(2)]
        r = [s.sb(f"r{u}", [P, D]) for u in range(2)]
        o = [s.sb(f"o{u}", [P, D]) for u in range(2)]
        st = [s.sb(f"st{u}", [P, 2, 6]) for u in range(2)]
        ag = [s.sb(f"ag{u}", [P, 2]) for u in range(2)]
        va = [s.sb(f"va{u}", [P, 1]) for u in range(2)]
        sd = [s.sb(f"sd{u}", [P, 1]) for u in range(2)]
        ps = s.banks(4)
        w_in, chain, aggr_turn = s.sem("w_in"), s.sem("chain"), s.sem("aggr_turn")
        yz_full, x_full = s.sems("yz_full", 2), s.sems("x_full", 2)
        silu_ready, mix_ready = s.sems("silu_ready", 2), s.sems("mix_ready", 2)
        y_full, res_ready = s.sems("y_full", 2), s.sems("res_ready", 2)
        var_ready, sd_ready = s.sems("var_ready", 2), s.sems("sd_ready", 2)
        o_full, o_out = s.sems("o_full", 2), s.sems("o_out", 2)
        rows = [gate] + ([gain] if kind != "plain" else []) + ([bias] if kind == "ln" else [])
        yv, zv = yT.rearrange("(k p) t -> p k t", p=P), zT.rearrange("(k p) t -> p k t", p=P)
        eps = 1e-5 if kind == "ln" else 1e-6
        rounds = tiles // 2

        with nc.Block() as block:
            @block.sync
            def _(sp):
                for row, dst in zip(rows, (gate_r, gain_r, bias_r)):
                    sp.dma_start(dst[:], row.partition_broadcast(P)).then_inc(w_in, 16)
                for k in range(KT):
                    if k >= 2:
                        sp.wait_ge(w_split[k % 2], k // 2)
                    sp.dma_start(w_sb[k % 2][:], w[k * P:(k + 1) * P, :]).then_inc(w_full[k % 2], 16)
                with sp.Fori(0, rounds) as i:
                    for u in range(2):
                        cols = ds((i * 2 + u) * P + token0, P)
                        sp.wait_ge(mix_ready[u], i)
                        sp.dma_start(y[u][:], yv[:, :, cols]).then_inc(yz_full[u], 16)
                        sp.dma_start(z[u][:], zv[:, :, cols]).then_inc(yz_full[u], 16)
                        sp.wait_ge(res_ready[u], i)
                        sp.dma_start(x[u][:], x_in[ds((i * 2 + u) * P, P), :]).then_inc(x_full[u], 16)

            @block.scalar
            def _(act):
                def silu(i, u):
                    act.wait_ge(yz_full[u], (i + 1) * 32)
                    nc.scalar.activation(z[u][:], z[u][:], ACT.Silu).then_inc(silu_ready[u], 1)

                def tail(i, u):
                    if kind != "plain":
                        act.wait_ge(var_ready[u], i + 1)
                        nc.scalar.activation(sd[u][:], va[u][:], ACT.Sqrt).then_inc(sd_ready[u], 1)
                    act.wait_ge(o_full[u], i + 1)
                    act.dma_start(out[ds((i * 2 + u) * P, P), :], o[u][:]).then_inc(o_out[u], 16)

                for k in range(KT):
                    act.wait_ge(w_full[k % 2], (k // 2 + 1) * 16)
                    nc.scalar.copy(w_part[0][:, k, :], w_sb[k % 2][:]).then_inc(w_high, 1)
                silu(0, 0)
                silu(0, 1)
                if rounds > 1:
                    with act.Fori(0, rounds - 1) as i:
                        for u in range(2):
                            silu(i + 1, u)
                            tail(i, u)
                tail(rounds - 1, 0)
                tail(rounds - 1, 1)
                for u in range(2):
                    act.wait_ge(o_out[u], 16 * rounds)

            @block.tensor
            def _(pe):
                for u in range(2):
                    pe.wait_ge(w_split[u], KT // 2)
                with pe.Fori(0, rounds) as i:
                    for u in range(2):
                        pe.wait_ge(m_split[u], i + 1)
                        pe.wait_ge(res_ready[u], i)
                        for h in range(2):
                            for k in range(KT):
                                mm = split_product(nc, ps[2 * u + h][:], [a[:, k, :] for a in m_part[u]],
                                                   [a[:, k, h * NT:(h + 1) * NT] for a in w_part], k == 0, k == KT - 1)
                        mm.then_inc(y_full[u], 1)

            @block.gpsimd
            def _(pool):
                with pool.Fori(0, rounds) as i:
                    for u in range(2):
                        pool.wait_ge(mix_ready[u], i + 1)
                        pool.wait_ge(y_full[u], i)
                        pool.sem_inc(pool_turn, 1)
                        split_high(nc.gpsimd, m_part[u][0][:], m[u][:]).then_inc(m_high[u], 1)
                        pool.wait_ge(m_high[u], i + 1)
                        split_low(nc.gpsimd, m_part[u][1][:], m[u][:], m_part[u][0][:]).then_inc(m_split[u], 1)

            @block.vector
            def _(dve):
                link = Chain(dve, chain)
                dve.wait_ge(w_in, 16 * len(rows))

                def mix(i, u):
                    dve.wait_ge(silu_ready[u], i + 1)
                    dve.wait_ge(m_split[u], i)
                    nc.vector.tensor_tensor(m[u][:], y[u][:], z[u][:], ALU.mult).then_inc(mix_ready[u], 1)

                def finish(i, u):
                    dve.wait_ge(y_full[u], i + 1)
                    dve.wait_ge(x_full[u], (i + 1) * 16)
                    for h in range(2):
                        c = slice(h * NT, (h + 1) * NT)
                        g = nc.vector.tensor_tensor(r[u][:, c], ps[2 * u + h][:], gate_r[:, c], ALU.mult)
                    link(g)
                    dve.wait_ge(o_out[u], i * 16)
                    dst = o if kind == "plain" else r
                    res = nc.vector.scalar_tensor_tensor(dst[u][:], x[u][:], a, r[u][:], ALU.mult, ALU.add)
                    res.then_inc(res_ready[u], 1)
                    if kind == "plain":
                        dve.wait_ge(res_ready[u], i + 1)
                        dve.sem_inc(o_full[u], 1)
                        return
                    dve.wait_ge(res_ready[u], i + 1)
                    for h in range(2):
                        b = nc.vector.bn_stats(st[u][:, h, :], r[u][:, h * NT:(h + 1) * NT])
                    link(b)
                    dve.sem_inc(aggr_turn, 1)
                    link(nc.vector.bn_aggr(ag[u][:], st[u][:]))
                    if kind == "ln":
                        link(nc.vector.tensor_copy(va[u][:], ag[u][:, 1:2]))
                    else:
                        link(nc.vector.scalar_tensor_tensor(va[u][:], ag[u][:, 0:1], ag[u][:, 0:1], ag[u][:, 1:2],
                                                            ALU.mult, ALU.add))
                    nc.vector.tensor_scalar(va[u][:], va[u][:], eps, None, ALU.add).then_inc(var_ready[u], 1)
                    dve.wait_ge(sd_ready[u], i + 1)
                    link(nc.vector.reciprocal(sd[u][:], sd[u][:]))
                    if kind == "ln":
                        link(nc.vector.tensor_scalar(r[u][:], r[u][:], ag[u][:, 0:1], sd[u][:], ALU.subtract, ALU.mult))
                        link(nc.vector.tensor_tensor(r[u][:], r[u][:], gain_r[:], ALU.mult))
                        nc.vector.tensor_tensor(o[u][:], r[u][:], bias_r[:], ALU.add).then_inc(o_full[u], 1)
                    else:
                        link(nc.vector.tensor_scalar(r[u][:], r[u][:], sd[u][:], None, ALU.mult))
                        nc.vector.tensor_tensor(o[u][:], r[u][:], gain_r[:], ALU.mult).then_inc(o_full[u], 1)

                steps = {"plain": 1, "ln": 7, "rms": 6}[kind]
                for k in range(KT):
                    dve.wait_ge(w_high, k + 1)
                    split_low(nc.vector, w_part[1][:, k, :], w_sb[k % 2][:], w_part[0][:, k, :]).then_inc(w_split[k % 2], 1)
                mix(0, 0)
                mix(0, 1)
                if rounds > 1:
                    with dve.Fori(0, rounds - 1) as i:
                        link.body(i, 2 * steps)
                        for u in range(2):
                            mix(i + 1, u)
                            finish(i, u)
                    link.end(rounds - 1)
                finish(rounds - 1, 0)
                finish(rounds - 1, 1)


POOL_CH, POOL_PAD = 256, 8


def pool_branch(nc, PT, w, scale, inv_count, yT):
    ROWS, W = SEQ // HD, HD
    WP = W + 2 * POOL_PAD
    with ExitStack() as ctx:
        s = Scope(nc, ctx, "pool")
        u = [s.sb(f"u{t}", [P, ROWS, WP]) for t in range(2)]
        a1, a2, a4, a8 = (s.sb(f"a{k}", [P, ROWS, WP]) for k in (1, 2, 4, 8))
        pooled = [s.sb(f"pooled{t}", [P, ROWS, W]) for t in range(2)]
        cnt = s.sb("cnt", [P, 2, W])
        wd = s.sb("wd", [P, 2, P])
        sc = s.sb("sc", [P, 2])
        o = [s.sb(f"o{t}", [P, SEQ]) for t in range(2)]
        ps = s.banks(4)
        zeroed, const_in, u_in = s.sem("zeroed"), s.sem("const_in"), s.sem("u_in")
        chain, pooled_ready, prod, scaled, stored = (s.sem(n) for n in ("chain", "pooled_ready", "prod", "scaled", "stored"))

        with nc.Block() as block:
            @block.sync
            def _(sp):
                sp.wait_ge(zeroed, 3)
                for t in range(2):
                    sp.dma_start(u[t][:, :, POOL_PAD:POOL_PAD + W],
                                 PT[t * P:(t + 1) * P, 0:SEQ].rearrange("p (r w) -> p r w", w=W)).then_inc(u_in, 16)
                sp.dma_start(cnt[:], inv_count).then_inc(const_in, 16)
                sp.dma_start(sc[:], scale.rearrange("(t p) -> p t", p=P), allow_slow_non_contiguous=True).then_inc(const_in, 16)
                for g in range(4):
                    h = g % 2 * HD
                    sp.dma_start(wd[h:h + HD, g // 2, h:h + HD], w[g]).then_inc(const_in, 16)
                for t in range(2):
                    sp.wait_ge(scaled, 4 * (t + 1))
                    sp.dma_start(yT[t * P:(t + 1) * P, 0:SEQ], o[t][:]).then_inc(stored, 16)
                sp.wait_ge(stored, 32)

            @block.vector
            def _(dve):
                link = Chain(dve, chain)
                for b in (u[0], u[1], wd):
                    nc.vector.memset(b[:], 0.0).then_inc(zeroed, 1)
                dve.wait_ge(u_in, 32)
                dve.wait_ge(const_in, 16 * 6)
                for t in range(2):
                    for dst, src, lo, hi, r in ((a1, u[t], 1, WP, (-1, 0)), (a2, a1, 2, WP - 1, (-1, 1)),
                                                (a4, a2, 4, WP - 3, (-2, 2)), (a8, a4, 8, WP - 7, (-4, 4))):
                        if t == 0 and dst in (a4, a8):
                            continue
                        link(nc.vector.tensor_tensor(dst[:, :, lo:hi], src[:, :, lo + r[0]:hi + r[0]],
                                                     src[:, :, lo + r[1]:hi + r[1]], ALU.add))
                    for h, sums in enumerate(((a1, a2), (a4, a8))[t]):
                        q = slice(h * HD, (h + 1) * HD)
                        link(nc.vector.tensor_tensor(pooled[t][q], sums[q, :, POOL_PAD:POOL_PAD + W],
                                                     cnt[q, t:t + 1, :].broadcast_to([HD, ROWS, W]), ALU.mult))
                    nc.vector.tensor_tensor(pooled[t][:], pooled[t][:], u[t][:, :, POOL_PAD:POOL_PAD + W], ALU.subtract
                                            ).then_inc(pooled_ready, 1)

            @block.tensor
            def _(pe):
                for t in range(2):
                    pe.wait_ge(pooled_ready, t + 1)
                    for c in range(4):
                        if t:
                            pe.wait_ge(scaled, c + 1)
                        nc.tensor.matmul(ps[c][:], wd[:, t, :], pooled[t][:, c * 8:(c + 1) * 8, :].rearrange("p r w -> p (r w)"),
                                         start=True, stop=True).then_inc(prod, 1)

            @block.scalar
            def _(act):
                for t in range(2):
                    for c in range(4):
                        act.wait_ge(prod, 4 * t + c + 1)
                        nc.scalar.activation(o[t][:, c * NT:(c + 1) * NT], ps[c][:], ACT.Copy, scale=sc[:, t:t + 1]).then_inc(scaled, 1)


D_R = 384
MT_R = D_R // P
CH = T // P
DECAY = 0.6065306597126334


def step_of(d, c):
    nl, ncx = SEQ // P, CTX // P
    if d == 0:
        return c - nl if c >= nl else c + ncx
    return ncx - 1 - (c - nl) if c >= nl else ncx + nl - 1 - c


def rwkv_inputs(nc, PT, row0, shift, w0, w_up, a0, a_up, k_k, k_a, r_k, head_ones, seg, R, E, bonusT):
    UW = T + 3
    SPLIT = [(0, SEQ, 1), (SEQ, CTX, SEQ + 2)]
    CHUNKS = [(c * NT, NT) for c in range(4)] + [(SEQ, CTX)]
    with ExitStack() as ctx:
        s = Scope(nc, ctx, "rin")
        raw = [s.sb(f"raw{i}", [P, UW]) for i in range(2)]
        tw, xa, r, k, v, kk, sg, a, cum, wi, w, tmp, t2, bon = (
            s.sb(n, [P, T]) for n in ("tw", "xa", "r", "k", "v", "kk", "sg", "a", "cum", "wi", "w", "tmp", "t2", "bon"))
        al, be, ka, rh = (s.sb(n, [P, T]) for n in ("al", "be", "ka", "rh"))
        e = s.sb("e", [P, 6, CH])
        sh = s.sb("sh", [P, 3, 11])
        prm = s.sb("prm", [P, 8, MT_R])
        rk = s.sb("rk", [P, 2, MT_R])
        wu, au = s.sb("wu", [P, D_R]), s.sb("au", [P, D_R])
        eps_col = s.sb("eps", [P, 1])
        ho, sgm = s.sb("ho", [P, P]), s.sb("sgm", [P, 2, T])
        ps = s.banks(8)
        const_in, raw_in, raw_used = s.sem("const_in"), s.sems("raw_in", 2), s.sems("raw_used", 2)
        chain, achain = s.sem("chain"), s.sem("achain")
        prod, taken = s.sem("prod"), s.sem("taken")
        tanh_ready, xa_ready, sq_ready, rt_ready = (s.sem(n) for n in ("tanh_ready", "xa_ready", "sq_ready", "rt_ready"))
        xw_ready, sig_ready, cum_ready, exp_ready, arrays_ready, dir_used = (
            s.sem(n) for n in ("xw_ready", "sig_ready", "cum_ready", "exp_ready", "arrays_ready", "dir_used"))
        stored, bon_ready, bon_sum, bon_out, pads = (s.sem(n) for n in ("stored", "bon_ready", "bon_sum", "bon_out", "pads"))
        ORDER = [9, 10] + [t for m in range(MT_R) for t in (m, 3 + m, 6 + m)]
        USES = []
        for m in range(MT_R):
            USES += [("norm", m, 0, c) for c in range(5)]
            for d in range(2):
                USES += [("w", m, d, c) for c in range(5)] + [("a", m, d, c) for c in range(5)]
            USES += [("bonus", m, 0, c) for c in range(4)]
        AT = {use: n for n, use in enumerate(USES)}

        with nc.Block() as block:
            @block.sync
            def _(sp):
                def col(dst, src):
                    sp.dma_start(dst, src, allow_slow_non_contiguous=True).then_inc(const_in, 16)
                for j in range(3):
                    col(sh[:, j, :], shift[j].rearrange("(t p) -> p t", p=P))
                for d in range(2):
                    col(prm[:, d, :], w0[d].rearrange("(t p) -> p t", p=P))
                    col(prm[:, 2 + d, :], a0[d].rearrange("(t p) -> p t", p=P))
                    col(rk[:, d, :], r_k[d].rearrange("(t h) k -> (h k) t", h=2))
                    sp.dma_start(wu[d * HD:(d + 1) * HD, :], w_up[d]).then_inc(const_in, 16)
                    sp.dma_start(au[d * HD:(d + 1) * HD, :], a_up[d]).then_inc(const_in, 16)
                col(prm[:, 4, :], k_k.rearrange("(t p) -> p t", p=P))
                col(prm[:, 5, :], k_a.rearrange("(t p) -> p t", p=P))
                sp.dma_start(ho[:], head_ones).then_inc(const_in, 16)
                sp.dma_start(sgm[:], seg).then_inc(const_in, 16)
                sp.wait_ge(pads, 3)
                for n, t in enumerate(ORDER):
                    if n >= 2:
                        sp.wait_ge(raw_used[n % 2], n // 2)
                    for t0, cnt, at in SPLIT:
                        sp.dma_start(raw[n % 2][:, at:at + cnt], PT[row0 + t * P:row0 + (t + 1) * P, t0:t0 + cnt]
                                     ).then_inc(raw_in[n % 2], 16)

            @block.gpsimd
            def _(pool):
                for b in (raw[0], raw[1]):
                    nc.gpsimd.memset(b[:], 0.0).then_inc(pads, 1)
                nc.gpsimd.memset(eps_col[:], 1e-12).then_inc(pads, 1)
                for m in range(MT_R):
                    for d in range(2):
                        n = m * 2 + d
                        pool.wait_ge(arrays_ready, n + 1)
                        for j, arr in enumerate((al, rh, be, ka, v)):
                            pool.dma_start(R[:, m, d, :, j, :].rearrange("c p t -> p c t"), arr[:].rearrange("p (c t) -> p c t", t=P)
                                           ).then_inc(stored, 16)
                        pool.wait_ge(stored, 16 * 5 * (n + 1))
                        pool.sem_inc(dir_used, 1)
                    pool.wait_ge(bon_sum, m + 1)
                    pool.dma_start(bonusT[m * P:(m + 1) * P, :], bon[:, 0:SEQ]).then_inc(bon_out, 16)
                    pool.wait_ge(bon_out, 16 * (m + 1))
                pool.dma_start(E, e[:]).then_inc(bon_out, 16)
                pool.wait_ge(bon_out, 16 * (MT_R + 1))

            @block.vector
            def _(dve):
                link = Chain(dve, chain)
                dve.wait_ge(const_in, 16 * 17)
                link(nc.vector.tensor_scalar(prm[:, 6, :], prm[:, 5, :], -1.0, 1.0, ALU.mult, ALU.add))

                def shifted(n, dst):
                    t = ORDER[n]
                    dve.wait_ge(raw_in[n % 2], 32 * (n // 2 + 1))
                    src = raw[n % 2]
                    for j in range(3):
                        for t0, cnt, at in SPLIT:
                            x, o = src[:, at - 1 + j:at - 1 + j + cnt], dst[:, t0:t0 + cnt]
                            if j == 0:
                                ins = nc.vector.tensor_scalar(o, x, sh[:, 0, t:t + 1], None, ALU.mult)
                            else:
                                ins = nc.vector.scalar_tensor_tensor(o, x, sh[:, j, t:t + 1], o, ALU.mult, ALU.add)
                            last = ins
                        link(last)
                    dve.sem_inc(raw_used[n % 2], 1)

                shifted(0, tmp)
                dve.sem_inc(xw_ready, 1)
                shifted(1, xa)
                dve.sem_inc(xa_ready, 1)
                dve.wait_ge(tanh_ready, 1)
                for m in range(MT_R):
                    if m:
                        dve.wait_ge(dir_used, 2 * m)
                    for j, dst in enumerate((r, k, v)):
                        shifted(2 + 3 * m + j, dst)
                    link(nc.vector.tensor_scalar(kk[:], k[:], prm[:, 4, m:m + 1], None, ALU.mult))
                    nc.vector.tensor_tensor(tmp[:], kk[:], kk[:], ALU.mult).then_inc(sq_ready, 1)
                    dve.wait_ge(rt_ready, m + 1)
                    link(nc.vector.reciprocal(t2[:], t2[:]))
                    link(nc.vector.tensor_tensor(kk[:], kk[:], t2[:], ALU.mult))
                    for d in range(2):
                        n = m * 2 + d
                        dve.wait_ge(sig_ready, n + 1)
                        rev = slice(None, None, -1) if d else slice(None)
                        link(nc.vector.tensor_tensor_scan(cum[:, rev], sgm[:, d, rev], sg[:, rev], 0.0, ALU.mult, ALU.add))
                        nc.vector.tensor_tensor(tmp[:], cum[:], sg[:], ALU.subtract).then_inc(cum_ready, 1)
                        link(nc.vector.tensor_scalar(t2[:], a[:], prm[:, 5, m:m + 1], prm[:, 6, m:m + 1], ALU.mult, ALU.add))
                        link(nc.vector.tensor_tensor(t2[:], t2[:], k[:], ALU.mult))
                        link(nc.vector.tensor_tensor(a[:], a[:], kk[:], ALU.mult))
                        if d == 0:
                            if m:
                                dve.wait_ge(bon_out, 16 * m)
                            link(nc.vector.scalar_tensor_tensor(bon[:], r[:], rk[:, d, m:m + 1], t2[:], ALU.mult, ALU.mult))
                        dve.wait_ge(exp_ready, n + 1)
                        if n:
                            dve.wait_ge(dir_used, n)
                        link(nc.vector.tensor_tensor(be[:], a[:], wi[:], ALU.mult))
                        link(nc.vector.tensor_tensor(ka[:], t2[:], wi[:], ALU.mult))
                        link(nc.vector.tensor_tensor(rh[:], r[:], w[:], ALU.mult))
                        link(nc.vector.tensor_tensor(al[:], kk[:], tmp[:], ALU.mult))
                        at = P - 1 if d == 0 else 0
                        wv = w[:, :].rearrange("p (c t) -> p c t", t=P)[:, :, at]
                        for t0, cnt in ((0, SEQ // P), (SEQ // P, CTX // P)):
                            s0 = step_of(d, t0)
                            o = e[:, n, s0:s0 + cnt] if d == 0 else e[:, n, s0 - cnt + 1:s0 + 1]
                            src = wv[:, t0:t0 + cnt] if d == 0 else wv[:, t0:t0 + cnt][:, ::-1]
                            cp = nc.vector.tensor_copy(o, src)
                        cp.then_inc(arrays_ready, 1)
                        if d == 1:
                            link(nc.vector.scalar_tensor_tensor(t2[:], r[:], rk[:, d, m:m + 1], t2[:], ALU.mult, ALU.mult))
                            nc.vector.tensor_tensor(bon[:], bon[:], t2[:], ALU.add).then_inc(bon_ready, 1)
                            dve.wait_ge(bon_ready, m + 1)
                    for c in range(4):
                        q = AT[("bonus", m, 0, c)]
                        dve.wait_ge(prod, q + 1)
                        b = nc.vector.tensor_tensor(bon[:, c * NT:(c + 1) * NT], ps[q % 8][:], v[:, c * NT:(c + 1) * NT], ALU.mult)
                        b.then_inc(taken, 1)
                    dve.wait_ge(taken, AT[("bonus", m, 0, 3)] + 1)
                    dve.sem_inc(bon_sum, 1)

            @block.tensor
            def _(pe):
                pe.wait_ge(const_in, 16 * 17)
                pe.wait_ge(tanh_ready, 1)
                pe.wait_ge(xa_ready, 1)
                for q, (what, m, d, c) in enumerate(USES):
                    t0, n = CHUNKS[c]
                    if q >= 8:
                        pe.wait_ge(taken, q - 7)
                    out = ps[q % 8][:, 0:n]
                    h = slice(d * HD, (d + 1) * HD)
                    if what == "norm":
                        pe.wait_ge(sq_ready, m + 1)
                        mm = nc.tensor.matmul(out, ho[:], tmp[:, t0:t0 + n], start=True, stop=True)
                    elif what == "w":
                        mm = nc.tensor.matmul(out, wu[h, m * P:(m + 1) * P], tw[h, t0:t0 + n], start=True, stop=True)
                    elif what == "a":
                        mm = nc.tensor.matmul(out, au[h, m * P:(m + 1) * P], xa[h, t0:t0 + n], start=True, stop=True)
                    else:
                        pe.wait_ge(bon_ready, m + 1)
                        mm = nc.tensor.matmul(out, ho[:], bon[:, t0:t0 + n], start=True, stop=True)
                    mm.then_inc(prod, 1)

            @block.scalar
            def _(act):
                link = Chain(act, achain)
                act.wait_ge(const_in, 16 * 17)
                act.wait_ge(pads, 3)
                act.wait_ge(xw_ready, 1)
                nc.scalar.activation(tw[:], tmp[:], ACT.Tanh).then_inc(tanh_ready, 1)
                for m in range(MT_R):
                    for c, (t0, n) in enumerate(CHUNKS):
                        q = AT[("norm", m, 0, c)]
                        act.wait_ge(prod, q + 1)
                        nc.scalar.activation(t2[:, t0:t0 + n], ps[q % 8][:, 0:n], ACT.Sqrt, bias=eps_col[:, 0:1]).then_inc(taken, 1)
                    act.wait_ge(taken, q + 1)
                    act.sem_inc(rt_ready, 1)
                    for d in range(2):
                        nn = m * 2 + d
                        if nn:
                            act.wait_ge(arrays_ready, nn)
                        for what, dst, col in (("w", sg, d), ("a", a, 2 + d)):
                            for c, (t0, n) in enumerate(CHUNKS):
                                q = AT[(what, m, d, c)]
                                act.wait_ge(prod, q + 1)
                                nc.scalar.activation(dst[:, t0:t0 + n], ps[q % 8][:, 0:n], ACT.Sigmoid, bias=prm[:, col, m:m + 1]).then_inc(taken, 1)
                        act.wait_ge(taken, q + 1)
                        act.sem_inc(sig_ready, 1)
                        act.wait_ge(cum_ready, nn + 1)
                        link(nc.scalar.activation(w[:], cum[:], ACT.Exp, scale=-DECAY))
                        link(nc.scalar.activation(wi[:], cum[:], ACT.Exp, scale=DECAY))
                        nc.scalar.activation(tmp[:], tmp[:], ACT.Exp, scale=-DECAY).then_inc(exp_ready, 1)


def rwkv_scan(nc, R, E, masks, levels, ident, YR):
    NL = 4
    LV = 7
    X_AL, X_RH, X_BE, X_KA, X_V = range(5)
    LB_RUNS = ((1, 2), (2, 4), (4, LV))
    LBN = 2 + len(LB_RUNS)
    NCX, NLT = CTX // P, SEQ // P
    BODY = [("gram", 1), ("first", 1)] + [(f"{w}{b}", 1) for b in range(1, LV) for w in "zn"] + [("x", 2), ("pt", 1)]
    KINDS = {False: BODY + [("chain", 1)], True: BODY + [("chain", 1), ("out", 2)]}

    with ExitStack() as ctx:
        s = Scope(nc, ctx, "rsc")
        X = [[s.sb(f"X{m}{d}", [P, 5, P]) for d in range(2)] for m in range(MT_R)]
        S = [[s.sb(f"S{m}{d}", [P, HD]) for d in range(2)] for m in range(MT_R)]
        TL = [s.sb(f"TL{d}", [P, 4, P]) for d in range(2)]
        M4 = [s.sb(f"M4{h}", [P, 4 * P]) for h in range(NL)]
        LB = [s.sb(f"LB{h}", [P, LV, P]) for h in range(NL)]
        W = [s.sb(f"W{h}", [P, HD + 2 * P]) for h in range(NL)]
        Z = [s.sb(f"Z{h}", [P, P]) for h in range(NL)]
        X12 = [s.sb(f"X12{h}", [P, P]) for h in range(NL)]
        X1T = [s.sb(f"X1T{h}", [P, P]) for h in range(NL)]
        PT = [s.sb(f"PT{h}", [P, HD]) for h in range(NL)]
        U = [s.sb(f"U{h}", [P, HD]) for h in range(NL)]
        Y = [[s.sb(f"Y{m}{d}", [P, P]) for d in range(2)] for m in range(MT_R)]
        mk = s.sb("mk", [P, 2, 4 * P])
        lv = s.sb("lv", [P, 2, LV, P])
        idn = s.sb("idn", [P, P])
        e = s.sb("e", [P, 6, CH])
        bank = s.banks(NL)
        tbank = [ctx.enter_context(nc.psum_tensor(f"rsc_tbank{d}", [P, 4, P], F32)) for d in range(2)]
        const_in, zeroed = s.sem("const_in"), s.sem("zeroed")
        x_in, x_used = s.sems("x_in", MT_R), s.sems("x_used", MT_R)
        prod, evac, lb_ready = s.sems("prod", NL), s.sems("evac", NL), s.sems("lb_ready", NL)
        t_prod, t_evac = s.sems("t_prod", 2), s.sems("t_evac", 2)
        y_out = s.sems("y_out", MT_R)

        def rows(h):
            return slice(h % 2 * HD, h % 2 * HD + HD)

        def counts(emit, i, m):
            p, v = (len(KINDS[emit]), sum(n for _, n in KINDS[emit]))
            p0, v0 = (len(KINDS[False]) * MT_R * NCX, sum(n for _, n in KINDS[False]) * MT_R * NCX) if emit else (0, 0)
            u0 = NCX * MT_R if emit else 0
            return (i * MT_R + m) * p + p0, (i * MT_R + m) * v + v0, i * MT_R + m + u0

        def scan(eng, unit):
            with eng.Fori(0, NCX) as i:
                for m in range(MT_R):
                    unit(False, i, m, *counts(False, i, m))
            with eng.Fori(0, NLT) as i:
                for m in range(MT_R):
                    unit(True, i, m, *counts(True, i, m))

        def walk(emit):
            v = 0
            for n, (name, k) in enumerate(KINDS[emit]):
                yield name, n, v
                v += k

        with nc.Block() as block:
            @block.sync
            def _(sp):
                for dst, src in ((mk, masks), (lv, levels), (idn, ident), (e, E)):
                    sp.dma_start(dst[:], src).then_inc(const_in, 16)

                def unit(emit, i, m, p, v, n):
                    step = i + NCX if emit else i
                    sp.wait_ge(x_used[m], step)
                    for d in range(2):
                        c = (i if d == 0 else i * -1 + (NLT - 1)) if emit else (i + NLT if d == 0 else i * -1 + (NLT + NCX - 1))
                        sp.dma_start(X[m][d][:], R[ds(c, 1), m, d].rearrange("o p a t -> p (o a) t")).then_inc(x_in[m], 16)

                scan(sp, unit)

            @block.gpsimd
            def _(pool):
                for m in range(MT_R):
                    for d in range(2):
                        nc.gpsimd.memset(S[m][d][:], 0.0).then_inc(zeroed, 1)
                pool.wait_ge(const_in, 64)

                def unit(emit, i, m, p, v, n):
                    for h in range(NL):
                        pool.wait_ge(evac[h], v + 1)
                        nc.gpsimd.tensor_tensor(LB[h][:, 0, :], M4[h][:, 0:P], lv[:, h // 2, 0, :], ALU.mult).then_inc(lb_ready[h], 1)
                        pool.wait_ge(lb_ready[h], n * LBN + 1)
                        nc.gpsimd.tensor_tensor(W[h][:, HD + P:], LB[h][:, 0, :], idn[:], ALU.add).then_inc(lb_ready[h], 1)
                    for lo, hi in LB_RUNS:
                        for h in range(NL):
                            nc.gpsimd.tensor_tensor(LB[h][:, lo:hi, :], M4[h][:, 0:P].unsqueeze(1).broadcast_to([P, hi - lo, P]),
                                                    lv[:, h // 2, lo:hi, :], ALU.mult).then_inc(lb_ready[h], 1)

                scan(pool, unit)

            @block.tensor
            def _(pe):
                pe.wait_ge(const_in, 64)
                pe.wait_ge(zeroed, 6)

                def mm(out, l, r, start=True, stop=True):
                    return nc.tensor.matmul(out, l, r, start=start, stop=stop)

                def unit(emit, i, m, p, v, n):
                    step = i + NCX if emit else i
                    pe.wait_ge(x_in[m], (step + 1) * 32)
                    for d in range(2):
                        pe.wait_ge(t_evac[d], n)
                        for j, a in enumerate((X_AL, X_BE, X_KA, X_V)):
                            t = nc.tensor.transpose(tbank[d][:, j, :], X[m][d][:, a, :], idn[:])
                        t.then_inc(t_prod[d], 1)
                    for name, pn, vn in walk(emit):
                        for h in range(NL):
                            d, q, b = h // 2, rows(h), bank[h]
                            x, w = X[m][d], W[h]
                            pe.wait_ge(evac[h], v + vn)
                            if name == "gram":
                                mm(b[:, 0:2 * P], x[q, X_BE, :], x[q, X_AL:X_RH + 1, :].rearrange("p a t -> p (a t)"))
                                last = mm(b[:, 2 * P:], x[q, X_KA, :], x[q, X_AL:X_RH + 1, :].rearrange("p a t -> p (a t)"))
                            elif name == "first":
                                if h % 2 == 0:
                                    pe.wait_ge(t_evac[d], n + 1)
                                pe.wait_ge(lb_ready[h], n * LBN + 2)
                                mm(b[:, 0:HD], M4[h][:, 2 * P:3 * P], TL[d][:, 3, q])
                                last = nc.tensor.transpose(b[:, HD:HD + P], w[:, HD + P:], idn[:])
                            elif name[0] == "z":
                                for x_, (lo, _) in enumerate(LB_RUNS):
                                    if int(name[1]) == lo:
                                        pe.wait_ge(lb_ready[h], n * LBN + 3 + x_)
                                last = mm(b[:, 0:P], LB[h][:, int(name[1]), :], w[:, HD:HD + P])
                            elif name[0] == "n":
                                if int(name[1]) < LV - 1:
                                    mm(b[:, P:2 * P], w[:, HD + P:], Z[h][:])
                                last = mm(b[:, 2 * P:3 * P], Z[h][:], w[:, HD + P:])
                            elif name == "x":
                                mm(b[:, 0:HD], w[:, HD + P:], TL[d][:, 0, q])
                                mm(b[:, HD:P], w[:, HD + P:], w[:, 0:HD])
                                last = mm(b[q, P:2 * P], TL[d][:, 0, q], w[:, HD + P:])
                            elif name == "pt":
                                last = mm(b[q, 0:HD], X12[h][:, 0:HD], TL[d][:, 1, q])
                            elif name == "chain":
                                if emit:
                                    mm(b[:, 0:HD], X1T[h][q, :], S[m][d][q, :])
                                mm(b[q, HD:P], TL[d][:, 2, q], TL[d][:, 3, q], stop=False)
                                mm(b[q, HD:P], PT[h][q, :], S[m][d][q, :], start=False, stop=False)
                                last = mm(b[q, HD:P], TL[d][:, 1, q], X12[h][:, HD:P], start=False)
                            else:
                                mm(b[q, P:2 * P], TL[d][:, 3, q], M4[h][:, 3 * P:], stop=False)
                                mm(b[q, P:2 * P], S[m][d][q, :], x[q, X_RH, :], start=False, stop=False)
                                last = mm(b[q, P:2 * P], U[h][:], M4[h][:, P:2 * P], start=False)
                            last.then_inc(prod[h], 1)

                scan(pe, unit)

            @block.scalar
            def _(act):
                act.wait_ge(const_in, 64)

                def unit(emit, i, m, p, v, n):
                    for d in range(2):
                        act.wait_ge(t_prod[d], n + 1)
                        nc.scalar.copy(TL[d][:], tbank[d][:]).then_inc(t_evac[d], 1)
                    for name, pn, vn in walk(emit):
                        for h in range(NL):
                            d, q, b = h // 2, rows(h), bank[h]
                            if name == "first":
                                act.wait_ge(prod[h], p + pn + 1)
                                nc.scalar.copy(W[h][:, 0:HD + P], b[:, 0:HD + P]).then_inc(evac[h], 1)
                            elif name[0] == "z":
                                act.wait_ge(prod[h], p + pn + 1)
                                nc.scalar.copy(Z[h][:], b[:, 0:P]).then_inc(evac[h], 1)
                            elif name == "x":
                                act.wait_ge(prod[h], p + pn + 1)
                                nc.scalar.mul(X12[h][:], b[:, 0:P], -1.0).then_inc(evac[h], 1)
                                nc.scalar.mul(X1T[h][q, :], b[q, P:2 * P], -1.0).then_inc(evac[h], 1)
                    if emit:
                        for h in range(NL):
                            act.wait_ge(evac[h], v + sum(k for _, k in KINDS[True]))
                        for d in range(2):
                            tok = (i * P) if d == 0 else (i * -P + (NLT - 1) * P)
                            act.dma_start(YR[d, m * P:(m + 1) * P, ds(tok, P)], Y[m][d][:]).then_inc(y_out[m], 16)

                scan(act, unit)
                for m in range(MT_R):
                    act.wait_ge(y_out[m], 32 * NLT)

            @block.vector
            def _(dve):
                dve.wait_ge(const_in, 64)

                def unit(emit, i, m, p, v, n):
                    step = i + NCX if emit else i
                    for name, pn, vn in walk(emit):
                        for h in range(NL):
                            d, q, b = h // 2, rows(h), bank[h]
                            if name in ("first", "x") or name[0] == "z":
                                continue
                            dve.wait_ge(prod[h], p + pn + 1)
                            if name == "gram":
                                ins = nc.vector.tensor_tensor(M4[h][:], b[:], mk[:, d, :], ALU.mult)
                            elif name[0] == "n":
                                lo = P if int(name[1]) < LV - 1 else 2 * P
                                w = W[h][:, HD + lo - P:]
                                ins = nc.vector.tensor_tensor(w, w, b[:, lo:3 * P], ALU.subtract)
                            elif name == "pt":
                                ins = nc.vector.tensor_tensor(PT[h][q, :], b[q, 0:HD], idn[q, q], ALU.add)
                            elif name == "chain" and emit:
                                ins = nc.vector.tensor_tensor(U[h][:], b[:, 0:HD], X12[h][:, HD:P], ALU.add)
                            else:
                                ins = nc.vector.tensor_scalar(S[m][d][q, :], b[q, HD:P],
                                                              e[q, m * 2 + d, ds(step, 1)], None, ALU.mult)
                                if emit:
                                    ins.then_inc(evac[h], 1)
                                    if h == 0:
                                        dve.wait_ge(y_out[m], i * 32)
                                    ins = nc.vector.tensor_copy(Y[m][d][q, :], b[q, P:2 * P])
                            ins.then_inc(evac[h], 1)
                    dve.sem_inc(x_used[m], 1)

                scan(dve, unit)


def hgrn(nc, PT, q0, i0, z0, seg, masks, ident, YH):
    LV = 7
    HALF = SEQ // 2
    HC = HALF // P
    NLT, NCX = SEQ // P, CTX // P
    WALK = [(d, c) for d in range(2) for c in sorted(range(CH), key=lambda c: step_of(d, c))]
    LAT = [(d, c) for d, c in WALK if c < NLT]
    NW, NL = len(WALK), len(LAT)
    AHEAD_ACT, AHEAD_DVE = (2, 7, 8, 9), (3, 4, 5, 11, 12)
    LEVELS = (range(0, 3), range(3, 5), range(5, LV))
    with ExitStack() as ctx:
        s = Scope(nc, ctx, "hg")
        q, v, z, cum = s.sb("q", [P, SEQ]), s.sb("v", [P, T]), s.sb("z", [P, T]), s.sb("cum", [P, T])
        k = [s.sb(f"k{d}", [P, T]) for d in range(2)]
        qe = [s.sb(f"qe{d}", [P, SEQ]) for d in range(2)]
        ke = [s.sb(f"ke{d}", [P, T]) for d in range(2)]
        ec = [s.sb(f"ec{d}", [P, CH]) for d in range(2)]
        LVL = [s.sb(f"lv{u}", [P, LV, HALF]) for u in range(2)]
        sgm, mk, idn = s.sb("sgm", [P, T]), s.sb("mk", [P, 2, LV + 1, P]), s.sb("idn", [P, P])
        KI = [s.sb(f"KI{u}", [P, 2, P]) for u in range(2)]
        PR = [[s.sb(f"P{u}{h}", [P, LV + 1, P]) for h in range(2)] for u in range(2)]
        S = [s.sb(f"S{u}", [P, HD]) for u in range(2)]
        Y = [s.sb(f"Y{u}", [P, HALF]) for u in range(2)]
        sc = [ctx.enter_context(nc.psum_tensor(f"hg_sc{h}", [P, LV + 1, P], F32)) for h in range(2)]
        tb = [ctx.enter_context(nc.psum_tensor(f"hg_tb{u}", [P, 2, P], F32)) for u in range(2)]
        yb = s.banks(2)
        const_in = s.sem("const_in")
        qv_in, z_in, seg_in, qv_used = s.sem("qv_in"), s.sem("z_in"), s.sem("seg_in"), s.sem("qv_used")
        chain, achain = s.sem("chain"), s.sem("achain")
        ln_ready, arg_ready, cum_ready, kearg_ready, exp_ready = (
            s.sem(n) for n in ("ln_ready", "arg_ready", "cum_ready", "kearg_ready", "exp_ready"))
        kq_ready, lvarg, lvexp, lvl_ready = s.sem("kq_ready"), s.sems("lvarg", 2), s.sems("lvexp", 2), s.sems("lvl_ready", 2)
        sc_prod, sc_evac = s.sems("sc_prod", 2), s.sems("sc_evac", 2)
        t_prod, t_evac, y_prod, y_evac = s.sems("t_prod", 2), s.sems("t_evac", 2), s.sems("y_prod", 2), s.sems("y_evac", 2)
        y_out, lv_used = s.sems("y_out", 2), s.sems("lv_used", 2)

        def runs(d):
            return [(0, 0), (1, HALF)] if d == 0 else [(0, HALF), (1, 0)]

        def halves(ap, b, d):
            x = ap.rearrange("p (n h b) -> p n h b", h=2, b=b)
            return (x[:, :, 1, :], x[:, :, 0, :], x[:, :, 0, b - 1:b]) if d == 0 else (x[:, :, 0, :], x[:, :, 1, :], x[:, :, 1, 0:1])

        with nc.Block() as block:
            @block.sync
            def _(sp):
                sp.dma_start(mk[:], masks).then_inc(const_in, 16)
                sp.dma_start(idn[:], ident).then_inc(const_in, 16)
                with sp.Fori(0, MT_R) as m:
                    for d in range(2):
                        sp.wait_ge(cum_ready, m * 2 + d)
                        sp.dma_start(z[:], PT[ds(m * P + (z0 + d * D_R), P), :]).then_inc(z_in, 16)
                        sp.dma_start(sgm[:], seg[:, d, :]).then_inc(z_in, 16)
                        if d == 0:
                            sp.wait_ge(y_evac[0], m * (NW // 2))
                            sp.wait_ge(y_evac[1], m * (NW // 2))
                            sp.dma_start(q[:], PT[ds(m * P + q0, P), 0:SEQ]).then_inc(qv_in, 16)
                            sp.dma_start(v[:], PT[ds(m * P + i0, P), :]).then_inc(qv_in, 16)
                    for d in range(2):
                        for w, t0 in runs(d):
                            n = d * CH + NCX + HC * (w + 1) - 1
                            for b in range(2):
                                sp.wait_ge(y_evac[b], m * (NW // 2) + (n - (n % 2 != b)) // 2 + 1)
                            sp.dma_start(YH[d, ds(m * P, P), t0:t0 + HALF], Y[w][:]).then_inc(y_out[w], 16)
                for w in range(2):
                    sp.wait_ge(y_out[w], 16 * 2 * MT_R)

            @block.gpsimd
            def _(pool):
                with pool.Fori(0, MT_R) as m:
                    for d in range(2):
                        pool.wait_ge(kearg_ready, m * 2 + d + 1)
                        for u, t0 in runs(d):
                            pool.wait_ge(lv_used[u], m * 2 + d)
                            for j in range(LV):
                                later, earlier, r = halves(cum[:, t0:t0 + HALF], 2 ** j, d)
                                lo, eo, _ = halves(LVL[u][:, j, :], 2 ** j, d)
                                rb = r.broadcast_to([P, HALF >> (j + 1), 2 ** j])
                                nc.gpsimd.tensor_tensor(lo, later, rb, ALU.subtract)
                                last = nc.gpsimd.tensor_tensor(eo, rb, earlier, ALU.subtract)
                            last.then_inc(lvarg[u], 1)

            @block.scalar
            def _(act):
                act.wait_ge(const_in, 32)
                link = Chain(act, achain)

                def transposed(n, m):
                    u = n % 2
                    act.wait_ge(t_prod[u], m * (NW // 2) + n // 2 + 1)
                    nc.scalar.copy(KI[u][:], tb[u][:]).then_inc(t_evac[u], 1)

                with act.Fori(0, MT_R) as m:
                    link.body(m, 4)
                    act.wait_ge(y_evac[0], m * (NW // 2))
                    act.wait_ge(y_evac[1], m * (NW // 2))

                    def softplus(d):
                        act.wait_ge(z_in, (m * 2 + d + 1) * 32)
                        link(nc.scalar.activation(k[d][:], z[:], ACT.Abs))
                        link(nc.scalar.activation(k[d][:], k[d][:], ACT.Exp, scale=-1.0))
                        nc.scalar.activation(k[d][:], k[d][:], ACT.Ln, bias=1.0).then_inc(ln_ready, 1)

                    def exp_k(d):
                        act.wait_ge(kearg_ready, m * 2 + d + 1)
                        nc.scalar.activation(k[d][:], k[d][:], ACT.Exp)

                    def exp_cum(d):
                        nc.scalar.activation(qe[d][:], cum[:, 0:SEQ], ACT.Exp)
                        at = P - 1 if d == 0 else 0
                        nc.scalar.activation(ec[d][:], cum[:].rearrange("p (c t) -> p c t", t=P)[:, :, at], ACT.Exp)

                    def exp_ke(d):
                        nc.scalar.activation(ke[d][:], ke[d][:], ACT.Exp).then_inc(exp_ready, 1)

                    def exp_levels(d, u):
                        act.wait_ge(lvarg[u], m * 2 + d + 1)
                        nc.scalar.activation(LVL[u][:], LVL[u][:], ACT.Exp).then_inc(lvexp[u], 1)

                    for part in (softplus, exp_k, exp_cum, exp_ke):
                        part(0)
                    exp_levels(0, 0)
                    for n in range(NW):
                        d, k0 = divmod(n, CH)
                        if k0 == 4:
                            exp_levels(d, 1)
                        if d == 0 and k0 in AHEAD_ACT:
                            (softplus, exp_k, exp_cum, exp_ke)[AHEAD_ACT.index(k0)](1)
                        if d == 0 and k0 == 14:
                            exp_levels(1, 0)
                        transposed(n, m)

            @block.vector
            def _(dve):
                link = Chain(dve, chain)
                dve.wait_ge(const_in, 32)

                def log_f(m, d):
                    dve.wait_ge(ln_ready, m * 2 + d + 1)
                    link(nc.vector.scalar_tensor_tensor(ke[d][:], z[:], 0.0, k[d][:], ALU.min, ALU.subtract))
                    link(nc.vector.tensor_tensor(k[d][:], ke[d][:], z[:], ALU.subtract))

                def running_sums(m, d):
                    rev = slice(None, None, -1) if d else slice(None)
                    for u in range(2):
                        dve.wait_ge(lvarg[u], m * 2 + d)
                    nc.vector.tensor_tensor_scan(cum[:, rev], sgm[:, rev], ke[d][:, rev], 0.0, ALU.mult, ALU.add).then_inc(cum_ready, 1)

                def ke_exponent(m, d):
                    dve.wait_ge(cum_ready, m * 2 + d + 1)
                    at = P - 1 if d == 0 else 0
                    cv = cum[:].rearrange("p (c t) -> p c t", t=P)
                    nc.vector.tensor_tensor(ke[d][:].rearrange("p (c t) -> p c t", t=P), cv[:, :, at:at + 1].broadcast_to([P, CH, P]),
                                            cv, ALU.subtract).then_inc(kearg_ready, 1)

                def times_k(m, d):
                    dve.wait_ge(exp_ready, m * 2 + d + 1)
                    nc.vector.tensor_tensor(ke[d][:], ke[d][:], k[d][:], ALU.mult)

                def times_q(m, d):
                    dve.wait_ge(qv_in, (m + 1) * 32)
                    nc.vector.tensor_tensor(qe[d][:], qe[d][:], q[:], ALU.mult).then_inc(kq_ready, 1)

                PREPARE = (log_f, running_sums, ke_exponent, times_k, times_q)

                def scale(m, d, u, levels):
                    t0 = runs(d)[u][1]
                    dve.wait_ge(lvexp[u], m * 2 + d + 1)
                    for j in levels:
                        lo, eo, _ = halves(LVL[u][:, j, :], 2 ** j, d)
                        lq, _, _ = halves(q[:, t0:t0 + HALF], 2 ** j, d)
                        _, ek, _ = halves(k[d][:, t0:t0 + HALF], 2 ** j, d)
                        nc.vector.tensor_tensor(lo, lo, lq, ALU.mult)
                        last = nc.vector.tensor_tensor(eo, eo, ek, ALU.mult)
                    if levels[-1] == LV - 1:
                        last.then_inc(lvl_ready[u], 1)

                def scores(m, n, h):
                    d, c = WALK[n]
                    nl = LAT.index((d, c))
                    dve.wait_ge(sc_prod[h], m * NL + nl + 1)
                    nc.vector.tensor_tensor(PR[n % 2][h][:], sc[h][:], mk[:, d], ALU.mult).then_inc(sc_evac[h], 1)

                def chunk_out(m, n):
                    d, c = WALK[n]
                    u = n % 2
                    dve.wait_ge(y_prod[u], m * (NW // 2) + n // 2 + 1)
                    if n:
                        dve.wait_ge(y_evac[1 - u], m * (NW // 2) + (n + 1) // 2)
                    if n % CH == 0:
                        st = nc.vector.tensor_copy(S[u][:], yb[u][:, P:P + HD])
                    else:
                        st = nc.vector.scalar_tensor_tensor(S[u][:], S[1 - u][:], ec[d][:, c:c + 1], yb[u][:, P:P + HD], ALU.mult, ALU.add)
                    if c < NLT:
                        nl = LAT.index((d, c))
                        w = nl // HC % 2
                        if nl % HC == 0:
                            dve.wait_ge(y_out[w], (m * 2 + d) * 16)
                        t = (c * P) % HALF
                        st = nc.vector.tensor_copy(Y[w][:, t:t + P], yb[u][:, 0:P])
                    st.then_inc(y_evac[u], 1)

                with dve.Fori(0, MT_R) as m:
                    link.body(m, 4)
                    for part in PREPARE:
                        part(m, 0)
                    scale(m, 0, 0, range(LV))
                    for d in range(2):
                        for n in range(d * CH, (d + 1) * CH):
                            k0 = n - d * CH
                            if k0 in (6, 7, 8):
                                scale(m, d, 1, LEVELS[k0 - 6])
                            if d == 0 and k0 in AHEAD_DVE:
                                PREPARE[AHEAD_DVE.index(k0)](m, 1)
                            if d == 0 and k0 in (15, 16, 17):
                                scale(m, 1, 0, LEVELS[k0 - 15])
                            if WALK[n][1] < NLT:
                                for h in range(2):
                                    scores(m, n, h)
                                if (k0 - NCX) % HC == HC - 1:
                                    dve.sem_inc(lv_used[(k0 - NCX) // HC], 1)
                            if n:
                                chunk_out(m, n - 1)
                    chunk_out(m, NW - 1)

            @block.tensor
            def _(pe):
                pe.wait_ge(const_in, 32)

                def front(m, n):
                    d, c = WALK[n]
                    u, t = n % 2, slice(c * P, (c + 1) * P)
                    if n % CH == 0:
                        pe.wait_ge(kq_ready, m * 2 + d + 1)
                    pe.wait_ge(t_evac[u], m * (NW // 2) + n // 2)
                    nc.tensor.transpose(tb[u][:, 0, :], ke[d][:, t], idn[:])
                    nc.tensor.transpose(tb[u][:, 1, :], v[:, t], idn[:]).then_inc(t_prod[u], 1)
                    if c >= NLT:
                        return
                    nl = LAT.index((d, c))
                    w = nl // HC % 2
                    if nl % HC == 0:
                        pe.wait_ge(lvl_ready[w], m * 2 + d + 1)
                    tl = slice(c * P % HALF, c * P % HALF + P)
                    for h in range(2):
                        r = slice(h * HD, (h + 1) * HD)
                        pe.wait_ge(sc_evac[h], m * NL + nl)
                        for j in range(LV):
                            nc.tensor.matmul(sc[h][:, j, :], LVL[w][r, j, tl], LVL[w][r, j, tl], start=True, stop=True)
                        nc.tensor.matmul(sc[h][:, LV, :], k[d][r, t], q[r, t], start=True, stop=True).then_inc(sc_prod[h], 1)

                def back(m, n):
                    d, c = WALK[n]
                    u, t = n % 2, slice(c * P, (c + 1) * P)
                    pe.wait_ge(t_evac[u], m * (NW // 2) + n // 2 + 1)
                    pe.wait_ge(y_evac[u], m * (NW // 2) + n // 2)
                    pe.wait_ge(y_evac[1 - u], m * (NW // 2) + (n + 1) // 2)
                    if c < NLT:
                        nl = LAT.index((d, c))
                        for h in range(2):
                            pe.wait_ge(sc_evac[h], m * NL + nl + 1)
                    for h in range(2):
                        r = slice(h * HD, (h + 1) * HD)
                        last = nc.tensor.matmul(yb[u][r, P:P + HD], KI[u][:, 0, r], KI[u][:, 1, r], start=True, stop=True)
                        if c < NLT:
                            for j in range(LV + 1):
                                nc.tensor.matmul(yb[u][r, 0:P], KI[u][:, 1, r], PR[u][h][:, j, :], start=(j == 0), stop=False)
                            last = nc.tensor.matmul(yb[u][r, 0:P], S[1 - u][r, :], qe[d][r, t], start=False, stop=True)
                    last.then_inc(y_prod[u], 1)

                with pe.Fori(0, MT_R) as m:
                    front(m, 0)
                    for n in range(NW):
                        if n + 1 < NW:
                            front(m, n + 1)
                        back(m, n)


def head_norm(nc, name, items, mean_ones, gather, spread, rope=None):
    with ExitStack() as ctx:
        s = Scope(nc, ctx, name)
        WMAX = max(it["w"] for it in items)
        NI = len(items)
        a, b, p = ([s.sb(f"{n}{h}", [P, WMAX]) for h in range(2)] for n in "abp")
        g = s.sb("g", [P, NI, 2])
        ep = s.sb("ep", [P, NI])
        mo = s.sb("mo", [P, P])
        ga, sp_ = s.sb("ga", [P, 4, P]), s.sb("sp", [P, 4, P])
        inv = [s.sb(f"inv{h}", [P, NT]) for h in range(2)]
        cs = s.sb("cs", [P, 2, SEQ if rope else 1])
        sw = s.sb("sw", [P, P])
        banks = s.banks(8)
        bank = [banks[0:4], banks[4:8]]
        const_in, set_up = s.sem("const_in"), s.sem("set_up")
        a_in, stored = s.sems("a_in", 2), s.sems("stored", 2)
        prod, sums, done = s.sems("prod", 2), s.sems("sums", 2), s.sems("done", 2)
        squared, root, inverse = s.sems("squared", 2), s.sems("root", 2), s.sems("inverse", 2)
        chain = s.sem("chain")
        NCONST = 3 + sum(P // it[key].shape[0] for it in items for key in ("gain", "bias") if it[key] is not None) + (3 if rope else 0)

        def chunks(it):
            return [(j, j * NT, min(NT, it["w"] - j * NT)) for j in range(-(-it["w"] // NT))]

        def groups():
            for n in range(0, NI, 2):
                yield [(h, n + h, items[n + h]) for h in range(2) if n + h < NI]

        def before(n, what):
            return sum(what(items[k]) for k in range(n % 2, n, 2))

        def loads(it):
            return 1 + (it["b"] is not None) + (it["plus"] is not None)

        def prods(it):
            return it["center"] + 2 + it["rotate"]

        with nc.Block() as block:
            @block.sync
            def _(sp):
                for dst, src in ((mo, mean_ones), (ga, gather), (sp_, spread)):
                    sp.dma_start(dst[:], src).then_inc(const_in, 16)
                if rope:
                    for dst, src in ((cs[:, 0, :], rope[0]), (cs[:, 1, :], rope[1]), (sw[:], rope[2])):
                        sp.dma_start(dst, src).then_inc(const_in, 16)
                for n, it in enumerate(items):
                    for j, key in enumerate(("gain", "bias")):
                        if it[key] is not None:
                            v = it[key]
                            for r in range(P // v.shape[0]):
                                sp.dma_start(g[r * v.shape[0]:(r + 1) * v.shape[0], n, j:j + 1], v.rearrange("(p o) -> p o", o=1)
                                             ).then_inc(const_in, 16)
                for gr in groups():
                    for h, n, it in gr:
                        if n >= 2:
                            sp.wait_ge(stored[h], 16 * (n // 2))
                        for dst, key in ((a, "a"), (b, "b"), (p, "plus")):
                            if it[key] is not None:
                                sp.dma_start(dst[h][:, 0:it["w"]], it[key]).then_inc(a_in[h], 16)

            @block.gpsimd
            def _(pool):
                for n, it in enumerate(items):
                    nc.gpsimd.memset(ep[:, n:n + 1], it["eps"]).then_inc(set_up, 1)

            @block.vector
            def _(dve):
                link = Chain(dve, chain)
                dve.wait_ge(const_in, 16 * NCONST)
                for gr in groups():
                    for h, n, it in gr:
                        w = it["w"]
                        dve.wait_ge(a_in[h], 16 * (before(n, loads) + loads(it)))
                        if it["b"] is not None:
                            nc.vector.tensor_tensor(a[h][:, 0:w], a[h][:, 0:w], b[h][:, 0:w], ALU.add).then_inc(sums[h], 1)
                        else:
                            dve.sem_inc(sums[h], 1)
                    for h, n, it in gr:
                        if it["center"]:
                            dve.wait_ge(prod[h], before(n, prods) + 1)
                            for j, t, c in chunks(it):
                                x = nc.vector.tensor_tensor(a[h][:, t:t + c], a[h][:, t:t + c], bank[h][j][:, 0:c], ALU.subtract)
                            x.then_inc(done[h], 1)
                    for h, n, it in gr:
                        dve.wait_ge(root[h], n // 2 + 1)
                        c = min(NT, it["w"])
                        nc.vector.reciprocal(inv[h][:, 0:c], inv[h][:, 0:c]).then_inc(inverse[h], 1)
                    for h, n, it in gr:
                        w = it["w"]
                        dve.wait_ge(prod[h], before(n, prods) + it["center"] + 2)
                        for j, t, c in chunks(it):
                            x = nc.vector.tensor_tensor(a[h][:, t:t + c], a[h][:, t:t + c], bank[h][j][:, 0:c], ALU.mult)
                        link(x)
                        o = nc.vector.tensor_scalar(a[h][:, 0:w], a[h][:, 0:w], g[:, n, 0:1],
                                                    None if it["bias"] is None else g[:, n, 1:2], ALU.mult,
                                                    *(() if it["bias"] is None else (ALU.add,)))
                        if it["plus"] is not None:
                            link(o)
                            o = nc.vector.tensor_tensor(a[h][:, 0:w], a[h][:, 0:w], p[h][:, 0:w], ALU.add)
                        o.then_inc(done[h], 1)
                    for h, n, it in gr:
                        if it["rotate"]:
                            w = it["w"]
                            dve.wait_ge(prod[h], before(n, prods) + prods(it))
                            for j, t, c in chunks(it):
                                x = nc.vector.tensor_tensor(b[h][:, t:t + c], bank[h][j][:, 0:c], cs[:, 1, t:t + c], ALU.mult)
                            nc.vector.tensor_tensor(a[h][:, 0:w], a[h][:, 0:w], cs[:, 0, 0:w], ALU.mult).then_inc(chain, 1)
                            link.n += 1
                            dve.wait_ge(chain, link.base + link.n)
                            nc.vector.tensor_tensor(a[h][:, 0:w], a[h][:, 0:w], b[h][:, 0:w], ALU.add).then_inc(done[h], 1)

            def dones(it):
                return it["center"] + 1 + it["rotate"]

            @block.tensor
            def _(pe):
                pe.wait_ge(const_in, 16 * NCONST)
                for gr in groups():
                    for h, n, it in gr:
                        if n >= 2:
                            pe.wait_ge(done[h], before(n, dones))
                        if it["center"]:
                            pe.wait_ge(sums[h], n // 2 + 1)
                            for j, t, c in chunks(it):
                                x = nc.tensor.matmul(bank[h][j][:, 0:c], mo[:], a[h][:, t:t + c], start=True, stop=True)
                            x.then_inc(prod[h], 1)
                    for h, n, it in gr:
                        pe.wait_ge(squared[h], n // 2 + 1)
                        for j, t, c in chunks(it):
                            x = nc.tensor.matmul(bank[h][0][:, 0:c], ga[:, j, :], b[h][:, t:t + c], start=(j == 0), stop=(t + c == it["w"]))
                        x.then_inc(prod[h], 1)
                    for h, n, it in gr:
                        pe.wait_ge(inverse[h], n // 2 + 1)
                        for j, t, c in chunks(it):
                            x = nc.tensor.matmul(bank[h][j][:, 0:c], sp_[:, j, :], inv[h][:, 0:c], start=True, stop=True)
                        x.then_inc(prod[h], 1)
                    for h, n, it in gr:
                        if it["rotate"]:
                            pe.wait_ge(done[h], before(n, dones) + dones(it) - 1)
                            for j, t, c in chunks(it):
                                x = nc.tensor.matmul(bank[h][j][:, 0:c], sw[:], a[h][:, t:t + c], start=True, stop=True)
                            x.then_inc(prod[h], 1)

            @block.scalar
            def _(act):
                act.wait_ge(set_up, NI)
                for gr in groups():
                    for h, n, it in gr:
                        w = it["w"]
                        act.wait_ge(sums[h], n // 2 + 1)
                        if it["b"] is None:
                            act.wait_ge(a_in[h], 16 * (before(n, loads) + loads(it)))
                        if it["center"]:
                            act.wait_ge(done[h], before(n, dones) + 1)
                        nc.scalar.activation(b[h][:, 0:w], a[h][:, 0:w], ACT.Square).then_inc(squared[h], 1)
                    for h, n, it in gr:
                        act.wait_ge(prod[h], before(n, prods) + it["center"] + 1)
                        c = min(NT, it["w"])
                        nc.scalar.activation(inv[h][:, 0:c], bank[h][0][:, 0:c], ACT.Sqrt, bias=ep[:, n:n + 1]).then_inc(root[h], 1)
                    for h, n, it in gr:
                        act.wait_ge(done[h], before(n, dones) + dones(it))
                        act.dma_start(it["out"], a[h][:, 0:it["w"]]).then_inc(stored[h], 16)
                for h in range(min(2, NI)):
                    act.wait_ge(stored[h], 16 * len(range(h, NI, 2)))


def conformer(nc, PT, w, b, ln_g, ln_b, ident, mean_ones, yT):
    NTL, K = 4, 31
    R = K // 2
    AT = [(0, SEQ, R), (SEQ, CTX, R + SEQ + R)]
    UW = R + SEQ + R + CTX + R
    CHUNKS = [(c * NT, NT) for c in range(4)] + [(SEQ, CTX)]
    ON_PE = (2, 3)
    with ExitStack() as ctx:
        s = Scope(nc, ctx, "cf")
        u = [s.sb(f"u{t}", [P, UW]) for t in range(NTL)]
        y = [s.sb(f"y{t}", [P, T]) for t in range(NTL)]
        g = [s.sb(f"g{i}", [P, T]) for i in range(2)]
        dg = s.sb("dg", [P, K, P])
        wt = s.sb("wt", [P, NTL, K])
        pr = s.sb("pr", [P, 3, NTL])
        idn, mo, ep = s.sb("idn", [P, P]), s.sb("mo", [P, P]), s.sb("ep", [P, 1])
        ps = s.banks(8)
        const_in, pads, g_in, u_in, gated, sig = (s.sem(n) for n in ("const_in", "pads", "g_in", "u_in", "gated", "sig"))
        dg_ready, tap_prod, tap_out, chain, conv_done = (s.sem(n) for n in ("dg_ready", "tap_prod", "tap_out", "chain", "conv_done"))
        mean_prod, centred, squared, var_prod, root, normed, acted, stored, used = (
            s.sem(n) for n in ("mean_prod", "centred", "squared", "var_prod", "root", "normed", "acted", "stored", "used"))

        with nc.Block() as block:
            @block.sync
            def _(sp):
                for t in range(NTL):
                    sp.dma_start(wt[:, t, :], w[:, t * P:(t + 1) * P].rearrange("k p -> p k"), allow_slow_non_contiguous=True).then_inc(const_in, 16)
                for j, v in enumerate((b, ln_g, ln_b)):
                    sp.dma_start(pr[:, j, :], v.rearrange("(t p) -> p t", p=P), allow_slow_non_contiguous=True).then_inc(const_in, 16)
                sp.dma_start(idn[:], ident).then_inc(const_in, 16)
                sp.dma_start(mo[:], mean_ones).then_inc(const_in, 16)
                sp.wait_ge(pads, NTL + 1)
                for n, t in enumerate((2, 0, 3, 1)):
                    for t0, cnt, at in AT:
                        sp.dma_start(u[t][:, at:at + cnt], PT[t * P:(t + 1) * P, t0:t0 + cnt]).then_inc(u_in, 16)
                    if n >= 2:
                        sp.wait_ge(gated, 2 * (n - 1))
                    sp.dma_start(g[n % 2][:], PT[(NTL + t) * P:(NTL + t + 1) * P, :]).then_inc(g_in, 16)
                    sp.wait_ge(g_in, 16 * (n + 1))
                    sp.wait_ge(u_in, 32 * (n + 1))
                for t in range(NTL):
                    sp.wait_ge(acted, t + 1)
                    sp.dma_start(yT[t * P:(t + 1) * P, :], y[t][:]).then_inc(stored, 16)
                sp.wait_ge(stored, 16 * NTL)

            @block.gpsimd
            def _(pool):
                for t in range(NTL):
                    nc.gpsimd.memset(u[t][:], 0.0).then_inc(pads, 1)
                nc.gpsimd.memset(ep[:], 1e-6).then_inc(pads, 1)
                pool.wait_ge(const_in, 16 * 9)
                for n, t in enumerate(ON_PE):
                    if n:
                        pool.wait_ge(tap_prod, 4)
                    for k in range(K):
                        nc.gpsimd.tensor_scalar(dg[:, k, :], idn[:], wt[:, t, k:k + 1], None, ALU.mult).then_inc(dg_ready, 1)

            @block.vector
            def _(dve):
                link = Chain(dve, chain)
                dve.wait_ge(const_in, 16 * 9)

                def gate(n, t):
                    dve.wait_ge(sig, n + 1)
                    dve.wait_ge(u_in, 32 * (n + 1))
                    for t0, cnt, at in AT:
                        nc.vector.tensor_tensor(u[t][:, at:at + cnt], u[t][:, at:at + cnt], g[n % 2][:, t0:t0 + cnt], ALU.mult).then_inc(gated, 1)
                    dve.wait_ge(gated, 2 * (n + 1))

                def taps(t, spans):
                    for k in range(K):
                        for t0, cnt, at in spans:
                            src, o = u[t][:, at - R + k:at - R + k + cnt], y[t][:, t0:t0 + cnt]
                            if k == 0:
                                x = nc.vector.tensor_scalar(o, src, wt[:, t, 0:1], pr[:, 0, t:t + 1], ALU.mult, ALU.add)
                            else:
                                x = nc.vector.scalar_tensor_tensor(o, src, wt[:, t, k:k + 1], o, ALU.mult, ALU.add)
                        link(x)

                gate(0, 2)
                gate(1, 0)
                gate(2, 3)
                gate(3, 1)
                for t in range(NTL):
                    taps(t, AT[1:] if t in ON_PE else AT)
                dve.sem_inc(conv_done, 1)
                dve.wait_ge(mean_prod, 5)
                for t in range(NTL):
                    for c, (t0, n) in enumerate(CHUNKS):
                        x = nc.vector.tensor_tensor(y[t][:, t0:t0 + n], y[t][:, t0:t0 + n], ps[c][:, 0:n], ALU.subtract)
                    x.then_inc(centred, 1)
                dve.wait_ge(root, 1)
                link(nc.vector.reciprocal(g[0][:], g[0][:]))
                for t in range(NTL):
                    nc.vector.tensor_tensor(y[t][:], y[t][:], g[0][:], ALU.mult).then_inc(normed, 1)

            @block.tensor
            def _(pe):
                pe.wait_ge(const_in, 16 * 9)
                for n, t in enumerate(ON_PE):
                    pe.wait_ge(gated, 2 if t == 2 else 6)
                    for k in range(K):
                        pe.wait_ge(dg_ready, n * K + k + 1)
                        for c in range(4):
                            x = nc.tensor.matmul(ps[4 * n + c][:], dg[:, k, :], u[t][:, c * NT + k:c * NT + k + NT],
                                                 start=(k == 0), stop=(k == K - 1))
                            if k == K - 1:
                                x.then_inc(tap_prod, 1)
                pe.wait_ge(conv_done, 1)
                pe.wait_ge(tap_out, 8)
                for c, (t0, n) in enumerate(CHUNKS):
                    for t in range(NTL):
                        x = nc.tensor.matmul(ps[c][:, 0:n], mo[:], y[t][:, t0:t0 + n], start=(t == 0), stop=(t == NTL - 1))
                    x.then_inc(mean_prod, 1)
                for c, (t0, n) in enumerate(CHUNKS):
                    pe.wait_ge(centred, NTL)
                    for t in range(NTL):
                        pe.wait_ge(squared, t + 1)
                        x = nc.tensor.matmul(ps[c][:, 0:n], mo[:], u[t][:, t0:t0 + n], start=(t == 0), stop=(t == NTL - 1))
                    x.then_inc(var_prod, 1)

            @block.scalar
            def _(act):
                act.wait_ge(const_in, 16 * 9)
                act.wait_ge(pads, NTL + 1)
                for n in range(NTL):
                    act.wait_ge(g_in, 16 * (n + 1))
                    nc.scalar.activation(g[n % 2][:], g[n % 2][:], ACT.Sigmoid).then_inc(sig, 1)
                for n, t in enumerate(ON_PE):
                    for c in range(4):
                        act.wait_ge(tap_prod, 4 * n + c + 1)
                        nc.scalar.activation(y[t][:, c * NT:(c + 1) * NT], ps[4 * n + c][:], ACT.Identity, bias=pr[:, 0, t:t + 1]).then_inc(tap_out, 1)
                for t in range(NTL):
                    act.wait_ge(centred, t + 1)
                    nc.scalar.activation(u[t][:, 0:T], y[t][:], ACT.Square).then_inc(squared, 1)
                for c, (t0, n) in enumerate(CHUNKS):
                    act.wait_ge(var_prod, c + 1)
                    x = nc.scalar.activation(g[0][:, t0:t0 + n], ps[c][:, 0:n], ACT.Sqrt, bias=ep[:, 0:1])
                x.then_inc(root, 1)
                for t in range(NTL):
                    act.wait_ge(normed, t + 1)
                    nc.scalar.activation(y[t][:], y[t][:], ACT.Silu, bias=pr[:, 2, t:t + 1], scale=pr[:, 1, t:t + 1]).then_inc(acted, 1)


class StackedSplit:

    def __init__(self, s, width_q, width_k):
        self.raw_q, self.raw_k = s.sb("raw_q", [P, width_q]), s.sb("raw_k", [P, width_k])
        self.q = [s.sb(f"q{u}", [P, width_q], F32R) for u in range(2)]
        self.k = [[s.sb(f"k{u}_{part}", [P, width_k], F32R) for part in ("high", "low")] for u in range(2)]
        self.raw_full, self.raw_used, self.high_ready, self.low_ready, self.turn = (
            s.sem(n) for n in ("raw_full", "raw_used", "high_ready", "low_ready", "split_turn"))
        self.ready = s.sems("qk_ready", 2)

    def load(self, sp, h, q_src, k_src):
        sp.wait_ge(self.raw_used, h)
        for r in range(2):
            sp.dma_start(self.raw_q[r * HD:(r + 1) * HD, :], q_src).then_inc(self.raw_full, 16)
            sp.dma_start(self.raw_k[r * HD:(r + 1) * HD, :], k_src).then_inc(self.raw_full, 16)

    def split(self, nc, pool, h, pair, u, slot_used):
        pool.wait_ge(self.raw_full, (h + 1) * 64)
        pool.wait_ge(slot_used, pair)
        pool.sem_inc(self.turn, 1)
        split_high(nc.gpsimd, self.k[u][0][:], self.raw_k[:])
        split_high(nc.gpsimd, self.q[u][:], self.raw_q[:]).then_inc(self.high_ready, 1)
        pool.wait_ge(self.high_ready, h + 1)
        split_low(nc.gpsimd, self.k[u][1][:], self.raw_k[:], self.k[u][0][:]).then_inc(self.low_ready, 1)
        pool.wait_ge(self.low_ready, h + 1)
        split_low(nc.gpsimd, self.q[u][HD:P, :], self.raw_q[HD:P, :], self.q[u][HD:P, :]).then_inc(self.ready[u], 1)
        pool.wait_ge(self.ready[u], pair + 1)
        pool.sem_inc(self.raw_used, 1)

    def product(self, nc, out, u, queries, keys):
        nc.tensor.matmul(out, self.q[u][:, queries], self.k[u][0][:, keys], start=True, stop=False)
        return nc.tensor.matmul(out, self.q[u][:, queries], self.k[u][1][:, keys], start=False, stop=True)


def attention(nc, QK, VT, ident, yT, row0):
    NH, NK, QT = 8, T // P, T // P
    NQL = SEQ // P
    SC = HD ** -0.5
    CHUNKS = [(c * NT, NT) for c in range(4)] + [(SEQ, CTX)]
    VG = [range(0, 6), range(6, 12), range(12, 18)]
    NGRP = len(VG) + NQL * 5 + 2 + 1
    assert NGRP % 2 == 0
    with ExitStack() as ctx:
        s = Scope(nc, ctx, "at")
        qk = StackedSplit(s, T, T)
        vt = [s.sb(f"vt{u}", [HD, T]) for u in range(2)]
        v = s.sb("v", [P, NK, HD])
        pr = [s.sb(f"p{u}", [P, T]) for u in range(2)]
        pt = [s.sb(f"pt{u}", [P, NK, P]) for u in range(2)]
        mx = [s.sb(f"mx{u}", [P, 5]) for u in range(2)]
        nb = [s.sb(f"nb{u}", [P, 1]) for u in range(2)]
        sm = [s.sb(f"sm{u}", [P, 5]) for u in range(2)]
        rs = [s.sb(f"rs{u}", [P, 1]) for u in range(2)]
        top_ = s.sb("top", [P, 1])
        o = [s.sb(f"o{u}", [P, HD]) for u in range(2)]
        y = [s.sb(f"y{u}", [HD, T]) for u in range(2)]
        idn = s.sb("idn", [P, P])
        sb_ = s.banks(5)
        tb = [ctx.enter_context(nc.psum_tensor(f"at_tb{u}", [P, NT], F32)) for u in range(2)]
        ob = ctx.enter_context(nc.psum_tensor("at_ob", [P, NT], F32))
        const_in, chain = s.sem("const_in"), s.sem("chain")
        in_full, in_used = s.sems("in_full", 2), s.sems("in_used", 2)
        s_full, s_free = s.sems("s_full", 5), s.sems("s_free", 5)
        t_full, t_free = s.sems("t_full", 2), s.sems("t_free", 2)
        nb_ready, sum_ready, pt_ready, v_ready = s.sem("nb_ready"), s.sem("sum_ready"), s.sems("pt_ready", 5), s.sem("v_ready")
        o_full, o_norm, ot_out = s.sem("o_full"), s.sem("o_norm"), s.sem("ot_out")
        y_out, turn_ = s.sems("y_out", 2), s.sem("turn")

        def groups(t):
            return range(5) if t < NQL else (4,)

        def cnt(h, t, c):
            return h * (NQL if c < 4 else QT) + t

        def grp(h, g):
            return g % 2, h * (NGRP // 2) + g // 2

        def gidx(t, g):
            return len(VG) + (t * 5 + g if t < NQL else NQL * 5 + t - NQL)

        def heads(eng, body):
            with eng.Fori(0, 2) as kv:
                with eng.Fori(0, 2) as j:
                    for u in range(2):
                        body(kv, kv * 4 + j * 2 + u, kv * 2 + j, u)

        BY_DVE = (0, 2, 4)

        with nc.Block() as block:
            @block.sync
            def _(sp):
                sp.dma_start(idn[:], ident).then_inc(const_in, 16)

                def body(kv, h, pair, u):
                    qk.load(sp, h, QK[ds(h * HD, HD), :], QK[ds(kv * HD + NH * HD, HD), :])
                    sp.wait_ge(in_used[u], pair)
                    sp.dma_start(vt[u][:], VT[ds(kv * HD, HD), :]).then_inc(in_full[u], 16)

                heads(sp, body)

            @block.tensor
            def _(pe):
                pe.wait_ge(const_in, 16)

                def score(h, u, t, c):
                    t0, n = CHUNKS[c]
                    pe.wait_ge(s_free[c], cnt(h, t, c))
                    qk.product(nc, sb_[c][:, 0:n], u, slice(t * P, (t + 1) * P), slice(t0, t0 + n)).then_inc(s_full[c], 1)

                def step(h, u, t):
                    x = t % 2
                    gs = groups(t)

                    def turn(g):
                        b, n = grp(h, gidx(t, g))
                        pe.wait_ge(t_free[b], n)
                        pe.wait_ge(s_free[g], cnt(h, t, g) + 1)
                        for j in range(4 if g < 4 else 2):
                            tr = nc.tensor.transpose(tb[b][:, j * P:(j + 1) * P], pr[x][:, (4 * g + j) * P:(4 * g + j + 1) * P], idn[:])
                        if g == 4 and t:
                            tr = last(h, t - 1, b)
                        tr.then_inc(t_full[b], 1)

                    def product(g):
                        if g == gs[0] and t:
                            pe.wait_ge(o_norm, h * QT + t)
                        pe.wait_ge(pt_ready[g], cnt(h, t, g) + 1)
                        for j in range(4 if g < 4 else 2):
                            kt = 4 * g + j
                            m = nc.tensor.matmul(ob[:, 0:HD], pt[x][:, kt, :], v[:, kt, :], start=(g == gs[0] and j == 0), stop=(kt == NK - 1))
                        return m

                    for i, g in enumerate(gs):
                        if t + 1 < QT and (g == 4 or t + 1 < NQL):
                            score(h, u, t + 1, g)
                        if i >= 2:
                            product(g - 2)
                        turn(g)
                    for g in gs[-2:]:
                        m = product(g)
                    m.then_inc(o_full, 1)

                def last(h, t, b):
                    pe.wait_ge(o_norm, h * QT + t + 1)
                    pe.sem_inc(turn_, 1)
                    return nc.tensor.transpose(tb[b][0:HD, 2 * P:3 * P], o[t % 2][:], idn[:])

                def body(kv, h, pair, u):
                    pe.wait_ge(in_full[u], (pair + 1) * 16)
                    for g, tiles in enumerate(VG):
                        b, n = grp(h, g)
                        pe.wait_ge(t_free[b], n)
                        pe.sem_inc(turn_, 1)
                        for j, kt in enumerate(tiles):
                            tr = nc.tensor.transpose(tb[b][:, j * HD:(j + 1) * HD], vt[u][:, kt * P:(kt + 1) * P], idn[0:HD, 0:HD])
                        tr.then_inc(t_full[b], 1)
                    pe.wait_ge(qk.ready[u], pair + 1)
                    for c in range(5):
                        score(h, u, 0, c)
                    pe.wait_ge(v_ready, (h + 1) * len(VG))
                    for t in range(QT):
                        step(h, u, t)
                    b, n = grp(h, NGRP - 1)
                    pe.wait_ge(t_free[b], n)
                    last(h, QT - 1, b).then_inc(t_full[b], 1)

                heads(pe, body)

            @block.vector
            def _(dve):
                dve.wait_ge(const_in, 16)
                link = Chain(dve, chain)

                def top(h, t, c):
                    x, n = t % 2, CHUNKS[c][1]
                    dve.wait_ge(s_full[c], cnt(h, t, c) + 1)
                    m = nc.vector.reduce_max(mx[x][:, c:c + 1], sb_[c][:, 0:n], AX)
                    if c < 4:
                        return
                    link(m)
                    src = mx[x][:] if t < NQL else mx[x][:, 4:5]
                    link(nc.vector.reduce_max(top_[:], src, AX))
                    nc.vector.tensor_scalar(nb[x][:], top_[:], -SC, None, ALU.mult).then_inc(nb_ready, 1)
                    dve.wait_ge(nb_ready, h * QT + t + 1)

                def take(h, t, g, u):
                    x = t % 2
                    b, n = grp(h, gidx(t, g))
                    w = 4 if g < 4 else 2
                    dve.wait_ge(t_full[b], n + 1)
                    nc.vector.tensor_copy(pt[x][:, 4 * g:4 * g + w, :].rearrange("p a b -> p (a b)"), tb[b][:, 0:w * P]).then_inc(pt_ready[g], 1)
                    dve.wait_ge(pt_ready[g], cnt(h, t, g) + 1)
                    if g == 4 and t:
                        store(h, t - 1, u, b)
                    dve.sem_inc(t_free[b], 1)

                def normalise(h, t):
                    x = t % 2
                    dve.wait_ge(sum_ready, h * QT + t + 1)
                    src = sm[x][:] if t < NQL else sm[x][:, 4:5]
                    link(nc.vector.reduce_sum(rs[x][:], src, AX))
                    link(nc.vector.reciprocal(rs[x][:], rs[x][:]))
                    dve.wait_ge(o_full, h * QT + t + 1)
                    nc.vector.tensor_scalar(o[x][:], ob[:, 0:HD], rs[x][:], None, ALU.mult).then_inc(o_norm, 1)

                def store(h, t, u, b):
                    if t == 0:
                        dve.wait_ge(y_out[u], y_before)
                    nc.vector.tensor_copy(y[u][:, t * P:(t + 1) * P], tb[b][0:HD, 2 * P:3 * P]).then_inc(ot_out, 1)
                    dve.wait_ge(ot_out, h * QT + t + 1)

                def body(kv, h, pair, u):
                    nonlocal y_before
                    y_before = pair * 16
                    link.base, link.n = h * (4 * QT), 0
                    for c in range(5):
                        top(h, 0, c)
                    for t in range(QT):
                        if t:
                            normalise(h, t - 1)
                        for g in groups(t):
                            if t + 1 < QT and (g == 4 or t + 1 < NQL):
                                top(h, t + 1, g)
                            if g in BY_DVE:
                                take(h, t, g, u)
                    normalise(h, QT - 1)
                    b, n = grp(h, NGRP - 1)
                    dve.wait_ge(t_full[b], n + 1)
                    store(h, QT - 1, u, b)
                    dve.sem_inc(t_free[b], 1)
                    assert link.n == 4 * QT, link.n
                    dve.sem_inc(in_used[u], 1)

                y_before = 0
                heads(dve, body)

            @block.scalar
            def _(act):
                act.wait_ge(const_in, 16)

                def weights(h, t, c):
                    x, (t0, n) = t % 2, CHUNKS[c]
                    nc.scalar.activation(pr[x][:, t0:t0 + n], sb_[c][:, 0:n], ACT.Exp, bias=nb[x][:], scale=SC,
                                         accum_out=sm[x][:, c:c + 1]).then_inc(s_free[c], 1)

                def take(h, t, g):
                    x = t % 2
                    b, n = grp(h, gidx(t, g))
                    act.wait_ge(t_full[b], n + 1)
                    nc.scalar.copy(pt[x][:, 4 * g:4 * g + 4, :].rearrange("p a b -> p (a b)"), tb[b][:]).then_inc(pt_ready[g], 1)
                    act.wait_ge(pt_ready[g], cnt(h, t, g) + 1)
                    act.sem_inc(t_free[b], 1)

                def step(h, t):
                    act.wait_ge(nb_ready, h * QT + t + 1)
                    if t >= 2:
                        act.wait_ge(o_norm, h * QT + t - 1)
                    gs = groups(t)
                    for c in gs:
                        weights(h, t, c)
                        if c == 2:
                            take(h, t, 1)
                    for c in gs:
                        act.wait_ge(s_free[c], cnt(h, t, c) + 1)
                    act.sem_inc(sum_ready, 1)
                    if len(gs) > 1:
                        take(h, t, 3)

                def body(kv, h, pair, u):
                    for g, tiles in enumerate(VG):
                        b, n = grp(h, g)
                        act.wait_ge(t_full[b], n + 1)
                        nc.scalar.copy(v[:, tiles[0]:tiles[-1] + 1, :].rearrange("p a b -> p (a b)"), tb[b][:, 0:len(tiles) * HD]).then_inc(v_ready, 1)
                        act.wait_ge(v_ready, h * len(VG) + g + 1)
                        act.sem_inc(t_free[b], 1)
                    for t in range(QT):
                        step(h, t)
                    act.wait_ge(ot_out, (h + 1) * QT)
                    act.dma_start(yT[ds(h * HD + row0, HD), :], y[u][:]).then_inc(y_out[u], 16)

                heads(act, body)
                for u in range(2):
                    act.wait_ge(y_out[u], 16 * NH // 2)

            @block.gpsimd
            def _(pool):
                heads(pool, lambda kv, h, pair, u: qk.split(nc, pool, h, pair, u, in_used[u]))


def fourier(nc, PT, w, dft_c, dft_l, yT):
    G, Q = 4, 4
    NTK = SEQ // P
    with ExitStack() as ctx:
        s = Scope(nc, ctx, "ft")
        f = [s.sb(f"f{u}", [P, G, P]) for u in range(2)]
        ab = [s.sb(f"ab{t}", [P, 2, G, P]) for t in range(NTK)]
        t1 = s.sb("t1", [P, 2, G, P])
        t2 = s.sb("t2", [P, 2, G, P])
        wg, cc = s.sb("wg", [P, G, P]), s.sb("cc", [P, 2, P])
        cw = s.sb("cw", [P, G, 2, P])
        dl = [s.sb(f"dl{u}", [P, 2, Q, NT]) for u in range(2)]
        y = [s.sb(f"y{g}", [P, SEQ]) for g in range(G)]
        ps = s.banks(8)
        const_in, f_in, cw_prod, cw_ready = (s.sem(n) for n in ("const_in", "f_in", "cw_prod", "cw_ready"))
        fin, f_used = s.sems("fin", 2), s.sem("f_used")
        ab_prod, ab_dve, ab_act, chain, folded = (s.sem(n) for n in ("ab_prod", "ab_dve", "ab_act", "chain", "folded"))
        dl_in, y_prod, y_out, stored = s.sems("dl_in", 2), s.sem("y_prod"), s.sem("y_out"), s.sem("stored")

        with nc.Block() as block:
            @block.sync
            def _(sp):
                sp.dma_start(wg[:], w.rearrange("g c e -> c g e")).then_inc(const_in, 16)
                sp.dma_start(cc[:], dft_c).then_inc(const_in, 16)
                fv = PT[0:G * P, 0:SEQ].rearrange("(g p) t -> p g t", p=P)
                for t in range(NTK):
                    if t >= 2:
                        sp.wait_ge(ab_prod, 2 * (t - 1))
                    sp.dma_start(f[t % 2][:], fv[:, :, t * P:(t + 1) * P]).then_inc(fin[t % 2], 16)
                for r in range(4):
                    if r >= 2:
                        sp.wait_ge(y_prod, G * (r - 1))
                    sp.dma_start(dl[r % 2][:], dft_l[:, r]).then_inc(dl_in[r % 2], 16)
                sp.wait_ge(y_out, 4 * G)
                for g in range(G):
                    sp.dma_start(yT[g * P:(g + 1) * P, 0:SEQ], y[g][:]).then_inc(stored, 16)
                sp.wait_ge(stored, 16 * G)

            @block.tensor
            def _(pe):
                pe.wait_ge(const_in, 32)
                for g in range(G):
                    for j in range(2):
                        x = nc.tensor.matmul(ps[g][:, j * P:(j + 1) * P], cc[:, j, :], wg[:, g, :], start=True, stop=True)
                x.then_inc(cw_prod, 1)
                pe.wait_ge(cw_ready, G)
                for t in range(NTK):
                    pe.wait_ge(fin[t % 2], 16 * (t // 2 + 1))
                    for j in range(2):
                        b = 4 * (t % 2) + j
                        if t >= 2:
                            pe.wait_ge((ab_dve, ab_act)[j], t - 1)
                        for h in range(2):
                            x = nc.tensor.matmul(ps[b][:, h * 2 * P:(h + 1) * 2 * P], f[t % 2][:, 2 * j + h, :],
                                                 cw[:, 2 * j + h, :, :].rearrange("p a e -> p (a e)"), start=True, stop=True)
                        x.then_inc(ab_prod, 1)
                pe.wait_ge(folded, Q)
                pe.wait_ge(ab_dve, NTK)
                pe.wait_ge(ab_act, NTK)
                for r in range(4):
                    pe.wait_ge(dl_in[r % 2], 16 * (r // 2 + 1))
                    for g in range(G):
                        n = r * G + g
                        if n >= 8:
                            pe.wait_ge(y_out, n - 7)
                        for j in range(Q):
                            for c in range(2):
                                x = nc.tensor.matmul(ps[n % 8][:], ab[j + 4 * r][:, c, g, :], dl[r % 2][:, c, j, :],
                                                     start=(j == 0 and c == 0), stop=(j == Q - 1 and c == 1))
                        x.then_inc(y_prod, 1)

            @block.scalar
            def _(act):
                for t in range(NTK):
                    act.wait_ge(ab_prod, 2 * t + 2)
                    nc.scalar.copy(ab[t][:, :, 2:4, :].rearrange("p a g e -> p g a e"),
                                   ps[4 * (t % 2) + 1][:].rearrange("p (g a e) -> p g a e", g=2, a=2)).then_inc(ab_act, 1)
                for n in range(4 * G):
                    r, g = n // G, n % G
                    act.wait_ge(y_prod, n + 1)
                    nc.scalar.mul(y[g][:, r::4], ps[n % 8][:], (SEQ * P) ** -0.5).then_inc(y_out, 1)

            @block.vector
            def _(dve):
                link = Chain(dve, chain)
                dve.wait_ge(cw_prod, 1)
                for g in range(G):
                    nc.vector.tensor_copy(cw[:, g, :, :].rearrange("p a e -> p (a e)"), ps[g][:, 0:2 * P]).then_inc(cw_ready, 1)
                for t in range(NTK):
                    dve.wait_ge(ab_prod, 2 * t + 1)
                    nc.vector.tensor_copy(ab[t][:, :, 0:2, :].rearrange("p a g e -> p g a e"),
                                          ps[4 * (t % 2)][:].rearrange("p (g a e) -> p g a e", g=2, a=2)).then_inc(ab_dve, 1)
                dve.wait_ge(ab_act, NTK)
                dve.wait_ge(ab_dve, NTK)
                tt = nc.vector.tensor_tensor
                for j in range(Q):
                    a0, a1, a2, a3 = (ab[j + 4 * q] for q in range(4))
                    tt(t1[:], a0[:], a2[:], ALU.subtract)
                    link(tt(t2[:], a1[:], a3[:], ALU.subtract))
                    tt(a0[:], a0[:], a2[:], ALU.add)
                    link(tt(a1[:], a1[:], a3[:], ALU.add))
                    tt(a2[:], a0[:], a1[:], ALU.subtract)
                    link(tt(a3[:, 0], t1[:, 0], t2[:, 1], ALU.add))
                    tt(a3[:, 1], t1[:, 1], t2[:, 0], ALU.subtract)
                    link(tt(a0[:], a0[:], a1[:], ALU.add))
                    tt(a1[:, 0], t1[:, 0], t2[:, 1], ALU.subtract)
                    link(tt(a1[:, 1], t1[:, 1], t2[:, 0], ALU.add))
                    dve.sem_inc(folded, 1)


def neighbours(nc, QKV, rpb, one_hot, ident, yT, row0):
    NH, QT, ROW = 8, SEQ // P, 64
    R, NDC, NDD = 8, 31, 16
    MASK = -1e30
    SC = HD ** -0.5
    NV = T // P
    VG = [range(0, 6), range(6, 12), range(12, 18)]
    NGRP = len(VG) + 2 * QT + 1

    def window(j):
        lo = min(max(2 * j - 4, 0), SEQ // ROW - R)
        inner = 2 <= j < QT - 2
        return lo, R + inner, lo - 2 * j + R - 1, inner

    with ExitStack() as ctx:
        s = Scope(nc, ctx, "na")
        bt = s.sb("bt", [P, NH, NDD, ROW])
        bi = s.sb("bi", [P, NH, R + 1, ROW])
        idn = s.sb("idn", [P, P])
        with ExitStack() as ctx1:
            s1 = Scope(nc, ctx1, "nat")
            oh = s1.sb("oh", [64, ROW, P])
            rp = s1.sb("rp", [64, NH, NDD])
            ps = s1.banks(4)
            const_in, filled, rp_ready, prod, taken = (s1.sem(n) for n in ("const_in", "filled", "rp_ready", "prod", "taken"))
            inner_ready, masked = s1.sem("inner_ready"), s1.sem("masked")
            with nc.Block() as block:
                @block.sync
                def _(sp):
                    sp.dma_start(oh[:], one_hot).then_inc(const_in, 16)
                    sp.dma_start(idn[:], ident).then_inc(const_in, 16)
                    sp.wait_ge(filled, 1)
                    for half in range(2):
                        for h in range(NH):
                            sp.dma_start(rp[32 * half:32 * half + NDC, h, half:half + 15], rpb[h].rearrange("r c -> c r"),
                                         allow_slow_non_contiguous=True).then_inc(const_in, 16)

                @block.vector
                def _(dve):
                    nc.vector.memset(rp[:], MASK).then_inc(filled, 1)
                    dve.wait_ge(const_in, 16 * 18)
                    nc.vector.tensor_scalar(rp[:], rp[:], 1.0 / SC, None, ALU.mult).then_inc(rp_ready, 1)
                    for n in range(ROW // 4):
                        dve.wait_ge(prod, n + 1)
                        nc.vector.tensor_copy(bt[:].rearrange("p h d w -> p (h d) w")[:, :, 4 * n:4 * n + 4],
                                              ps[n % 4][:].rearrange("p (w x) -> p x w", w=4)).then_inc(taken, 1)
                    dve.wait_ge(taken, ROW // 4)
                    nc.vector.tensor_copy(bi[:], bt[:, :, 3:3 + R + 1, :]).then_inc(inner_ready, 1)
                    dve.wait_ge(inner_ready, 1)
                    nc.vector.memset(bi[0:64, :, R, :], MASK / SC).then_inc(masked, 1)
                    nc.vector.memset(bi[64:128, :, 0, :], MASK / SC).then_inc(masked, 1)

                @block.tensor
                def _(pe):
                    pe.wait_ge(rp_ready, 1)
                    for n in range(ROW // 4):
                        if n >= 4:
                            pe.wait_ge(taken, n - 3)
                        for i in range(4):
                            x = nc.tensor.matmul(ps[n % 4][:, i * P:(i + 1) * P], oh[:, 4 * n + i, :], rp[:].rearrange("p h d -> p (h d)"),
                                                 start=True, stop=True)
                        x.then_inc(prod, 1)

        q, k = [s.sb(f"q{u}", [P, SEQ]) for u in range(2)], [s.sb(f"k{u}", [P, T]) for u in range(2)]
        vt = [s.sb(f"vt{u}", [HD, T]) for u in range(2)]
        v = s.sb("v", [P, NV, HD])
        NKEY = (R + 1) * ROW
        sw = [s.sb(f"sw{u}", [P, NKEY]) for u in range(2)]
        pr = [s.sb(f"p{u}", [P, NKEY + CTX]) for u in range(2)]
        pt = [s.sb(f"pt{u}", [P, 7, P]) for u in range(2)]
        mx = [s.sb(f"mx{u}", [P, 2]) for u in range(2)]
        nb = [s.sb(f"nb{u}", [P, 1]) for u in range(2)]
        sm = [s.sb(f"sm{u}", [P, 2]) for u in range(4)]
        rs = [s.sb(f"rs{u}", [P, 1]) for u in range(2)]
        top_ = s.sb("top", [P, 1])
        o = [s.sb(f"o{u}", [P, HD]) for u in range(2)]
        y = [s.sb(f"y{u}", [HD, SEQ]) for u in range(2)]
        win = s.banks(4)
        tb = [ctx.enter_context(nc.psum_tensor(f"na_tb{u}", [P, NT], F32)) for u in range(2)]
        ob = ctx.enter_context(nc.psum_tensor("na_ob", [P, NT], F32))
        chain, zeroed = s.sem("chain"), s.sem("zeroed")
        in_full, in_used = s.sems("in_full", 2), s.sems("in_used", 2)
        s_full, s_free = s.sems("s_full", 2), s.sems("s_free", 2)
        t_full, t_free = s.sems("t_full", 2), s.sems("t_free", 2)
        nb_ready, p_ready, pt_ready, v_ready = s.sem("nb_ready"), s.sem("p_ready"), s.sems("pt_ready", 2), s.sem("v_ready")
        o_full, o_norm, ot_out = s.sem("o_full"), s.sem("o_norm"), s.sem("ot_out")
        y_out, turn_ = s.sems("y_out", 2), s.sem("turn")

        def tiles(j):
            lo, rows, _, _ = window(j)
            n = rows * ROW
            a = [(i * P, min(P, n - i * P), lo * ROW // P + i) for i in range(-(-n // P))]
            return a + [(n + i * P, P, SEQ // P + i) for i in range(2)]

        def heads(eng, body):
            with eng.Fori(0, NH // 2) as i:
                for u in range(2):
                    body(i * 2 + u, i, u)

        def grp(h, g):
            return g % 2, h * (NGRP // 2) + g // 2

        with nc.Block() as block:
            @block.sync
            def _(sp):
                def body(h, pair, u):
                    sp.wait_ge(in_used[u], pair)
                    sp.dma_start(q[u][0:HD, :], QKV[ds(h * HD, HD), 0:SEQ]).then_inc(in_full[u], 16)
                    sp.dma_start(k[u][0:HD, :], QKV[ds(h * HD + NH * HD, HD), :]).then_inc(in_full[u], 16)
                    sp.dma_start(vt[u][:], QKV[ds(h * HD + 2 * NH * HD, HD), :]).then_inc(in_full[u], 16)

                heads(sp, body)

            @block.tensor
            def _(pe):
                def scores(h, u, j):
                    x = j % 2
                    lo, rows, _, _ = window(j)
                    n, a = rows * ROW, lo * ROW
                    pe.wait_ge(s_free[x], h * (QT // 2) + j // 2)
                    qs = slice(j * P, (j + 1) * P)
                    nc.tensor.matmul(win[2 * x][:], q[u][:, qs], k[u][:, a:a + NT], start=True, stop=True)
                    if n > NT:
                        nc.tensor.matmul(win[2 * x + 1][:, CTX:CTX + ROW], q[u][:, qs], k[u][:, a + NT:a + n], start=True, stop=True)
                    nc.tensor.matmul(win[2 * x + 1][:, 0:CTX], q[u][:, qs], k[u][:, SEQ:T], start=True, stop=True
                                     ).then_inc(s_full[x], 1)

                def last(h, j, b, c):
                    pe.wait_ge(o_norm, h * QT + j + 1)
                    pe.sem_inc(turn_, 1)
                    return nc.tensor.transpose(tb[b][0:HD, c * P:(c + 1) * P], o[j % 2][:], idn[:])

                def step(h, u, j):
                    x = j % 2
                    tl = tiles(j)
                    pe.wait_ge(p_ready, h * QT + j + 1)
                    for g in range(2):
                        b, n = grp(h, len(VG) + 2 * j + g)
                        pe.wait_ge(t_free[b], n)
                        pe.sem_inc(turn_, 1)
                        for i, (c, w, _) in enumerate(tl[4 * g:4 * g + 4]):
                            tr = nc.tensor.transpose(tb[b][0:w, i * P:(i + 1) * P], pr[x][:, c:c + w], idn[:])
                        if g == 1 and j >= 2:
                            tr = last(h, j - 2, b, 3)
                        tr.then_inc(t_full[b], 1)
                    if j + 3 < QT:
                        scores(h, u, j + 3)
                    if j:
                        pe.wait_ge(o_norm, h * QT + j)
                    for n, (c, w, vt_) in enumerate(tl):
                        if n % 4 == 0:
                            pe.wait_ge(pt_ready[n // 4], h * QT + j + 1)
                        m = nc.tensor.matmul(ob[:, 0:HD], pt[x][0:w, n, :], v[0:w, vt_, :], start=(n == 0), stop=(n == len(tl) - 1))
                    m.then_inc(o_full, 1)

                pe.wait_ge(zeroed, 4)

                def body(h, pair, u):
                    pe.wait_ge(in_full[u], (pair + 1) * 48)
                    for g, tl in enumerate(VG):
                        b, n = grp(h, g)
                        pe.wait_ge(t_free[b], n)
                        pe.sem_inc(turn_, 1)
                        for i, kt in enumerate(tl):
                            tr = nc.tensor.transpose(tb[b][:, i * HD:(i + 1) * HD], vt[u][:, kt * P:(kt + 1) * P], idn[0:HD, 0:HD])
                        tr.then_inc(t_full[b], 1)
                    for j in range(3):
                        scores(h, u, j)
                    pe.wait_ge(v_ready, (h + 1) * len(VG))
                    for j in range(QT):
                        step(h, u, j)
                    b, n = grp(h, NGRP - 1)
                    pe.wait_ge(t_free[b], n)
                    last(h, QT - 2, b, 0)
                    last(h, QT - 1, b, 1).then_inc(t_full[b], 1)

                heads(pe, body)

            @block.vector
            def _(dve):
                link = Chain(dve, chain)

                def weights(h, j):
                    x = j % 2
                    lo, rows, d0, inner = window(j)
                    n = rows * ROW
                    if j >= 2:
                        dve.wait_ge(p_ready, h * QT + j - 1)
                    dve.wait_ge(s_full[x], h * (QT // 2) + j // 2 + 1)
                    table = bi[:, ds(h, 1), :, :] if inner else bt[:, ds(h, 1), d0:d0 + R, :]
                    table = table.rearrange("p o d w -> p (o d) w")
                    last = nc.vector.tensor_tensor(sw[x][:, 0:NT].rearrange("p (d w) -> p d w", w=ROW),
                                                   win[2 * x][:].rearrange("p (d w) -> p d w", w=ROW), table[:, 0:R, :], ALU.add)
                    if inner:
                        last = nc.vector.tensor_tensor(sw[x][:, NT:n].rearrange("p (d w) -> p d w", w=ROW),
                                                       win[2 * x + 1][:, CTX:CTX + ROW].rearrange("p (d w) -> p d w", w=ROW), table[:, R:R + 1, :], ALU.add)
                    link(last)
                    nc.vector.reduce_max(mx[x][:, 0:1], sw[x][:, 0:n], AX)
                    link(nc.vector.reduce_max(mx[x][:, 1:2], win[2 * x + 1][:, 0:CTX], AX))
                    link(nc.vector.reduce_max(top_[:], mx[x][:], AX))
                    nc.vector.tensor_scalar(nb[x][:], top_[:], -SC, None, ALU.mult).then_inc(nb_ready, 1)
                    dve.wait_ge(nb_ready, h * QT + j + 1)

                def normalise(h, j):
                    x = j % 2
                    link(nc.vector.tensor_tensor(rs[x][:], sm[j % 4][:, 0:1], sm[j % 4][:, 1:2], ALU.add))
                    link(nc.vector.reciprocal(rs[x][:], rs[x][:]))
                    dve.wait_ge(o_full, h * QT + j + 1)
                    nc.vector.tensor_scalar(o[x][:], ob[:, 0:HD], rs[x][:], None, ALU.mult).then_inc(o_norm, 1)

                def take(h, j):
                    x = j % 2
                    b, n = grp(h, len(VG) + 2 * j)
                    dve.wait_ge(t_full[b], n + 1)
                    nc.vector.tensor_copy(pt[x][:, 0:4, :].rearrange("p a b -> p (a b)"), tb[b][:]).then_inc(pt_ready[0], 1)
                    dve.wait_ge(pt_ready[0], h * QT + j + 1)
                    dve.sem_inc(t_free[b], 1)

                def body(h, pair, u):
                    link.base, link.n = h * (5 * QT), 0
                    weights(h, 0)
                    weights(h, 1)
                    for j in range(QT):
                        if j + 2 < QT:
                            weights(h, j + 2)
                        if j:
                            normalise(h, j - 1)
                        take(h, j)
                    normalise(h, QT - 1)
                    assert link.n == 5 * QT, link.n

                heads(dve, body)

            @block.scalar
            def _(act):
                def exps(h, j):
                    x = j % 2
                    lo, rows, _, _ = window(j)
                    n = rows * ROW
                    act.wait_ge(nb_ready, h * QT + j + 1)
                    nc.scalar.activation(pr[x][:, n:n + CTX], win[2 * x + 1][:, 0:CTX], ACT.Exp, bias=nb[x][:], scale=SC,
                                         accum_out=sm[j % 4][:, 1:2]).then_inc(s_free[x], 1)
                    nc.scalar.activation(pr[x][:, 0:n], sw[x][:, 0:n], ACT.Exp, bias=nb[x][:], scale=SC,
                                         accum_out=sm[j % 4][:, 0:1]).then_inc(p_ready, 1)

                def store(h, j, u, b, c):
                    if j == 0:
                        act.wait_ge(y_out[u], y_before)
                    nc.scalar.copy(y[u][:, j * P:(j + 1) * P], tb[b][0:HD, c * P:(c + 1) * P]).then_inc(ot_out, 1)
                    act.wait_ge(ot_out, h * QT + j + 1)

                def take(h, j, u):
                    x = j % 2
                    tl = tiles(j)
                    if j >= 2:
                        act.wait_ge(o_norm, h * QT + j - 1)
                    b, n = grp(h, len(VG) + 2 * j + 1)
                    act.wait_ge(t_full[b], n + 1)
                    if tl[4][1] < P:
                        nc.scalar.copy(pt[x][0:HD, 4, :], tb[b][0:HD, 0:P])
                        c = nc.scalar.copy(pt[x][:, 5:7, :].rearrange("p a b -> p (a b)"), tb[b][:, P:3 * P])
                    else:
                        c = nc.scalar.copy(pt[x][:, 4:6, :].rearrange("p a b -> p (a b)"), tb[b][:, 0:2 * P])
                    c.then_inc(pt_ready[1], 1)
                    act.wait_ge(pt_ready[1], h * QT + j + 1)
                    if j >= 2:
                        store(h, j - 2, u, b, 3)
                    act.sem_inc(t_free[b], 1)

                y_before = 0

                def body(h, pair, u):
                    nonlocal y_before
                    y_before = pair * 16
                    for g, tl in enumerate(VG):
                        b, n = grp(h, g)
                        act.wait_ge(t_full[b], n + 1)
                        nc.scalar.copy(v[:, tl[0]:tl[-1] + 1, :].rearrange("p a b -> p (a b)"), tb[b][:, 0:len(tl) * HD]).then_inc(v_ready, 1)
                        act.wait_ge(v_ready, h * len(VG) + g + 1)
                        act.sem_inc(t_free[b], 1)
                    exps(h, 0)
                    exps(h, 1)
                    for j in range(QT):
                        take(h, j, u)
                        if j + 2 < QT:
                            exps(h, j + 2)
                    b, n = grp(h, NGRP - 1)
                    act.wait_ge(t_full[b], n + 1)
                    store(h, QT - 2, u, b, 0)
                    store(h, QT - 1, u, b, 1)
                    act.sem_inc(t_free[b], 1)
                    act.sem_inc(in_used[u], 1)

                heads(act, body)

            @block.gpsimd
            def _(pool):
                for u in range(2):
                    nc.gpsimd.memset(q[u][HD:P, :], 0.0).then_inc(zeroed, 1)
                    nc.gpsimd.memset(k[u][HD:P, :], 0.0).then_inc(zeroed, 1)

                def body(h, pair, u):
                    pool.wait_ge(ot_out, (h + 1) * QT)
                    pool.dma_start(yT[ds(h * HD + row0, HD), 0:SEQ], y[u][:]).then_inc(y_out[u], 16)

                heads(pool, body)
                for u in range(2):
                    pool.wait_ge(y_out[u], 16 * NH // 2)


def program(nc, a, out):
    def scratch(name, shape):
        return nc.dram_tensor(name, list(shape), F32).ap()

    mods = [scratch(f"mod{i}", (2, 3 * D)) for i in range(3)]
    pT1, pT2, pT3 = scratch("pT1", (33 * P, T)), scratch("pT2", (22 * P, T)), scratch("pT3", (24 * P, T))
    y1, y2, y3 = (scratch(f"y{i}", (D, T)) for i in range(3))
    R, E = scratch("rwkv_chunks", (CH, MT_R, 2, P, 5, P)), scratch("rwkv_ends", (P, 6, CH))
    bonus, YR, YH = scratch("bonus", (D_R, SEQ)), scratch("y_rwkv", (2, D_R, SEQ)), scratch("y_hgrn", (2, D_R, SEQ))
    x1, x2, c2, qk = scratch("x1", (SEQ, D)), scratch("x2", (SEQ, D)), scratch("c2", (CTX, D)), scratch("qk", (5 * P, T))

    modulation(nc, [(a["c"], a["c_ctx"], a["mod_w"][0], a["mod_b"][0], mods[0]),
                    (a["c_2"], a["c_ctx_2"], a["ab_w_ada_2"][0], a["ab_b_ada_2"][0], mods[1]),
                    (a["c_2"], a["c_ctx_2"], a["cd_w_ada_2"][0], a["cd_b_ada_2"][0], mods[2])])

    norm_project(nc, "p1", a["x"][0], a["ctx"][0], mods[0], None, a["w_in"][0], pT1,
                 [(0, 2, False), (2, 11, True), (13, 3, False), (16, 9, True), (25, 8, False)], a["ident"], 1e-5)
    pool_branch(nc, pT1, a["pool_w"][0], a["pool_scale"][0], a["inv_count"], y1)
    rwkv_inputs(nc, pT1, 2 * P, *[a[n][0] for n in ("rwkv_shift", "rwkv_w0", "rwkv_w_up", "rwkv_a0", "rwkv_a_up", "rwkv_k_k",
                                                    "rwkv_k_a", "rwkv_r_k")], a["head_ones"], a["seg"], R, E, bonus)
    rwkv_scan(nc, R, E, a["masks"], a["levels"], a["ident"], YR)
    hgrn(nc, pT1, 13 * P, 16 * P, 19 * P, a["seg"], a["hgrn_masks"], a["ident"], YH)
    items = []
    for m in range(MT_R):
        r = slice(m * P, (m + 1) * P)
        items.append(dict(w=SEQ, a=YR[0, r, :], b=YR[1, r, :], center=1, eps=64e-5, gain=a["rwkv_gn_g"][0, r],
                          bias=a["rwkv_gn_b"][0, r], plus=bonus[r, :], rotate=0, out=y1[(2 + m) * P:(3 + m) * P, 0:SEQ]))
        items.append(dict(w=SEQ, a=YH[0, r, :], b=YH[1, r, :], center=0, eps=1e-6, gain=a["hgrn_norm_g"][0, r],
                          bias=None, plus=None, rotate=0, out=y1[(5 + m) * P:(6 + m) * P, 0:SEQ]))
    head_norm(nc, "hn", items, a["head_mean"], a["head_gather"], a["head_spread"])
    out_project(nc, "o1", y1, pT1[25 * P:33 * P, :], a["w_out"][0], a["x"][0], mods[0][0, 2 * D:3 * D], "ln", a["ln_g"][0],
                a["ln_b"][0], x1, SEQ // P, 0)

    norm_project(nc, "p2", x1, a["ctx_2"][0], mods[1], a["ab_norm_g_2"][0], a["ab_w_in_2"][0], pT2, [(0, 22, True)], a["ident"], 1e-6)
    conformer(nc, pT2, a["ab_conv_w_2"][0], a["ab_conv_b_2"][0], a["ab_ln_g_2"][0], a["ab_ln_b_2"][0], a["ident"], a["mean_512"], y2)
    items = []
    for cols, rotate in ((slice(0, SEQ), 1), (slice(SEQ, T), 0)):
        for t in range(5):
            items.append(dict(w=cols.stop - cols.start, a=pT2[(8 + t) * P:(9 + t) * P, cols], b=None, center=0, eps=1e-6,
                              gain=a["ab_q_norm_g_2" if t < 4 else "ab_k_norm_g_2"][0], bias=None, plus=None, rotate=rotate,
                              out=qk[t * P:(t + 1) * P, cols]))
    head_norm(nc, "qk", items, a["head_mean"], a["head_gather"], a["head_spread"], (a["rope_cos"], a["rope_sin"], a["rope_swap"]))
    attention(nc, qk, pT2[13 * P:14 * P, :], a["ident"], y2, 512)
    gates = mods[1]
    out_project(nc, "o2", y2, pT2[14 * P:22 * P, :], a["ab_w_out_2"][0], x1, gates[0, 2 * D:3 * D], "plain", None, None, x2, SEQ // P, 0)
    out_project(nc, "o3", y2, pT2[14 * P:22 * P, :], a["ab_w_out_2"][0], a["ctx_2"][0], gates[1, 2 * D:3 * D], "plain", None, None,
                c2, CTX // P, SEQ)

    norm_project(nc, "p3", x2, c2, mods[2], a["cd_norm_g_2"][0], a["cd_w_in_2"][0], pT3,
                 [(0, 8, False), (8, 8, True), (16, 8, False)], a["ident"], 1e-6)
    fourier(nc, pT3, a["cd_w_fourier_2"][0], a["dft_c"], a["dft_l"], y3)
    neighbours(nc, pT3[4 * P:16 * P, :], a["cd_rpb_2"][0], a["one_hot"], a["ident"], y3, 512)
    out_project(nc, "o4", y3, pT3[16 * P:24 * P, :], a["cd_w_out_2"][0], x2, mods[2][0, 2 * D:3 * D], "rms", a["final_norm_g_2"], None,
                out[0], SEQ // P, 0)


def constants():
    f = np.float32
    c = {"ident": np.eye(P, dtype=f), "mean_512": np.full((P, P), 1 / 512, f)}
    ones = np.kron(np.eye(2), np.ones((HD, HD))).astype(f)
    c["head_ones"], c["head_mean"] = ones, ones / HD
    c["head_gather"], c["head_spread"] = np.zeros((P, 4, P), f), np.zeros((P, 4, P), f)
    for j in range(4):
        for h in range(2):
            c["head_gather"][h * HD:(h + 1) * HD, j, 32 * j + h] = 1 / HD
            c["head_spread"][32 * j + h, j, h * HD:(h + 1) * HD] = 1
    t = np.arange(HD)
    c["inv_count"] = np.zeros((P, 2, HD), f)
    for g, win in enumerate((2, 4, 8, 16)):
        left = win // 2
        n = np.minimum(t + win - 1 - left, HD - 1) + 1 - np.maximum(t - left, 0)
        c["inv_count"][g % 2 * HD:(g % 2 + 1) * HD, g // 2] = 1.0 / n
    m = np.ones((2, T), f)
    m[0, 0::P], m[1, P - 1::P] = 0, 0
    c["seg"] = np.broadcast_to(m, (P, 2, T)).copy()
    s, t = np.arange(P)[:, None], np.arange(P)[None]
    c["masks"] = np.zeros((P, 2, 4 * P), f)
    lv = np.zeros((P, 2, 7, P), f)
    for d in range(2):
        strict, incl = (s < t, s <= t) if d == 0 else (s > t, s >= t)
        c["masks"][:, d] = np.concatenate([strict, incl, strict, incl], 1)
        for j in range(7):
            b = 2 ** j
            late_t, late_s = t % (2 * b) >= b, s % (2 * b) >= b
            lv[:, d, j] = (s // (2 * b) == t // (2 * b)) & ((late_t & ~late_s) if d == 0 else (~late_t & late_s))
    c["hgrn_masks"] = np.concatenate([lv, np.broadcast_to(np.eye(P, dtype=f)[:, None, None], (P, 2, 1, P))], 2)
    c["levels"] = lv.copy()
    c["levels"][:, :, 0] *= -1
    tok = np.arange(SEQ)
    inv = f(10000.0) ** (-np.arange(16, dtype=f) / f(16))
    ang = np.concatenate([(tok // 64).astype(f)[:, None] * inv, (tok % 64).astype(f)[:, None] * inv], -1).astype(f)
    c["rope_cos"], c["rope_sin"] = (np.tile(np.repeat(fn(ang).T, 2, axis=0), (2, 1)).astype(f) for fn in (np.cos, np.sin))
    c["rope_swap"] = np.zeros((P, P), f)
    for i in range(0, P, 2):
        c["rope_swap"][i + 1, i], c["rope_swap"][i, i + 1] = -1.0, 1.0
    n = np.arange(P)
    a = 2 * np.pi * (np.outer(n, n) % P) / P
    c["dft_c"] = np.stack([np.cos(a), np.sin(a)], 1).astype(f)
    m = np.arange(512)[:, None]
    c["dft_l"] = np.zeros((P, 4, 2, 4, 512), f)
    for r in range(4):
        a = 2 * np.pi * ((m * (4 * np.arange(512)[None] + r)) % SEQ) / SEQ
        for j, v in enumerate((np.cos(a), -np.sin(a))):
            c["dft_l"][:, r, j] = v.reshape(4, P, 512).transpose(1, 0, 2)
    c["one_hot"] = np.zeros((64, 64, P), f)
    for wq in range(64):
        cs = min(max(wq - 8, 0), 48)
        for wk in range(64):
            for r in range(2):
                c["one_hot"][32 * r + (wk - wq + 15 if cs <= wk < cs + 16 else 31), wk, 64 * r + wq] = 1
    return c


_INS = ["x", "c", "ctx", "c_ctx", "mod_w", "mod_b", "w_in", "rwkv_shift", "pool_w", "pool_scale", "rwkv_w0", "rwkv_w_up",
        "rwkv_a0", "rwkv_a_up", "rwkv_k_k", "rwkv_k_a", "rwkv_r_k", "rwkv_gn_g", "rwkv_gn_b", "hgrn_norm_g", "w_out", "ln_g",
        "ln_b", "c_2", "ctx_2", "c_ctx_2", "ab_w_ada_2", "ab_b_ada_2", "ab_norm_g_2", "ab_w_in_2", "ab_conv_w_2",
        "ab_conv_b_2", "ab_ln_g_2", "ab_ln_b_2", "ab_q_norm_g_2", "ab_k_norm_g_2", "ab_w_out_2", "cd_w_ada_2", "cd_b_ada_2",
        "cd_norm_g_2", "cd_w_in_2", "cd_w_fourier_2", "cd_rpb_2", "cd_w_out_2", "final_norm_g_2"]


def kernel(**inputs):
    import numpy as _np
    import concourse.bacc as _bacc
    from concourse import mybir as _mybir
    from concourse.bass_utils import run_bass_kernel_spmd as _run

    nc = _bacc.Bacc("TRN2", target_bir_lowering=False, num_devices=1)
    arrays, aps = {}, {}
    for name, value in [(n, inputs[n]) for n in _INS] + list(constants().items()):
        a = _np.ascontiguousarray(value)
        arrays[f"in_{name}_dram"] = a
        aps[name] = nc.dram_tensor(f"in_{name}_dram", a.shape, _mybir.dt.from_np(a.dtype), kind="ExternalInput").ap()
    out = nc.dram_tensor("out_0_dram", (1, SEQ, D), F32, kind="ExternalOutput").ap()
    program(nc, aps, out)
    r = _run(nc, [arrays], core_ids=[0])
    return r.results[0]["out_0_dram"]
```
